# Optimizing a Trainium2 kernel written in Bass

```python
import math
import jax
import jax.numpy as jnp
from jax import lax
import numpy as np

D_MODEL = 1024
BATCH = 1
SEQ = 512
DEPTH = 2
DEC_BATCH = 8
DEC_SEQ = 8
PAST_LEN = 256
PAGE_SIZE = 128

MIX_WIDTH = D_MODEL
NORM_EPS = 1e-6
A_HEADS = 4
A_HD = 64
A_W = A_HEADS * A_HD
A_DECAY_LORA = 64
A_ICL_LORA = 64
A_GATE_LORA = 128
A_COLS = 3 * A_W + A_DECAY_LORA + A_ICL_LORA + A_GATE_LORA
A_LN_EPS = 64e-5
B_HEADS = 4
B_HD = 64
B_W = B_HEADS * B_HD
B_CONV = 4
B_CHUNK = 64
B_COLS = 4 * B_W + 2 * B_HEADS
C_HEADS = 4
C_HD = 64
C_VD = 2 * C_HD
C_W = C_HEADS * C_VD
C_COLS = 3 * C_W
Q_BLOCK = 128
REL_BUCKETS = 32
REL_MAX_DIST = 128
P_COLS = A_COLS + B_COLS + C_COLS
PK_HEADS = 8
PK_NKEYS = 128
PK_EXPERTS = PK_NKEYS * PK_NKEYS
PK_DIM = 256
PK_HALF = PK_DIM // 2
PK_TOPK = 16
PK_TOKEN_BLOCK = 256

kernel_name = 'hymba_rwkv7_gdn_diffattn_peer_step'

def rms_norm(x, g, eps=NORM_EPS):
    xf = x.astype(jnp.float32)
    y = xf * lax.rsqrt(jnp.mean(xf * xf, axis=-1, keepdims=True) + eps)
    return (y * g.astype(jnp.float32)).astype(x.dtype)

def l2norm(x, eps=1e-6):
    xf = x.astype(jnp.float32)
    return xf * lax.rsqrt(jnp.sum(xf * xf, axis=-1, keepdims=True) + eps)

def t5_bucket(rel):
    n = jnp.maximum(-rel, 0)
    max_exact = REL_BUCKETS // 2
    nf = jnp.maximum(n, 1).astype(jnp.float32)
    large = max_exact + (jnp.log(nf / max_exact) / math.log(REL_MAX_DIST / max_exact)
                         * (REL_BUCKETS - max_exact)).astype(jnp.int32)
    large = jnp.minimum(large, REL_BUCKETS - 1)
    return jnp.where(n < max_exact, n, large)

def rwkv7_scan(r, decay, k, v, a_vec, b_vec, S0):
    def step(S, inp):
        r_t, w_t, k_t, v_t, a_t, b_t = inp
        sa = jnp.einsum('bhij,bhj->bhi', S, a_t)
        S = S * w_t[:, :, None, :] + sa[..., None] * b_t[:, :, None, :] + v_t[..., None] * k_t[:, :, None, :]
        return S, jnp.einsum('bhij,bhj->bhi', S, r_t)
    xs = tuple(jnp.moveaxis(t.astype(jnp.float32), 1, 0) for t in (r, decay, k, v, a_vec, b_vec))
    S, ys = lax.scan(step, S0.astype(jnp.float32), xs)
    return jnp.moveaxis(ys, 0, 1), S

def rwkv7_mixer(hA, shift_prev, S0, P):
    Bn, L, _ = hA.shape
    prev = jnp.concatenate([shift_prev[:, None].astype(hA.dtype), hA[:, :-1]], axis=1)
    hs = (hA + (prev - hA) * P['rw_mu']).astype(jnp.float32)
    r = hs[..., :A_W]
    k = hs[..., A_W:2 * A_W]
    v = hs[..., 2 * A_W:3 * A_W]
    o = 3 * A_W
    xw = hs[..., o:o + A_DECAY_LORA]
    o += A_DECAY_LORA
    xa = hs[..., o:o + A_ICL_LORA]
    o += A_ICL_LORA
    xg = hs[..., o:]
    w = -jax.nn.softplus(-(P['rw_w0'] + jnp.tanh(xw) @ P['rw_w2'])) - 0.5
    a = jax.nn.sigmoid(P['rw_a0'] + xa @ P['rw_a2'])
    g = jax.nn.sigmoid(xg) @ P['rw_g2']
    heads = lambda t: t.reshape(Bn, L, A_HEADS, A_HD)
    kk = l2norm(heads(k * P['rw_kk']))
    k = k * (1.0 + (a - 1.0) * P['rw_ka'])
    r, k, v, a = heads(r), heads(k), heads(v), heads(a)
    decay = jnp.exp(-jnp.exp(heads(w)))
    y, S = rwkv7_scan(r, decay, k, v, -kk, kk * a, S0)
    mu = jnp.mean(y, axis=-1, keepdims=True)
    var = jnp.mean(jnp.square(y - mu), axis=-1, keepdims=True)
    y = ((y - mu) * lax.rsqrt(var + A_LN_EPS)).reshape(Bn, L, A_W) * P['rw_ln_g'] + P['rw_ln_b']
    y = y + (jnp.sum(r * k * P['rw_rk'], axis=-1, keepdims=True) * v).reshape(Bn, L, A_W)
    return (y * g).astype(hA.dtype), S.astype(S0.dtype), hA[:, -1]

def gated_delta_chunked(q, k, v, g, beta, S0):
    f32 = jnp.float32
    q, k, v, g, beta, S = (t.astype(f32) for t in (q, k, v, g, beta, S0))
    Bn, L, H, dk = q.shape
    dv = v.shape[-1]
    C = min(B_CHUNK, L)
    n = -(-L // C)
    pad = n * C - L

    def chunk(t):
        t = jnp.pad(t, ((0, 0), (0, pad)) + ((0, 0),) * (t.ndim - 2))
        t = t.reshape((Bn, n, C) + t.shape[2:])
        return jnp.moveaxis(t, 3, 1)

    q = chunk(q) * dk ** -0.5
    k, v, g, beta = chunk(k), chunk(v), chunk(g), chunk(beta)
    gc = jnp.cumsum(g, axis=-1)
    idx = jnp.arange(C)
    incl = idx[:, None] >= idx[None, :]
    strict = idx[:, None] > idx[None, :]
    dec = jnp.exp(jnp.where(incl, gc[..., :, None] - gc[..., None, :], -jnp.inf))
    kb = k * beta[..., None]
    A = jnp.where(strict, jnp.einsum('bhnid,bhnjd->bhnij', kb, k) * dec, 0.0)
    eye = jnp.eye(C, dtype=f32)
    T = lax.linalg.triangular_solve(eye + A, jnp.broadcast_to(eye, A.shape),
                                    left_side=True, lower=True, unit_diagonal=True)
    u = T @ (v * beta[..., None])
    w = T @ (kb * jnp.exp(gc)[..., None])
    att = jnp.einsum('bhnid,bhnjd->bhnij', q, k) * dec
    q_dec = q * jnp.exp(gc)[..., None]
    k_tail = k * jnp.exp(gc[..., -1:] - gc)[..., None]
    g_last = jnp.exp(gc[..., -1])

    def step(S, inp):
        qd, kt, ui, wi, ai, gl = inp
        v_new = ui - wi @ S
        o = qd @ S + ai @ v_new
        S = S * gl[..., None, None] + jnp.swapaxes(kt, -1, -2) @ v_new
        return S, o

    xs = tuple(jnp.moveaxis(t, 2, 0) for t in (q_dec, k_tail, u, w, att, g_last))
    S, o = lax.scan(step, S, xs)
    o = jnp.moveaxis(o, 0, 2).reshape(Bn, H, n * C, dv)
    return jnp.moveaxis(o, 1, 2)[:, :L], S

def gdn_mixer(hB, conv_prev, S0, P):
    Bn, L, _ = hB.shape
    qkv = hB[..., :3 * B_W]
    xcat = jnp.concatenate([conv_prev.astype(hB.dtype), qkv], axis=1)
    cw = P['dn_conv_w']
    conv = sum(cw[j] * xcat[:, j:j + L] for j in range(B_CONV))
    conv = jax.nn.silu(conv.astype(jnp.float32))
    heads = lambda t: t.reshape(Bn, L, B_HEADS, B_HD)
    q = l2norm(heads(conv[..., :B_W]))
    k = l2norm(heads(conv[..., B_W:2 * B_W]))
    v = heads(conv[..., 2 * B_W:])
    o0 = 3 * B_W
    a_raw = hB[..., o0:o0 + B_HEADS].astype(jnp.float32)
    b_raw = hB[..., o0 + B_HEADS:o0 + 2 * B_HEADS].astype(jnp.float32)
    z = hB[..., o0 + 2 * B_HEADS:].astype(jnp.float32)
    g = -jnp.exp(P['dn_a_log'].astype(jnp.float32)) * jax.nn.softplus(a_raw + P['dn_dt_bias'])
    beta = jax.nn.sigmoid(b_raw)
    o, S = gated_delta_chunked(q, k, v, g, beta, S0)
    o = rms_norm(o, P['dn_norm_g']) * jax.nn.silu(heads(z))
    return o.reshape(Bn, L, B_W).astype(hB.dtype), S.astype(S0.dtype), xcat[:, -(B_CONV - 1):]

def diff_attention(q, k, v, lam, rel_bias, q_off):
    Bn, Lq = q.shape[:2]
    Lk = k.shape[1]
    QB = min(Q_BLOCK, Lq)
    nb = -(-Lq // QB)
    qp = jnp.pad(q, ((0, 0), (0, nb * QB - Lq), (0, 0), (0, 0), (0, 0)))
    qb = jnp.moveaxis(qp.reshape(Bn, nb, QB, C_HEADS, 2, C_HD), 1, 0)
    k_pos = jnp.arange(Lk)
    scale = C_HD ** -0.5

    def one_block(args):
        qi, bi = args
        q_pos = q_off + bi * QB + jnp.arange(QB)
        rel = k_pos[None, :] - q_pos[:, None]
        bias = jnp.transpose(rel_bias[t5_bucket(rel)], (2, 0, 1)).astype(jnp.float32)
        s = jnp.einsum('bqhcd,bkhcd->bchqk', qi, k).astype(jnp.float32) * scale + bias
        s = jnp.where(rel <= 0, s, -jnp.inf)
        p = jax.nn.softmax(s, axis=-1)
        pd = p[:, 0] - lam * p[:, 1]
        return jnp.einsum('bhqk,bkhe->bqhe', pd.astype(v.dtype), v)

    o = lax.map(one_block, (qb, jnp.arange(nb)))
    return jnp.moveaxis(o, 0, 1).reshape(Bn, nb * QB, C_HEADS, C_VD)[:, :Lq]

def peer_ffn(xn, wq, keys, u_tab, v_tab):
    Bn, L, D = xn.shape
    T = Bn * L
    TB = min(PK_TOKEN_BLOCK, T)
    nb = -(-T // TB)
    xt = jnp.pad(xn.reshape(T, D), ((0, nb * TB - T), (0, 0))).reshape(nb, TB, D)

    def route_and_mix(xb):
        q = (xb @ wq).reshape(TB, PK_HEADS, 2, PK_HALF)
        s = jnp.einsum('thcd,hcnd->thcn', q, keys).astype(jnp.float32)
        sv, si = lax.top_k(s, PK_TOPK)
        cand = (sv[:, :, 0, :, None] + sv[:, :, 1, None, :]).reshape(TB, PK_HEADS, PK_TOPK * PK_TOPK)
        cidx = (si[:, :, 0, :, None] * PK_NKEYS + si[:, :, 1, None, :]).reshape(TB, PK_HEADS, PK_TOPK * PK_TOPK)
        tv, ti = lax.top_k(cand, PK_TOPK)
        eidx = jnp.take_along_axis(cidx, ti, axis=-1).reshape(TB, PK_HEADS * PK_TOPK)
        gate = jax.nn.softmax(tv, axis=-1).reshape(TB, PK_HEADS * PK_TOPK)
        act = jax.nn.gelu(jnp.einsum('td,tjd->tj', xb, u_tab[eidx]).astype(jnp.float32), approximate=False)
        return jnp.einsum('tj,tjd->td', (gate * act).astype(xb.dtype), v_tab[eidx])

    out = lax.map(route_and_mix, xt).reshape(nb * TB, D)[:T]
    return out.reshape(Bn, L, D).astype(xn.dtype)

def trunk_layer(x, shiftA, SA, convB, SB, past_k, past_v, q_off, P, rel_bias, lam_init):
    Bn, L, _ = x.shape
    h = rms_norm(x, P['rms_mix_g']) @ P['w_in']
    hA = h[..., :A_COLS]
    hB = h[..., A_COLS:A_COLS + B_COLS]
    hC = h[..., A_COLS + B_COLS:]
    oA, SA_new, shift_new = rwkv7_mixer(hA, shiftA, SA, P)
    oB, SB_new, conv_new = gdn_mixer(hB, convB, SB, P)
    q = rms_norm(hC[..., :C_W].reshape(Bn, L, C_HEADS, 2, C_HD), P['df_qn_g'])
    k = rms_norm(hC[..., C_W:2 * C_W].reshape(Bn, L, C_HEADS, 2, C_HD), P['df_kn_g'])
    v = hC[..., 2 * C_W:].reshape(Bn, L, C_HEADS, C_VD)
    if past_k is None:
        k_all, v_all = k, v
    else:
        k_all = jnp.concatenate([past_k.reshape(Bn, -1, C_HEADS, 2, C_HD).astype(k.dtype), k], axis=1)
        v_all = jnp.concatenate([past_v.astype(v.dtype), v], axis=1)
    f32 = jnp.float32
    lam = (jnp.exp(jnp.sum(P['df_lq1'].astype(f32) * P['df_lk1'].astype(f32)))
           - jnp.exp(jnp.sum(P['df_lq2'].astype(f32) * P['df_lk2'].astype(f32))) + lam_init)
    oC = diff_attention(q, k_all, v_all, lam, rel_bias, q_off)
    oC = (rms_norm(oC, P['df_subln_g']) * (1.0 - lam_init)).reshape(Bn, L, C_W).astype(x.dtype)
    x = x + jnp.concatenate([oA, oB, oC], axis=-1) @ P['w_out']
    x = x + peer_ffn(rms_norm(x, P['rms_ffn_g']), P['pk_wq'], P['pk_keys'], P['pk_u'], P['pk_v'])
    return x, k.reshape(Bn, L, C_HEADS, 2 * C_HD), v, SA_new, shift_new, SB_new, conv_new

def setup_inputs(seed: int = 0) -> dict:
    key = jax.random.key(seed)
    ks = iter(jax.random.split(key, 64))
    f32 = jnp.float32
    nrm = lambda shape, s: jax.random.normal(next(ks), shape, f32) * s
    gain = lambda shape: 1.0 + 0.05 * jax.random.normal(next(ks), shape, f32)
    n_pages = PAST_LEN // PAGE_SIZE
    used = DEC_BATCH * n_pages
    n_pool = used + max(1, used // 4)
    page_table = jax.random.permutation(next(ks), n_pool)[:used].reshape(DEC_BATCH, n_pages).astype(jnp.int32)
    dt = jnp.exp(jax.random.uniform(next(ks), (DEPTH, B_HEADS), f32, math.log(1e-3), math.log(1e-1)))
    dt_bias = dt + jnp.log(-jnp.expm1(-dt))
    return {
        'x_prompt': nrm((BATCH, SEQ, D_MODEL), 1.0),
        'x_sample': nrm((DEC_BATCH, DEC_SEQ, D_MODEL), 1.0),
        'cache_k': nrm((n_pool, DEPTH, PAGE_SIZE, C_HEADS, 2 * C_HD), 1.0),
        'cache_v': nrm((n_pool, DEPTH, PAGE_SIZE, C_HEADS, C_VD), 1.0),
        'state_rwkv': nrm((DEPTH, DEC_BATCH, A_HEADS, A_HD, A_HD), 0.1),
        'state_rwkv_shift': nrm((DEPTH, DEC_BATCH, A_COLS), 1.0),
        'state_dn': nrm((DEPTH, DEC_BATCH, B_HEADS, B_HD, B_HD), 0.1),
        'state_dn_conv': nrm((DEPTH, DEC_BATCH, B_CONV - 1, 3 * B_W), 1.0),
        'page_table': page_table,
        'rms_mix_g': gain((DEPTH, D_MODEL)),
        'w_in': nrm((DEPTH, D_MODEL, P_COLS), D_MODEL ** -0.5),
        'w_out': nrm((DEPTH, MIX_WIDTH, D_MODEL), MIX_WIDTH ** -0.5),
        'rw_mu': jax.random.uniform(next(ks), (DEPTH, A_COLS), f32),
        'rw_w0': jax.random.uniform(next(ks), (DEPTH, A_W), f32, -6.0, -0.5),
        'rw_w2': nrm((DEPTH, A_DECAY_LORA, A_W), 0.1 * A_DECAY_LORA ** -0.5),
        'rw_a0': nrm((DEPTH, A_W), 0.1),
        'rw_a2': nrm((DEPTH, A_ICL_LORA, A_W), 0.5 * A_ICL_LORA ** -0.5),
        'rw_g2': nrm((DEPTH, A_GATE_LORA, A_W), A_GATE_LORA ** -0.5),
        'rw_kk': 0.85 + nrm((DEPTH, A_W), 0.05),
        'rw_ka': gain((DEPTH, A_W)),
        'rw_rk': nrm((DEPTH, A_HEADS, A_HD), 0.1),
        'rw_ln_g': gain((DEPTH, A_W)),
        'rw_ln_b': nrm((DEPTH, A_W), 0.01),
        'dn_conv_w': nrm((DEPTH, B_CONV, 3 * B_W), B_CONV ** -0.5),
        'dn_a_log': jnp.log(jax.random.uniform(next(ks), (DEPTH, B_HEADS), f32, 1.0, 16.0)),
        'dn_dt_bias': dt_bias,
        'dn_norm_g': gain((DEPTH, B_HD)),
        'df_qn_g': gain((DEPTH, 2, C_HD)),
        'df_kn_g': gain((DEPTH, 2, C_HD)),
        'df_lq1': nrm((DEPTH, C_HD), 0.1),
        'df_lk1': nrm((DEPTH, C_HD), 0.1),
        'df_lq2': nrm((DEPTH, C_HD), 0.1),
        'df_lk2': nrm((DEPTH, C_HD), 0.1),
        'df_subln_g': gain((DEPTH, C_VD)),
        'rel_bias': nrm((REL_BUCKETS, C_HEADS), 0.5),
        'rms_ffn_g': gain((DEPTH, D_MODEL)),
        'pk_wq': nrm((DEPTH, D_MODEL, PK_HEADS * PK_DIM), D_MODEL ** -0.5),
        'pk_keys': nrm((DEPTH, PK_HEADS, 2, PK_NKEYS, PK_HALF), PK_HALF ** -0.5),
        'pk_u': nrm((DEPTH, PK_EXPERTS, D_MODEL), D_MODEL ** -0.5),
        'pk_v': nrm((DEPTH, PK_EXPERTS, D_MODEL), 0.5 * PK_HEADS ** -0.5),
    }

def reference(x_prompt, x_sample, cache_k, cache_v, state_rwkv, state_rwkv_shift, state_dn, state_dn_conv,
              page_table, rms_mix_g, w_in, w_out, rw_mu, rw_w0, rw_w2, rw_a0, rw_a2, rw_g2, rw_kk, rw_ka,
              rw_rk, rw_ln_g, rw_ln_b, dn_conv_w, dn_a_log, dn_dt_bias, dn_norm_g, df_qn_g, df_kn_g,
              df_lq1, df_lk1, df_lq2, df_lk2, df_subln_g, rel_bias, rms_ffn_g, pk_wq, pk_keys, pk_u, pk_v):
    n_pages = PAST_LEN // PAGE_SIZE
    bp = x_prompt.shape[0]
    bs = x_sample.shape[0]
    dt = x_prompt.dtype
    xp, xs = x_prompt, x_sample
    kp_l, vp_l, ks_l, vs_l = [], [], [], []
    sap_l, sas_l, shp_l, shs_l, sbp_l, sbs_l, cvp_l, cvs_l = [], [], [], [], [], [], [], []
    for l in range(DEPTH):
        P = dict(rms_mix_g=rms_mix_g[l], w_in=w_in[l], w_out=w_out[l], rw_mu=rw_mu[l], rw_w0=rw_w0[l],
                 rw_w2=rw_w2[l], rw_a0=rw_a0[l], rw_a2=rw_a2[l], rw_g2=rw_g2[l], rw_kk=rw_kk[l],
                 rw_ka=rw_ka[l], rw_rk=rw_rk[l], rw_ln_g=rw_ln_g[l], rw_ln_b=rw_ln_b[l],
                 dn_conv_w=dn_conv_w[l], dn_a_log=dn_a_log[l], dn_dt_bias=dn_dt_bias[l],
                 dn_norm_g=dn_norm_g[l], df_qn_g=df_qn_g[l], df_kn_g=df_kn_g[l], df_lq1=df_lq1[l],
                 df_lk1=df_lk1[l], df_lq2=df_lq2[l], df_lk2=df_lk2[l], df_subln_g=df_subln_g[l],
                 rms_ffn_g=rms_ffn_g[l], pk_wq=pk_wq[l], pk_keys=pk_keys[l], pk_u=pk_u[l], pk_v=pk_v[l])
        lam_init = 0.8 - 0.6 * math.exp(-0.3 * l)
        xp, kp, vp, sap, shp, sbp, cvp = trunk_layer(
            xp, jnp.zeros((bp, A_COLS), dt), jnp.zeros((bp, A_HEADS, A_HD, A_HD), dt),
            jnp.zeros((bp, B_CONV - 1, 3 * B_W), dt), jnp.zeros((bp, B_HEADS, B_HD, B_HD), dt),
            None, None, 0, P, rel_bias, lam_init)
        past_k = cache_k[page_table, l].reshape(bs, n_pages * PAGE_SIZE, C_HEADS, 2 * C_HD)
        past_v = cache_v[page_table, l].reshape(bs, n_pages * PAGE_SIZE, C_HEADS, C_VD)
        xs, ksn, vsn, sas, shs, sbs, cvs = trunk_layer(
            xs, state_rwkv_shift[l], state_rwkv[l], state_dn_conv[l], state_dn[l],
            past_k, past_v, n_pages * PAGE_SIZE, P, rel_bias, lam_init)
        kp_l.append(kp); vp_l.append(vp); ks_l.append(ksn); vs_l.append(vsn)
        sap_l.append(sap); sas_l.append(sas); shp_l.append(shp); shs_l.append(shs)
        sbp_l.append(sbp); sbs_l.append(sbs); cvp_l.append(cvp); cvs_l.append(cvs)
    return (xp, xs,
            jnp.stack(kp_l, axis=1), jnp.stack(vp_l, axis=1),
            jnp.stack(ks_l, axis=1), jnp.stack(vs_l, axis=1),
            jnp.stack(sap_l, axis=0), jnp.stack(sas_l, axis=0),
            jnp.stack(shp_l, axis=0), jnp.stack(shs_l, axis=0),
            jnp.stack(sbp_l, axis=0), jnp.stack(sbs_l, axis=0),
            jnp.stack(cvp_l, axis=0), jnp.stack(cvs_l, axis=0))


_drawn_inputs = setup_inputs


def setup_inputs(seed=0):
    import zlib

    import numpy as np

    out = dict(_drawn_inputs(seed))
    spreads = {}
    factors = {'rw_w2': 8.0, 'rw_ln_g': 2.853, 'rw_ln_b': 7.325, 'dn_norm_g': 2.698, 'rms_ffn_g': 2.702}
    for name, (base, spread) in spreads.items():
        noise = np.random.default_rng([zlib.crc32(name.encode()), seed]).standard_normal(out[name].shape)
        drawn = base * np.exp(spread * noise) if base else spread * noise
        out[name] = jnp.asarray(drawn.astype(out[name].dtype))
    for name, factor in factors.items():
        out[name] = (out[name] * factor).astype(out[name].dtype)
    return out
```

```python
import math
from contextlib import ExitStack, contextmanager

import numpy as np

import concourse.bass as bass
from concourse import mybir

F32 = mybir.dt.float32
BF16 = mybir.dt.bfloat16
U32 = mybir.dt.uint32
ALU = mybir.AluOpType
ACT = mybir.ActivationFunctionType
AX = mybir.AxisListType

P = 128
D = 1024
KC = D // P
SEQ = 512
DEPTH = 2
NSEQ = 8
NEW = 8
SAMP = NSEQ * NEW
TOK = SEQ + SAMP
TILES = 5
TOKP = TILES * P
PAST = 256
PAGE = 128
PAGES = PAST // PAGE
H = 4
HD = 64
CH = 64
NCH = TOK // CH
A_COLS, B_COLS, C_W = 1024, 1032, 512
COL_B, COL_AB, COL_Z, COL_C = 1024, 1792, 1800, 2056
EPS = 1e-6
KAPPA = math.exp(-0.5)
NEG = -1e30
BUCKETS = 32
REL = 639
PK_HEADS, PK_KEYS, TOPK = 8, 128, 16
SLOT = 2 * TOK

COLS = {}
for _name, _n in (("mix_g", 8), ("ffn_g", 8), ("mu", 8), ("w0", 2), ("a0", 2), ("kk", 2), ("ka", 2),
                  ("rk", 2), ("ln_g", 2), ("ln_b", 2), ("conv", 24), ("subln", 1), ("dn_g", 1),
                  ("a_log", 2), ("dt", 2), ("lam_init", 1), ("lam_rest", 1)):
    COLS[_name] = (sum(n for _, n in COLS.values()), _n)
NCOL = sum(n for _, n in COLS.values())

CONST = {}
for _name, _n in (("ident", 128), ("head_mean", 128), ("all_mean", 128), ("iota", 128), ("id64", 64),
                  ("U_p", 64), ("SU_p", 64), ("SUt_p", 64), ("U_s", 64), ("SU_s", 64), ("SUt_s", 64),
                  ("lev", 6 * 64), ("seq_of", 8), ("ones", 64), ("is_c0", 1), ("is_c1", 1), ("last", 8)):
    CONST[_name] = (sum(n for _, n in CONST.values()), _n)
NCONST = sum(n for _, n in CONST.values())


def constants():
    c = np.zeros((P, NCONST), np.float32)

    def put(name, a):
        o, n = CONST[name]
        c[:, o:o + n] = a
    i = np.arange(64)
    s, t = i[:, None], i[None, :]
    same = (s // NEW) == (t // NEW)
    dup = lambda m: np.concatenate([m, m], 0).astype(np.float32)
    put("ident", np.eye(P))
    put("head_mean", np.kron(np.eye(2), np.full((64, 64), 1 / 64)))
    put("all_mean", np.full((P, P), 1 / P))
    put("iota", np.tile(np.arange(P), (P, 1)))
    put("id64", dup(np.eye(64)))
    put("U_p", dup(s <= t)); put("SU_p", dup(s > t)); put("SUt_p", dup(s < t))
    put("U_s", dup((s <= t) & same)); put("SU_s", dup((s > t) & same)); put("SUt_s", dup((s < t) & same))
    lev = [((s // (2 * b)) == (t // (2 * b))) & (s % (2 * b) >= b) & (t % (2 * b) < b) for b in (1, 2, 4, 8, 16, 32)]
    put("lev", np.concatenate([dup(m) for m in lev], 1))
    put("seq_of", dup((i[:, None] // NEW) == np.arange(8)[None, :]))
    put("ones", 1.0)
    row = np.arange(P)
    put("is_c0", ((row // 8) % 2 == 0)[:, None]); put("is_c1", ((row // 8) % 2 == 1)[:, None])
    dist = 511 - np.arange(REL)
    n = np.maximum(dist, 0)
    nf = np.maximum(n, 1).astype(np.float32)
    big = 16 + (np.log(nf / np.float32(16)) / np.float32(math.log(8)) * np.float32(16)).astype(np.int32)
    bucket = np.where(n < 16, n, np.minimum(big, 31))
    buckets = ((np.arange(BUCKETS)[:, None] == bucket[None]) & (dist >= 0)[None]).astype(np.float32)
    future = np.where(dist < 0, NEG, 0.0).astype(np.float32)[None].repeat(P, 0)
    return c, buckets, future


@contextmanager
def stage(nc, *names):
    with ExitStack() as ctx:
        sems = [ctx.enter_context(nc.semaphore(n)) for n in names]
        with nc.Block() as block:
            yield (block, *sems)
        for s in sems:
            nc.gpsimd.sem_clear(s)
        nc.all_engine_barrier()


class Steps:

    def __init__(self, eng, sem):
        self.eng, self.sem, self.n = eng, sem, 0

    def did(self, ins):
        self.n += 1
        ins.then_inc(self.sem, 1)

    def settle(self):
        self.eng.wait_ge(self.sem, self.n)

    def link(self, ins):
        self.did(ins)
        self.settle()


def bc(ap, axis, n):
    shape = list(ap.shape)
    shape.insert(axis, n)
    return ap.unsqueeze(axis).broadcast_to(shape)


def trunk(nc, t):
    ctx = ExitStack()
    with ctx:
        def sb(name, shape, dt=F32):
            return ctx.enter_context(nc.sbuf_tensor(name, shape, dt))

        x_sb = sb("x_sb", [P, TILES, D])
        cst = sb("cst", [P, NCONST])
        cols = sb("cols_sb", [P, NCOL])
        rows = sb("rows_sb", [P, 512])
        bias_p = sb("bias_p", [P, H, 512])
        bias_s = sb("bias_s", [64, PAST + NEW])
        bias_own = sb("bias_own", [64, NSEQ, SAMP])
        work_s = sb("work_s", [64, 2 * (PAST + SAMP)])
        S_sb = sb("S_sb", [P, 256])
        arena = sb("arena", [P, 34 * SLOT])
        small = sb("small", [P, 1024])
        ps = ctx.enter_context(nc.psum_tensor("ps", [P, 8, 512], F32))

        def C(name, i=None):
            o, n = CONST[name]
            return cst[:, o:o + n] if i is None else cst[:, o + i * 64:o + (i + 1) * 64]

        def col(name, i=0, p=slice(0, P)):
            o, _ = COLS[name]
            return cols[p, o + i:o + i + 1]

        def slot(i, n=1):
            return arena[:, i * SLOT:(i + n) * SLOT]

        def ch(i):
            return slot(i).rearrange("p (j t) -> p j t", j=2)

        def tm(i):
            return slot(i).rearrange("p (c j t) -> p c j t", c=NCH, j=2)

        small_at = [0]

        def sm(n):
            small_at[0] += n
            assert small_at[0] <= 1024
            return small[:, small_at[0] - n:small_at[0]]

        cat = slot(0, 4).rearrange("p (c t) -> p c t", c=KC)
        z_ch = ch(4)
        hA = slot(5, 5)
        hAp = hA[:, 0:8 * 513].rearrange("p (c t) -> p c t", c=8)
        hAs = hA[:, 8 * 513:8 * 513 + 576].rearrange("p (c b t) -> p c b t", c=8, b=8)
        hB = slot(10, 4)
        hBp = hB[:, 0:6 * 515].rearrange("p (c t) -> p c t", c=6)
        hBs = hB[:, 6 * 515:6 * 515 + 528].rearrange("p (c b t) -> p c b t", c=6, b=8)
        hC = slot(14, 7)[:, 0:TILES * 1536].rearrange("p (i n) -> p i n", i=TILES)
        xnT = slot(21, 5)[:, 0:KC * TOKP].rearrange("p (k t) -> p k t", k=KC)
        W2 = slot(26, 8)[:, 0:8192].rearrange("p (s k n) -> p s k n", s=2, k=KC)
        beta_g = sm(36).rearrange("p (k c j) -> p k c j", k=2, c=NCH)
        lam = sm(8)
        stat = sm(64)
        GL = sm(36).rearrange("p (m c j) -> p m c j", m=2, c=NCH)
        GLs = sm(32).rearrange("p (m j b) -> p m j b", m=2, j=2)
        gcol = sm(108).rearrange("p (k c j) -> p k c j", k=6, c=NCH)
        tails_o = sm(234)
        tails_i = sm(208)

        RP = REL + 1
        relb = slot(0)[0:32, 0:4]
        relb_bc = slot(0)[0:32, 128:128 + H * P].rearrange("b (h p) -> b h p", h=H)
        onehot = slot(1)[0:32, 0:REL]
        fut = slot(2)[:, 0:REL]
        r4 = slot(3, 3)[:, 0:H * RP].rearrange("p (h n) -> p h n", h=H)
        with stage(nc, "consts_in", "x_in", "steps", "rel_copied", "rel_mm", "rel_row", "rel_out", "rel_in", "own_ready") as (
                block, consts_in, x_in, steps_, rel_copied, rel_mm, rel_row, rel_out, rel_in, own_ready):
            rd = t["rel_scratch"]

            @block.sync
            def _(sp):
                sp.dma_start(relb, t["rel_bias"]).then_inc(consts_in, 16)
                sp.dma_start(onehot, t["buckets"]).then_inc(consts_in, 16)
                sp.dma_start(fut, t["future"]).then_inc(consts_in, 16)
                sp.dma_start(cst[:, :], t["consts"]).then_inc(consts_in, 16)
                sp.dma_start(x_sb[:, 0:4, :], t["x_prompt"].rearrange("(i p) d -> p i d", p=P)).then_inc(x_in, 16)
                sp.dma_start(x_sb[0:64, 4, :], t["x_sample"]).then_inc(x_in, 16)
                sp.wait_ge(rel_row, 2 * H)
                sp.dma_start(rd, r4.rearrange("p h n -> p (h n)")).then_inc(rel_out, 16)
                sp.wait_ge(rel_out, 16)
                for h in range(H):
                    sp.dma_start(bias_p[:, h, :], bass.AP(rd.tensor, h * RP + 127, [[H * RP - 1, P], [1, 512]])).then_inc(rel_in, 16)
                    for c in range(2):
                        r = h * 16 + c * 8
                        sp.dma_start(bias_s[r:r + 8, :], bass.AP(rd.tensor, h * RP + 255, [[H * RP - 1, 8], [1, PAST + NEW]])).then_inc(rel_in, 16)
                sp.wait_ge(rel_in, 12 * 16)
                sp.wait_ge(x_in, 32)

            @block.vector
            def _(dve):
                st = Steps(dve, steps_)
                st.did(dve.memset(x_sb[64:P, 4, :], 0.0))
                st.did(dve.memset(r4[:, :, REL:RP], 0.0))
                st.did(dve.memset(bias_own[:, :, :], NEG))
                st.settle()
                dve.wait_ge(consts_in, 64)
                dve.tensor_copy(relb_bc, bc(relb, 2, P)).then_inc(rel_copied, 1)
                for h in range(H):
                    dve.wait_ge(rel_mm, h + 1)
                    dve.tensor_tensor(r4[:, h, 0:512], ps[:, 2 * h, :], fut[:, 0:512], ALU.add).then_inc(rel_row, 1)
                    dve.tensor_tensor(r4[:, h, 512:REL], ps[:, 2 * h + 1, 0:REL - 512], fut[:, 512:REL], ALU.add).then_inc(rel_row, 1)
                dve.wait_ge(rel_in, 12 * 16)
                for b in range(NSEQ):
                    last = dve.tensor_copy(bias_own[:, b, b * NEW:(b + 1) * NEW], bias_s[:, PAST:PAST + NEW])
                last.then_inc(own_ready, 1)

            @block.tensor
            def _(pe):
                pe.wait_ge(consts_in, 64)
                pe.wait_ge(rel_copied, 1)
                for h in range(H):
                    pe.matmul(ps[:, 2 * h, :], relb_bc[:, h], onehot[:, 0:512], start=True, stop=True)
                    pe.matmul(ps[:, 2 * h + 1, 0:REL - 512], relb_bc[:, h], onehot[:, 512:REL], start=True, stop=True).then_inc(rel_mm, 1)

        with nc.Fori(0, DEPTH) as layer:
            L = bass.ds(layer, 1)

            def at(name):
                a = t[name][L]
                n = len(a.shape)
                names = " ".join("abcdefg"[:n - 1])
                return a.rearrange(f"o {names} -> (o a) {names[2:]}" if n > 2 else f"o {names} -> o {names}")

            def norm_transposed(gain):
                junk = slot(26)[:, 0:D]
                xn = slot(27, 5).rearrange("p (i n) -> p i n", n=SLOT)[:, :, 0:D]
                with stage(nc, "par_in", "ssq_ready", "root_ready", "inv_steps", "xn_ready", "tr_done", "xnT_act", "xnT_dve") as (
                        block, par_in, ssq_ready, root_ready, inv_steps, xn_ready, tr_done, xnT_act, xnT_dve):
                    @block.sync
                    def _(sp):
                        sp.dma_start(cols[:, :], at("cols")).then_inc(par_in, 16)
                        sp.dma_start(rows[:, :], t["rows"][L].broadcast_to([P, 512])).then_inc(par_in, 16)

                    @block.scalar
                    def _(act):
                        sq = Steps(act, ssq_ready)
                        for i in range(TILES):
                            sq.link(act.activation(junk, x_sb[:, i, :], ACT.Square, accum_out=stat[:, i:i + 1]))
                        act.wait_ge(inv_steps, 1)
                        act.activation(stat[:, 16:21], stat[:, 8:13], ACT.Sqrt).then_inc(root_ready, 1)
                        act.wait_ge(par_in, 32)
                        for u in range(1, TILES * 2, 2):
                            i, hf = u // 2, u % 2
                            act.wait_ge(tr_done, u + 1)
                            for k in range(4):
                                kc = hf * 4 + k
                                last = act.activation(xnT[:, kc, i * P:(i + 1) * P], ps[:, u % 8, k * P:(k + 1) * P], ACT.Copy,
                                                      scale=col(gain, kc))
                            last.then_inc(xnT_act, 1)

                    @block.vector
                    def _(dve):
                        st = Steps(dve, inv_steps)
                        dve.wait_ge(ssq_ready, TILES)
                        st.link(dve.tensor_scalar(stat[:, 8:13], stat[:, 0:5], 1.0 / D, EPS, ALU.mult, ALU.add))
                        dve.wait_ge(root_ready, 1)
                        st.link(dve.reciprocal(stat[:, 24:29], stat[:, 16:21]))
                        for i in range(TILES):
                            dve.tensor_scalar(xn[:, i, :], x_sb[:, i, :], stat[:, 24 + i:25 + i], None, ALU.mult).then_inc(xn_ready, 1)
                        dve.wait_ge(par_in, 32)
                        for u in range(0, TILES * 2, 2):
                            i, hf = u // 2, u % 2
                            dve.wait_ge(tr_done, u + 1)
                            for k in range(4):
                                kc = hf * 4 + k
                                last = dve.tensor_scalar(xnT[:, kc, i * P:(i + 1) * P], ps[:, u % 8, k * P:(k + 1) * P],
                                                         col(gain, kc), None, ALU.mult)
                            last.then_inc(xnT_dve, 1)

                    @block.tensor
                    def _(pe):
                        for u in range(TILES * 2):
                            i, hf = u // 2, u % 2
                            pe.wait_ge(xn_ready, i + 1)
                            if u >= 8:
                                pe.wait_ge(xnT_act if u % 2 else xnT_dve, (u - 8) // 2 + 1)
                            for k in range(4):
                                kc = hf * 4 + k
                                last = pe.transpose(ps[:, u % 8, k * P:(k + 1) * P], xn[:, i, kc * P:(kc + 1) * P], C("ident"))
                            last.then_inc(tr_done, 1)

            norm_transposed("mix_g")

            groups = [("A", 0, 512), ("A", 512, 512), ("B", COL_B, 512), ("B", COL_B + 512, 256), ("ab", COL_AB, 8),
                      ("z", COL_Z, 256), ("C", COL_C, 512), ("C", COL_C + 512, 512), ("C", COL_C + 1024, 512)]
            units = []
            for g, (kind, c0, w) in enumerate(groups):
                if kind == "C":
                    units += [(g, kind, c0, i) for i in range(TILES)]
                elif kind == "ab":
                    units += [(g, kind, c0, 0)]
                else:
                    units += [(g, kind, c0 + m * P, part) for m in range(w // P) for part in (0, 1)]
            group_last = [max(u for u, un in enumerate(units) if un[0] == g) for g in range(len(groups))]
            with stage(nc, "w_in0", "w_in1", "tails_in", "proj_done", "out_act", "out_dve", "tails_steps", "tail_ready", "tail_out") as (
                    block, w_s0, w_s1, tails_in, proj_done, out_act, out_dve, tails_steps, tail_ready, tail_out):
                w_sem = [w_s0, w_s1]
                wv = at("w_in").rearrange("(k p) n -> p k n", p=P)

                @block.sync
                def _(sp):
                    sp.dma_start(tails_i, at("tails")).then_inc(tails_in, 16)
                    for g, (kind, c0, w) in enumerate(groups):
                        if g >= 2:
                            sp.wait_ge(proj_done, group_last[g - 2] + 1)
                        sp.dma_start(W2[:, g % 2, :, 0:w], wv[:, :, c0:c0 + w]).then_inc(w_sem[g % 2], 16)
                    sp.wait_ge(tail_ready, 1)
                    sp.dma_start(at("o_tails"), tails_o).then_inc(tail_out, 16)
                    sp.wait_ge(tail_out, 16)

                def copies(u):
                    g, kind, c0, part = units[u]
                    b = ps[:, u % 8, :]
                    if kind == "C":
                        return [(hC[:, part, c0 - COL_C:c0 - COL_C + 512], b)]
                    if kind == "ab":
                        v = b[:, 0:NCH * 8].rearrange("p (c k j h) -> p h k c j", c=NCH, k=2, j=2)
                        return [(beta_g[64 * hf:64 * hf + 64, k], v[64 * hf:64 * hf + 64, hf, k]) for hf in range(2) for k in range(2)]
                    if kind == "z":
                        j = (c0 - COL_Z) // P
                        return [(z_ch[:, j, 0:SEQ], b)] if part == 0 else [(z_ch[:, j, SEQ:TOK], b[:, 0:SAMP])]
                    base, dp, ds_, lead = (0, hAp, hAs, 1) if kind == "A" else (COL_B, hBp, hBs, 3)
                    c = (c0 - base) // P
                    if part == 0:
                        return [(dp[:, c, lead:lead + SEQ], b)]
                    return [(ds_[:, c, :, lead:lead + NEW], b[:, 0:SAMP].rearrange("p (b t) -> p b t", b=NSEQ))]

                @block.scalar
                def _(act):
                    for u in range(0, len(units), 2):
                        act.wait_ge(proj_done, u + 1)
                        for d, s in copies(u):
                            last = act.copy(d, s)
                        last.then_inc(out_act, 1)

                @block.vector
                def _(dve):
                    st = Steps(dve, tails_steps)
                    st.did(dve.memset(hAp[:, :, 0:1], 0.0))
                    st.did(dve.memset(hBp[:, :, 0:3], 0.0))
                    dve.wait_ge(tails_in, 16)
                    st.did(dve.tensor_copy(hAs[:, :, :, 0:1], tails_i[:, 0:64].rearrange("p (c b o) -> p c b o", c=8, b=8)))
                    st.did(dve.tensor_copy(hBs[:, :, :, 0:3], tails_i[:, 64:208].rearrange("p (c b k) -> p c b k", c=6, b=8)))
                    for u in range(1, len(units), 2):
                        dve.wait_ge(proj_done, u + 1)
                        for d, s in copies(u):
                            last = dve.tensor_copy(d, s)
                        last.then_inc(out_dve, 1)
                    dve.wait_ge(out_act, (len(units) + 1) // 2)
                    dve.wait_ge(out_dve, len(units) // 2)
                    st.did(dve.tensor_copy(tails_o[:, 0:8].unsqueeze(2), hAp[:, :, SEQ:SEQ + 1]))
                    st.did(dve.tensor_copy(tails_o[:, 8:72].rearrange("p (c b o) -> p c b o", c=8, b=8), hAs[:, :, :, NEW:NEW + 1]))
                    st.did(dve.tensor_copy(tails_o[:, 72:90].rearrange("p (c k) -> p c k", c=6), hBp[:, :, SEQ:SEQ + 3]))
                    st.link(dve.tensor_copy(tails_o[:, 90:234].rearrange("p (c b k) -> p c b k", c=6, b=8), hBs[:, :, :, NEW:NEW + 3]))
                    dve.sem_inc(tail_ready, 1)

                @block.tensor
                def _(pe):
                    for u, (g, kind, c0, part) in enumerate(units):
                        s = g % 2
                        if u == 0 or units[u - 1][0] != g:
                            pe.wait_ge(w_sem[s], 16 * (g // 2 + 1))
                        if u >= 8:
                            pe.wait_ge(out_dve if u % 2 else out_act, (u - 8) // 2 + 1)
                        if kind == "ab":
                            for c, hf in ((c, hf) for c in range(NCH) for hf in range(2)):
                                for k in range(KC):
                                    last = pe.matmul(ps[64 * hf:64 * hf + 64, u % 8, c * 8:c * 8 + 8], xnT[:, k, c * CH:(c + 1) * CH],
                                                     W2[:, s, k, 0:8], start=(k == 0), stop=(k == KC - 1))
                        else:
                            m = c0 - groups[g][1]
                            for k in range(KC):
                                if kind == "C":
                                    last = pe.matmul(ps[:, u % 8, :], xnT[:, k, part * P:(part + 1) * P], W2[:, s, k, 0:512],
                                                     start=(k == 0), stop=(k == KC - 1))
                                else:
                                    t0, n = (0, SEQ) if part == 0 else (SEQ, SAMP)
                                    last = pe.matmul(ps[:, u % 8, 0:n], W2[:, s, k, m:m + P], xnT[:, k, t0:t0 + n],
                                                     start=(k == 0), stop=(k == KC - 1))
                        last.then_inc(proj_done, 1)

            QT = slot(21, 5)[:, 0:2560].rearrange("p (h t) -> p h t", h=H)
            KT = slot(21, 5)[:, 2560:5120].rearrange("p (h t) -> p h t", h=H)
            room = slot(26, 8)
            sq2 = room[:, 0:2048].rearrange("p (s n) -> p s n", s=2)
            ssq = room[:, 2048:2128].rearrange("p (i n) -> p i n", i=TILES)
            root = room[:, 2128:2208]
            rinv = room[:, 2208:2288].rearrange("p (i n) -> p i n", i=TILES)
            lprod = room[:, 2304:2432].rearrange("p (a n) -> p a n", a=2)
            coef = lam[0:64, 4:5]
            with stage(nc, "sq_ready", "ssq_steps", "mean_ready", "root_ready", "lam_sum", "lam_exp", "qk_ready", "t_done", "q_out",
                       "k_out", "rows_out") as (block, sq_ready, ssq_steps, mean_ready, root_ready, lam_sum, lam_exp, qk_ready,
                                                t_done, q_out, k_out, rows_out):
                @block.scalar
                def _(act):
                    for i in range(TILES):
                        if i >= 2:
                            act.wait_ge(ssq_steps, i - 1)
                        act.activation(sq2[:, i % 2, :], hC[:, i, 0:1024], ACT.Square).then_inc(sq_ready, 1)
                    act.wait_ge(mean_ready, 1)
                    act.activation(root, root, ACT.Sqrt).then_inc(root_ready, 1)
                    act.wait_ge(lam_sum, 1)
                    act.activation(lam[:, 0:2], lam[:, 0:2], ACT.Exp).then_inc(lam_exp, 1)
                    for i in range(TILES):
                        act.wait_ge(t_done, 2 * i + 1)
                        act.copy(QT[:, :, i * P:(i + 1) * P], ps[:, (2 * i) % 8, :].rearrange("p (h t) -> p h t", h=H)).then_inc(q_out, 1)

                @block.vector
                def _(dve):
                    st = Steps(dve, ssq_steps)
                    for i in range(TILES):
                        dve.wait_ge(sq_ready, i + 1)
                        st.did(dve.tensor_reduce(ssq[:, i, :], sq2[:, i % 2, :].rearrange("p (g n) -> p g n", n=HD), AX.X, ALU.add))
                    st.settle()
                    st.did(dve.tensor_tensor(lprod, rows[:, 256:512].rearrange("p (a b n) -> p b a n", a=2, b=2)[:, 0],
                                             rows[:, 256:512].rearrange("p (a b n) -> p b a n", a=2, b=2)[:, 1], ALU.mult))
                    dve.tensor_scalar(root.rearrange("p (i n) -> p i n", i=TILES), ssq, 1.0 / HD, EPS, ALU.mult, ALU.add).then_inc(mean_ready, 1)
                    st.settle()
                    dve.tensor_reduce(lam[:, 0:2], lprod, AX.X, ALU.add).then_inc(lam_sum, 1)
                    dve.wait_ge(root_ready, 1)
                    st.link(dve.reciprocal(rinv.rearrange("p i n -> p (i n)"), root))
                    for i in range(TILES):
                        v = hC[:, i, 0:1024].rearrange("p (g n) -> p g n", n=HD)
                        st.link(dve.tensor_tensor(v, v, bc(rinv[:, i, :], 2, HD), ALU.mult))
                        v = hC[:, i, 0:1024].rearrange("p (a h n) -> p a h n", a=2, h=H)
                        g = bc(rows[:, 0:256].rearrange("p (a n) -> p a n", a=2), 2, H)
                        dve.tensor_tensor(v, v, g, ALU.mult).then_inc(qk_ready, 1)
                    dve.wait_ge(lam_exp, 1)
                    st.link(dve.tensor_tensor(lam[:, 2:3], lam[:, 0:1], lam[:, 1:2], ALU.subtract))
                    st.link(dve.tensor_tensor(lam[:, 2:3], lam[:, 2:3], col("lam_init"), ALU.add))
                    st.link(dve.tensor_scalar(lam[:, 3:4], lam[:, 2:3], -1.0, None, ALU.mult))
                    st.link(dve.scalar_tensor_tensor(coef, C("is_c1")[0:64], lam[0:64, 3:4], C("is_c0")[0:64], ALU.mult, ALU.add))
                    for i in range(TILES):
                        dve.wait_ge(t_done, 2 * i + 2)
                        dve.tensor_copy(KT[:, :, i * P:(i + 1) * P], ps[:, (2 * i + 1) % 8, :].rearrange("p (h t) -> p h t", h=H)).then_inc(k_out, 1)

                @block.tensor
                def _(pe):
                    for i in range(TILES):
                        pe.wait_ge(qk_ready, i + 1)
                        if i == 4:
                            pe.wait_ge(q_out, 1)
                            pe.wait_ge(k_out, 1)
                        for a in range(2):
                            for h in range(H):
                                last = pe.transpose(ps[:, (2 * i + a) % 8, h * P:(h + 1) * P], hC[:, i, a * C_W + h * P:a * C_W + (h + 1) * P], C("ident"))
                            last.then_inc(t_done, 1)

                @block.sync
                def _(sp):
                    sp.dma_start(at("o_vp").rearrange("(i p) n -> p i n", p=P), hC[:, 0:4, 1024:1536]).then_inc(rows_out, 16)
                    sp.dma_start(at("o_vs"), hC[0:SAMP, 4, 1024:1536]).then_inc(rows_out, 16)
                    sp.wait_ge(qk_ready, TILES)
                    sp.dma_start(at("o_kp").rearrange("(i p) n -> p i n", p=P), hC[:, 0:4, 512:1024]).then_inc(rows_out, 16)
                    sp.dma_start(at("o_ks"), hC[0:SAMP, 4, 512:1024]).then_inc(rows_out, 16)
                    sp.wait_ge(rows_out, 64)

            Sb = room[:, 0:2048].rearrange("p (s c k) -> p s c k", s=2, c=2)
            pd = room[:, 2048:3072].rearrange("p (s k) -> p s k", s=2)
            PT = room[:, 3072:4096].rearrange("p (s k) -> p s k", s=2)
            st4 = room[:, 4096:4096 + 16].rearrange("p (s n) -> p s n", s=2)
            au = [(i, h) for i in range(4) for h in range(H)]
            OC = cat[:, 4:8, :]
            with stage(nc, "s_done", "biased", "max_ready", "exp_done", "fin_steps", "pd_ready", "pt_done", "pt_ready", "pv_done", "oc_ready") as (
                    block, s_done, biased, max_ready, exp_done, fin_steps, pd_ready, pt_done, pt_ready, pv_done, oc_ready):
                @block.tensor
                def _(pe):
                    def scores(u):
                        i, h = au[u]
                        if u >= 2:
                            pe.wait_ge(biased, u - 1)
                        for c in range(2):
                            last = pe.matmul(ps[:, 2 * (u % 2) + c, 0:(i + 1) * P], QT[64 * c:64 * c + 64, h, i * P:(i + 1) * P],
                                             KT[64 * c:64 * c + 64, h, 0:(i + 1) * P], start=True, stop=True)
                        last.then_inc(s_done, 1)

                    def turn(u):
                        i, h = au[u]
                        pe.wait_ge(pd_ready, u + 1)
                        if u >= 2:
                            pe.wait_ge(pt_ready, u - 1)
                        for j in range(i + 1):
                            last = pe.transpose(ps[:, 4 + u % 2, j * P:(j + 1) * P], pd[:, u % 2, j * P:(j + 1) * P], C("ident"))
                        last.then_inc(pt_done, 1)

                    def values(u):
                        i, h = au[u]
                        pe.wait_ge(pt_ready, u + 1)
                        if u >= 2:
                            pe.wait_ge(oc_ready, u - 1)
                        for j in range(i + 1):
                            last = pe.matmul(ps[:, 6 + u % 2, 0:P], hC[:, j, 1024 + h * P:1024 + (h + 1) * P], PT[:, u % 2, j * P:(j + 1) * P],
                                             start=(j == 0), stop=(j == i))
                        last.then_inc(pv_done, 1)
                    n = len(au)
                    for u in range(n + 2):
                        if u < n:
                            scores(u)
                        if 1 <= u <= n:
                            turn(u - 1)
                        if u >= 2:
                            values(u - 2)

                def copy_out(act, u):
                    i, h = au[u]
                    act.wait_ge(pt_done, u + 1)
                    if u >= 2:
                        act.wait_ge(pv_done, u - 1)
                    act.copy(PT[:, u % 2, 0:(i + 1) * P], ps[:, 4 + u % 2, 0:(i + 1) * P]).then_inc(pt_ready, 1)
                    act.wait_ge(pv_done, u + 1)
                    act.copy(OC[:, h, i * P:(i + 1) * P], ps[:, 6 + u % 2, 0:P]).then_inc(oc_ready, 1)

                @block.scalar
                def _(act):
                    for u, (i, h) in enumerate(au):
                        k, s, m = (i + 1) * P, Sb[:, u % 2], st4[:, u % 2]
                        act.wait_ge(max_ready, u + 1)
                        for c in range(2):
                            last = act.activation(s[:, c, 0:k], s[:, c, 0:k], ACT.Exp, bias=m[:, c:c + 1], accum_out=m[:, 2 + c:3 + c])
                        last.then_inc(exp_done, 1)
                        if u >= 1:
                            copy_out(act, u - 1)
                    copy_out(act, len(au) - 1)

                @block.vector
                def _(dve):
                    st = Steps(dve, fin_steps)

                    def finish(u):
                        i, h = au[u]
                        k, s, m = (i + 1) * P, Sb[:, u % 2], st4[:, u % 2]
                        dve.wait_ge(exp_done, u + 1)
                        st.link(dve.reciprocal(m[:, 4:6], m[:, 2:4]))
                        st.link(dve.tensor_tensor(m[:, 5:6], m[:, 5:6], lam[:, 3:4], ALU.mult))
                        if u >= 2:
                            dve.wait_ge(pt_done, u - 1)
                        st.link(dve.tensor_scalar(pd[:, u % 2, 0:k], s[:, 0, 0:k], m[:, 4:5], None, ALU.mult))
                        dve.scalar_tensor_tensor(pd[:, u % 2, 0:k], s[:, 1, 0:k], m[:, 5:6], pd[:, u % 2, 0:k],
                                                 ALU.mult, ALU.add).then_inc(pd_ready, 1)

                    for u, (i, h) in enumerate(au):
                        k, s, m = (i + 1) * P, Sb[:, u % 2], st4[:, u % 2]
                        dve.wait_ge(s_done, u + 1)
                        if u >= 2:
                            dve.wait_ge(pd_ready, u - 1)
                        dve.scalar_tensor_tensor(s[:, :, 0:k], ps[:, 2 * (u % 2):2 * (u % 2) + 2, 0:k], HD ** -0.5,
                                                 bc(bias_p[:, h, 512 - k:512], 1, 2), ALU.mult, ALU.add).then_inc(biased, 1)
                        dve.wait_ge(biased, u + 1)
                        dve.tensor_reduce(m[:, 0:2], s[:, :, 0:k], AX.X, ALU.max, negate=True).then_inc(max_ready, 1)
                        if u >= 1:
                            finish(u - 1)
                    finish(len(au) - 1)

            QX = room[:, 0:2048].rearrange("p (b h r) -> p b h r", b=NSEQ, h=H)
            pgK = room[:, 2048:4096].rearrange("p (s j n) -> p s j n", s=2, j=PAGES)
            pgV = room[:, 4096:6144].rearrange("p (s j n) -> p s j n", s=2, j=PAGES)
            KTb = room[:, 6144:8192].rearrange("p (s h t) -> p s h t", s=2, h=H)
            W_ = PAST + SAMP
            Ss = work_s[:, 0:2 * W_].rearrange("p (s k) -> p s k", s=2)
            PTa = room[:, 8192:8384].rearrange("p (j r) -> p j r", j=3)
            PTs = room[:, 8384:8384 + 192].rearrange("p (s j h q) -> p s j h q", s=2, j=3, h=H)
            ms = stat[0:64, 32:48].rearrange("p (s n) -> p s n", s=2)
            with stage(nc, "pages_in0", "pages_in1", "qx_steps", "kt_done", "kt_a", "kt_v", "s_done", "biased", "max_ready", "exp_done",
                       "p_steps", "p_ready", "pt_done", "pta_steps", "pt_ready", "pv_done", "oc_ready", "pid_in") as (
                    block, pages_in0, pages_in1, qx_steps, kt_done, kt_a, kt_v, s_done, biased, max_ready, exp_done,
                    p_steps, p_ready, pt_done, pta_steps, pt_ready, pv_done, oc_ready, pid_in):
                pages_in = [pages_in0, pages_in1]

                @block.sync
                def _(sp):
                    for b in range(NSEQ):
                        if b >= 2:
                            sp.wait_ge(kt_done, 2 * (b - 1))
                            sp.wait_ge(pv_done, b - 1)
                        for j in range(PAGES):
                            pid = sp.value_load(t["page_table"][b:b + 1, j:j + 1], min_val=0, max_val=t["cache_k"].shape[0] - 1)
                            for name, dst in (("cache_k", pgK), ("cache_v", pgV)):
                                src = t[name][bass.ds(pid, 1), L].rearrange("o a t h n -> (o a t) (h n)")
                                sp.dma_start(dst[:, b % 2, j, :], src).then_inc(pages_in[b % 2], 16)

                @block.tensor
                def _(pe):
                    def keys(b):
                        pe.wait_ge(pages_in[b % 2], 64 * (b // 2 + 1))
                        for j in range(PAGES):
                            if b >= 1:
                                pe.wait_ge(kt_v if j else kt_a, b)
                            for h in range(H):
                                last = pe.transpose(ps[:, j, h * P:(h + 1) * P], pgK[:, b % 2, j, h * P:(h + 1) * P], C("ident"))
                            last.then_inc(kt_done, 1)

                    def scores(b):
                        pe.wait_ge(kt_a, b + 1)
                        pe.wait_ge(kt_v, b + 1)
                        if b == 0:
                            pe.wait_ge(qx_steps, 9)
                        if b >= 2:
                            pe.wait_ge(biased, 2 * (b - 1))
                        for h in range(H):
                            pe.matmul(ps[0:64, 2 + b % 2, 0:PAST], QX[:, b, h, :], KTb[:, b % 2, h, :], start=(h == 0), stop=(h == 3))
                        for h in range(H):
                            last = pe.matmul(ps[0:64, 2 + b % 2, PAST:W_], QX[:, b, h, :], KT[:, h, SEQ:TOK], start=(h == 0), stop=(h == 3))
                        last.then_inc(s_done, 1)

                    def turn(b):
                        pe.wait_ge(p_ready, b + 1)
                        if b >= 2:
                            pe.wait_ge(pt_ready, b - 1)
                        for j in range(3):
                            k = min(P, W_ - j * P)
                            last = pe.transpose(ps[0:k, 4 + b % 2, j * 64:j * 64 + 64], Ss[:, b % 2, j * P:j * P + k], C("ident")[0:64, 0:64])
                        last.then_inc(pt_done, 1)

                    def values(b):
                        pe.wait_ge(pt_ready, b + 1)
                        for h in range(H):
                            o = ps[:, 6, h * 64 + b * NEW:h * 64 + (b + 1) * NEW]
                            for j in range(PAGES):
                                pe.matmul(o, pgV[:, b % 2, j, h * P:(h + 1) * P], PTs[:, b % 2, j, h, :], start=(j == 0), stop=False)
                            last = pe.matmul(o, hC[0:64, 4, 1024 + h * P:1024 + (h + 1) * P], PTs[0:64, b % 2, 2, h, :], start=False, stop=True)
                        last.then_inc(pv_done, 1)
                    for b in range(NSEQ + 2):
                        if b >= 2:
                            values(b - 2)
                        if b < NSEQ:
                            keys(b)
                        if 1 <= b <= NSEQ:
                            scores(b - 1)
                            turn(b - 1)

                @block.scalar
                def _(act):
                    for b in range(NSEQ + 1):
                        if b < NSEQ:
                            act.wait_ge(kt_done, 2 * b + 1)
                            if b >= 2:
                                act.wait_ge(s_done, b - 1)
                            act.copy(KTb[:, b % 2, :, 0:P], ps[:, 0, :].rearrange("p (h t) -> p h t", h=H)).then_inc(kt_a, 1)
                        if b >= 1:
                            u = b - 1
                            act.wait_ge(max_ready, u + 1)
                            act.activation(Ss[:, u % 2, :], Ss[:, u % 2, :], ACT.Exp, bias=ms[:, u % 2, 0:1], accum_out=ms[:, u % 2, 1:2]).then_inc(exp_done, 1)
                    act.wait_ge(pv_done, NSEQ)
                    act.copy(OC[:, :, SEQ:TOK], ps[:, 6, 0:256].rearrange("p (h t) -> p h t", h=H)).then_inc(oc_ready, 1)

                @block.vector
                def _(dve):
                    q = Steps(dve, qx_steps)
                    q.link(dve.memset(QX, 0.0))
                    for h in range(H):
                        for c in range(2):
                            p = slice(64 * c, 64 * c + 64)
                            q.did(dve.tensor_copy(QX[p, :, h, h * 16 + c * 8:h * 16 + c * 8 + 8],
                                                  QT[p, h, SEQ:TOK].rearrange("p (b t) -> p b t", b=NSEQ)))
                    st = Steps(dve, p_steps)
                    pt = Steps(dve, pta_steps)

                    def softmax(b):
                        s, m = Ss[:, b % 2], ms[:, b % 2]
                        dve.wait_ge(s_done, b + 1)
                        if b >= 2:
                            dve.wait_ge(pt_done, b - 1)
                        dve.scalar_tensor_tensor(s[:, 0:PAST], ps[0:64, 2 + b % 2, 0:PAST], HD ** -0.5, bias_s[:, 0:PAST],
                                                 ALU.mult, ALU.add).then_inc(biased, 1)
                        dve.scalar_tensor_tensor(s[:, PAST:W_], ps[0:64, 2 + b % 2, PAST:W_], HD ** -0.5, bias_own[:, b, :],
                                                 ALU.mult, ALU.add).then_inc(biased, 1)
                        dve.wait_ge(biased, 2 * b + 2)
                        dve.tensor_reduce(m[:, 0:1], s, AX.X, ALU.max, negate=True).then_inc(max_ready, 1)
                        dve.wait_ge(exp_done, b + 1)
                        st.link(dve.reciprocal(m[:, 2:3], m[:, 1:2]))
                        st.link(dve.tensor_tensor(m[:, 2:3], m[:, 2:3], coef, ALU.mult))
                        dve.tensor_scalar(s, s, m[:, 2:3], None, ALU.mult).then_inc(p_ready, 1)
                        dve.wait_ge(pt_done, b + 1)
                        if b >= 2:
                            dve.wait_ge(pv_done, b - 1)
                        for p, js in ((slice(0, P), slice(0, 2)), (slice(0, 64), slice(2, 3))):
                            n = js.stop - js.start
                            raw = ps[p, 4 + b % 2, js.start * 64:js.stop * 64]
                            pt.link(dve.tensor_copy(PTa[p, js, :], raw.rearrange("p (j r) -> p j r", j=n)))
                            v = PTa[p, js, :].rearrange("p j (h c q) -> p c j h q", h=H, c=2)
                            for j in range(n):
                                last = dve.tensor_tensor(PTs[p, b % 2, js.start + j], v[:, 0, j], v[:, 1, j], ALU.add)
                                pt.did(last)
                        pt.settle()
                        dve.sem_inc(pt_ready, 1)
                    for b in range(NSEQ + 1):
                        if b < NSEQ:
                            dve.wait_ge(kt_done, 2 * b + 2)
                            if b >= 2:
                                dve.wait_ge(s_done, b - 1)
                            dve.tensor_copy(KTb[:, b % 2, :, P:PAST], ps[:, 1, :].rearrange("p (h t) -> p h t", h=H)).then_inc(kt_v, 1)
                        if b >= 1:
                            softmax(b - 1)

            hs = slot(14, 4).rearrange("p (c t) -> p c t", c=8)
            r_, k_, v_, lora = ch(14), ch(15), ch(16), ch(17)
            sig, a_, gate, kkn = ch(18), ch(19), ch(20), ch(21)
            t1, t2, cumA, cumB = ch(22), ch(23), ch(24), ch(25)
            Gd, Gi = ch(26), ch(27)
            Qr, Ar, Kr, Br, yadd = ch(28), ch(29), ch(30), ch(31), ch(32)
            lw = slot(33)[:, 0:512]
            halves = [(j, q) for j in range(2) for q in range(2)]
            HN = TOK // 2

            def chunked(a):
                return (a[:, :, 0:SEQ].rearrange("p j (c t) -> p j c t", t=CH), a[:, :, SEQ:TOK].rearrange("p j (b t) -> p j b t", t=NEW))

            def flat(a):
                return a.rearrange("p j t -> p (j t)")

            with stage(nc, "lora_in", "v_steps", "lora_ready", "lora_act", "mm_done", "act_out", "sq_ready", "kk_mm", "root_ready",
                       "rk_ready", "rk_mm", "rk_out", "cum_ready", "exp_ready") as (
                    block, lora_in, v_steps, lora_ready, lora_act, mm_done, act_out, sq_ready, kk_mm, root_ready,
                    rk_ready, rk_mm, rk_out, cum_ready, exp_ready):
                @block.sync
                def _(sp):
                    sp.dma_start(lw, at("lora")).then_inc(lora_in, 16)

                @block.tensor
                def _(pe):
                    pe.wait_ge(lora_in, 16)
                    pe.wait_ge(lora_act, 2)
                    for u in range(12):
                        kind, (j, q) = u // 4, halves[u % 4]
                        if u >= 8:
                            pe.wait_ge(act_out, u - 7)
                        w, x = [(lw[0:64, j * P:(j + 1) * P], lora[0:64, 0]), (lw[64:P, j * P:(j + 1) * P], lora[64:P, 0]),
                                (lw[:, 256 + j * P:256 + (j + 1) * P], lora[:, 1])][kind]
                        pe.matmul(ps[:, u % 8, 0:HN], w, x[:, q * HN:(q + 1) * HN], start=True, stop=True).then_inc(mm_done, 1)
                    pe.wait_ge(sq_ready, 1)
                    pe.wait_ge(act_out, 12)
                    for u, (j, q) in enumerate(halves):
                        pe.matmul(ps[:, u, 0:HN], C("head_mean"), t1[:, j, q * HN:(q + 1) * HN], start=True, stop=True).then_inc(kk_mm, 1)
                    pe.wait_ge(rk_ready, 2)
                    for u, (j, q) in enumerate(halves):
                        pe.matmul(ps[:, 4 + u, 0:HN], C("head_mean"), t1[:, j, q * HN:(q + 1) * HN], start=True, stop=True).then_inc(rk_mm, 1)

                @block.scalar
                def _(act):
                    act.wait_ge(lora_ready, 4)
                    act.activation(lora[0:64, 0], lora[0:64, 0], ACT.Tanh).then_inc(lora_act, 1)
                    act.activation(lora[:, 1], lora[:, 1], ACT.Sigmoid).then_inc(lora_act, 1)
                    for u in range(12):
                        kind, (j, q) = u // 4, halves[u % 4]
                        act.wait_ge(mm_done, u + 1)
                        src = ps[:, u % 8, 0:HN]
                        d = (sig, a_, gate)[kind][:, j, q * HN:(q + 1) * HN]
                        if kind == 2:
                            act.copy(d, src).then_inc(act_out, 1)
                        else:
                            act.activation(d, src, ACT.Sigmoid, bias=col("w0" if kind == 0 else "a0", j)).then_inc(act_out, 1)
                    for u, (j, q) in enumerate(halves):
                        act.wait_ge(kk_mm, u + 1)
                        act.activation(t2[:, j, q * HN:(q + 1) * HN], ps[:, u, 0:HN], ACT.Copy, scale=float(HD), bias=EPS).then_inc(root_ready, 1)
                    act.wait_ge(root_ready, 4)
                    act.activation(flat(t2), flat(t2), ACT.Sqrt).then_inc(root_ready, 1)
                    act.wait_ge(cum_ready, 1)
                    act.activation(flat(Gd), flat(cumB), ACT.Exp, scale=-KAPPA).then_inc(exp_ready, 1)
                    act.activation(flat(Gi), flat(cumB), ACT.Exp, scale=KAPPA).then_inc(exp_ready, 1)
                    act.wait_ge(cum_ready, 2)
                    act.activation(flat(cumA), flat(sig), ACT.Exp, scale=-KAPPA).then_inc(exp_ready, 1)

                @block.vector
                def _(dve):
                    st = Steps(dve, v_steps)
                    hsp, hss = hs[:, :, 0:SEQ], hs[:, :, SEQ:TOK].rearrange("p c (b t) -> p c b t", b=NSEQ)
                    for c in range(8):
                        st.did(dve.tensor_tensor(hsp[:, c], hAp[:, c, 0:SEQ], hAp[:, c, 1:SEQ + 1], ALU.subtract))
                    st.did(dve.tensor_tensor(hss, hAs[:, :, :, 0:NEW], hAs[:, :, :, 1:NEW + 1], ALU.subtract))
                    st.settle()
                    for n, c in enumerate((6, 7, 2, 3, 0, 1, 4, 5)):
                        sem = lora_ready if n < 2 else v_steps
                        dve.scalar_tensor_tensor(hsp[:, c], hsp[:, c], col("mu", c), hAp[:, c, 1:SEQ + 1], ALU.mult, ALU.add).then_inc(sem, 1)
                        dve.scalar_tensor_tensor(hss[:, c], hss[:, c], col("mu", c), hAs[:, c, :, 1:NEW + 1], ALU.mult, ALU.add).then_inc(sem, 1)
                    st.n += 12
                    st.settle()
                    for j in range(2):
                        st.did(dve.tensor_scalar(kkn[:, j], k_[:, j], col("kk", j), None, ALU.mult))
                    st.settle()
                    dve.tensor_tensor(flat(t1), flat(kkn), flat(kkn), ALU.mult).then_inc(sq_ready, 1)
                    dve.wait_ge(root_ready, 5)
                    st.link(dve.reciprocal(flat(t2), flat(t2)))
                    st.did(dve.tensor_tensor(flat(kkn), flat(kkn), flat(t2), ALU.mult))
                    for j in range(2):
                        st.did(dve.tensor_scalar(t1[:, j], a_[:, j], -1.0, col("ka", j), ALU.add, ALU.mult))
                    st.settle()
                    st.link(dve.scalar_tensor_tensor(flat(k_), flat(t1), 1.0, flat(k_), ALU.add, ALU.mult))
                    st.link(dve.tensor_tensor(flat(t1), flat(r_), flat(k_), ALU.mult))
                    for j in range(2):
                        dve.tensor_scalar(t1[:, j], t1[:, j], col("rk", j), None, ALU.mult).then_inc(rk_ready, 1)
                    for u, (j, q) in enumerate(halves):
                        dve.wait_ge(rk_mm, u + 1)
                        dve.scalar_tensor_tensor(yadd[:, j, q * HN:(q + 1) * HN], ps[:, 4 + u, 0:HN], float(HD), v_[:, j, q * HN:(q + 1) * HN],
                                                 ALU.mult, ALU.mult).then_inc(rk_out, 1)
                    src, dst = sig, cumA
                    for n in range(6):
                        w = 1 << n
                        (sp_, ss_), (dp_, ds_) = chunked(src), chunked(dst)
                        st.did(dve.tensor_tensor(dp_[:, :, :, w:], sp_[:, :, :, w:], sp_[:, :, :, :-w], ALU.add))
                        st.did(dve.tensor_copy(dp_[:, :, :, 0:w], sp_[:, :, :, 0:w]))
                        if n < 3:
                            st.did(dve.tensor_tensor(ds_[:, :, :, w:], ss_[:, :, :, w:], ss_[:, :, :, :-w], ALU.add))
                            st.did(dve.tensor_copy(ds_[:, :, :, 0:w], ss_[:, :, :, 0:w]))
                        elif n == 3:
                            st.did(dve.tensor_copy(ds_, ss_))
                        st.settle()
                        src, dst = dst, (cumB if dst is cumA else cumA)
                    assert src is cumB
                    dve.sem_inc(cum_ready, 1)
                    dve.tensor_tensor(flat(sig), flat(cumB), flat(sig), ALU.subtract).then_inc(cum_ready, 1)
                    dve.wait_ge(exp_ready, 2)
                    st.did(dve.tensor_tensor(flat(Qr), flat(r_), flat(Gd), ALU.mult))
                    st.did(dve.tensor_tensor(flat(Kr), flat(k_), flat(Gi), ALU.mult))
                    dve.wait_ge(rk_out, 4)
                    st.link(dve.tensor_tensor(flat(t1), flat(kkn), flat(a_), ALU.mult))
                    st.did(dve.tensor_tensor(flat(Br), flat(t1), flat(Gi), ALU.mult))
                    dve.wait_ge(exp_ready, 3)
                    st.did(dve.scalar_tensor_tensor(flat(Ar), flat(kkn), -1.0, flat(cumA), ALU.mult, ALU.mult))
                    (gp, gs) = chunked(Gd)
                    st.did(dve.tensor_copy(GL[:, 0, 0:8, :].rearrange("p c j -> p j c").unsqueeze(3), gp[:, :, :, CH - 1:CH]))
                    st.did(dve.tensor_copy(GLs[:, 0].unsqueeze(3), gs[:, :, :, NEW - 1:NEW]))
                    st.settle()
                    for d, s in ((t1, Kr), (t2, Br)):
                        (dp_, ds_), (sp_, ss_) = chunked(d), chunked(s)
                        for j in range(2):
                            st.did(dve.tensor_tensor(dp_[:, j], sp_[:, j], gp[:, j, :, CH - 1:CH].broadcast_to([P, 8, CH]), ALU.mult))
                            st.did(dve.tensor_tensor(ds_[:, j], ss_[:, j], gs[:, j, :, NEW - 1:NEW].broadcast_to([P, NSEQ, NEW]), ALU.mult))
                    st.settle()

            cg = [range(0, 4), range(4, 8), range(8, 9)]
            heads4 = [(j, hf, slice(64 * hf, 64 * hf + 64)) for j in range(2) for hf in range(2)]

            def per_head(g):
                return [((n * 2 + j) * CH, c, j, p) for n, c in enumerate(cg[g]) for j, hf, p in heads4]

            def bank3(b, g, n=CH):
                w = len(cg[g]) * 2
                return ps[:, b, 0:w * n].rearrange("p (x t) -> p x t", t=n)

            def part3(i, g):
                return tm(i)[:, cg[g].start:cg[g].stop].rearrange("p c j t -> p (c j) t")

            def mask3(m, g):
                return bc(C(m + ("_s" if g == 2 else "_p")), 1, len(cg[g]) * 2)

            En_r, MT, PB, PK, V_t, A_t, K_t, B_t, MV = 5, 6, 7, 8, 9, 14, 15, 17, 18
            rkinds = [("turn", v_, V_t), ("turn", Ar, A_t), ("turn", t1, K_t), ("turn", t2, B_t),
                      ("En", Ar, Br, En_r), ("MT", Kr, Ar, MT), ("PB", Br, Qr, PB), ("PK", Kr, Qr, PK), ("MV", MT, V_t, MV)]
            runits = [(k, g) for k in rkinds for g in range(3)]
            on_act = lambda kind: kind in ("turn", "En", "MV", "KK")
            with stage(nc, "mm_done", "act_out", "dve_out") as (block, mm_done, act_out, dve_out):
                def counts(units):
                    n, out = {True: 0, False: 0}, []
                    for k, g in units:
                        n[on_act(k[0])] += 1
                        out.append((on_act(k[0]), n[on_act(k[0])]))
                    return out
                cnt = counts(runits)

                @block.tensor
                def _(pe):
                    for u, (k, g) in enumerate(runits):
                        if u >= 8:
                            a, n = cnt[u - 8]
                            pe.wait_ge(act_out if a else dve_out, n)
                        if k[0] == "MV" and g == 0:
                            pe.wait_ge(dve_out, cnt[u - 1][1])
                            pe.wait_ge(act_out, 3)
                        for x, c, j, p in per_head(g):
                            tk = slice(c * CH, (c + 1) * CH)
                            if k[0] == "turn":
                                lhsT, rhs = k[1][p, j, tk], C("id64")[p]
                            elif k[0] == "MV":
                                lhsT, rhs = tm(MT)[p, c, j], tm(V_t)[p, c, j]
                            else:
                                lhsT, rhs = k[1][p, j, tk], k[2][p, j, tk]
                            last = pe.matmul(ps[p, u % 8, x:x + CH], lhsT, rhs, start=True, stop=True)
                        last.then_inc(mm_done, 1)

                @block.scalar
                def _(act):
                    for u, (k, g) in enumerate(runits):
                        if on_act(k[0]):
                            act.wait_ge(mm_done, u + 1)
                            act.activation(part3(k[-1], g), bank3(u % 8, g), ACT.Copy, scale=-1.0 if k[0] == "En" else 1.0).then_inc(act_out, 1)

                @block.vector
                def _(dve):
                    for u, (k, g) in enumerate(runits):
                        if not on_act(k[0]):
                            dve.wait_ge(mm_done, u + 1)
                            dve.tensor_tensor(part3(k[-1], g), bank3(u % 8, g), mask3("SUt" if k[0] == "MT" else "U", g), ALU.mult).then_inc(dve_out, 1)

            cv = slot(21, 3).rearrange("p (c t) -> p c t", c=6)
            sg3 = slot(24, 3).rearrange("p (c t) -> p c t", c=6)
            qd_, kd_, vd_ = ch(21), ch(22), ch(23)
            nq, nk = ch(24), ch(25)
            nrm2 = slot(24, 2)
            rt2 = slot(29, 2)
            g_, beta = beta_g[:, 0], beta_g[:, 1]
            sp_m, sp_a, sp_e = gcol[:, 3], gcol[:, 4], gcol[:, 5]
            eg, et, beg = gcol[:, 0], gcol[:, 1], gcol[:, 2]
            alog = stat[:, 48:50]
            g8 = stat[:, 0:16].rearrange("p (j b) -> p j b", j=2)
            with stage(nc, "v_steps", "conv_ready", "sig_ready", "sqn_ready", "mm_done", "root_ready", "ab_ready", "sp_exp", "g_ready",
                       "gsum_done", "gexp_ready") as (block, v_steps, conv_ready, sig_ready, sqn_ready, mm_done, root_ready, ab_ready,
                                                      sp_exp, g_ready, gsum_done, gexp_ready):
                @block.vector
                def _(dve):
                    st = Steps(dve, v_steps)
                    st.link(dve.tensor_tensor(g_, g_, bc(cols[:, COLS["dt"][0]:COLS["dt"][0] + 2], 1, NCH), ALU.add))
                    st.link(dve.tensor_scalar(sp_m, g_, 0.0, None, ALU.max))
                    dve.scalar_tensor_tensor(sp_a, sp_m, 2.0, g_, ALU.mult, ALU.subtract).then_inc(ab_ready, 1)
                    for n in range(4):
                        for c in range(6):
                            xp, xs = hBp[:, c, n:n + SEQ], hBs[:, c, :, n:n + NEW]
                            dp_, ds_ = cv[:, c, 0:SEQ], cv[:, c, SEQ:TOK].rearrange("p (b t) -> p b t", b=NSEQ)
                            w = col("conv", n * 6 + c)
                            for d, x in ((dp_, xp), (ds_, xs)):
                                if n == 0:
                                    i = dve.tensor_scalar(d, x, w, None, ALU.mult)
                                else:
                                    i = dve.scalar_tensor_tensor(d, x, w, d, ALU.mult, ALU.add)
                                if n == 3:
                                    i.then_inc(conv_ready, 1)
                                else:
                                    st.did(i)
                        if n < 3:
                            st.settle()
                    dve.wait_ge(conv_ready, 12)
                    dve.wait_ge(sig_ready, 3)
                    st.link(dve.tensor_tensor(slot(21, 3), slot(21, 3), slot(24, 3), ALU.mult))
                    dve.tensor_tensor(nrm2, slot(21, 2), slot(21, 2), ALU.mult).then_inc(sqn_ready, 1)
                    dve.wait_ge(sig_ready, 4)
                    st.did(dve.tensor_tensor(flat(z_ch), flat(z_ch), slot(27), ALU.mult))
                    dve.wait_ge(sp_exp, 3)
                    st.link(dve.tensor_tensor(sp_m, sp_m, sp_e, ALU.add))
                    st.link(dve.scalar_tensor_tensor(g_, sp_m, -1.0, bc(alog, 1, NCH), ALU.mult, ALU.mult))
                    st.did(dve.tensor_tensor(g8, bc(g_[:, 8], 2, NSEQ), bc(C("seq_of"), 1, 2), ALU.mult))
                    su, gb = tm(26), tm(31)
                    for m, a, b in (("_p", 0, 8), ("_s", 8, 9)):
                        for j in range(2):
                            st.did(dve.tensor_tensor(su[:, a:b, j], bc(C("SU" + m), 1, b - a), bc(g_[:, a:b, j], 2, CH), ALU.mult))
                    st.did(dve.tensor_copy(gb.rearrange("p c j t -> p (c j) t"), bc(g_.rearrange("p c j -> p (c j)"), 2, CH)))
                    st.settle()
                    dve.sem_inc(g_ready, 1)
                    dve.wait_ge(root_ready, 10)
                    st.link(dve.reciprocal(rt2, rt2))
                    st.did(dve.scalar_tensor_tensor(flat(qd_), flat(qd_), HD ** -0.5, slot(29), ALU.mult, ALU.mult))
                    st.did(dve.tensor_tensor(flat(kd_), flat(kd_), slot(30), ALU.mult))
                    dve.wait_ge(gexp_ready, 4)
                    st.did(dve.scalar_tensor_tensor(beg, eg, -1.0, beta, ALU.mult, ALU.mult))
                    st.settle()

                @block.scalar
                def _(act):
                    act.wait_ge(conv_ready, 12)
                    for n in range(3):
                        act.activation(slot(24 + n), slot(21 + n), ACT.Sigmoid).then_inc(sig_ready, 1)
                    act.activation(slot(27), flat(z_ch), ACT.Sigmoid).then_inc(sig_ready, 1)
                    act.activation(beta, beta, ACT.Sigmoid).then_inc(sp_exp, 1)
                    act.wait_ge(ab_ready, 1)
                    act.activation(sp_e, sp_a, ACT.Exp, scale=-1.0).then_inc(root_ready, 1)
                    act.activation(alog, cols[:, COLS["a_log"][0]:COLS["a_log"][0] + 2], ACT.Exp).then_inc(sp_exp, 1)
                    act.wait_ge(root_ready, 1)
                    act.activation(sp_e, sp_e, ACT.Ln, bias=1.0).then_inc(sp_exp, 1)
                    for u in range(8):
                        act.wait_ge(mm_done, u + 1)
                        i, (j, q) = u // 4, halves[u % 4]
                        act.activation(ch(29 + i)[:, j, q * HN:(q + 1) * HN], ps[:, u, 0:HN], ACT.Copy, scale=float(HD), bias=EPS).then_inc(root_ready, 1)
                    act.wait_ge(root_ready, 9)
                    act.activation(rt2, rt2, ACT.Sqrt).then_inc(root_ready, 1)
                    act.wait_ge(gsum_done, 1)
                    act.activation(eg.rearrange("p c j -> p (c j)"), ps[:, 0, 0:18], ACT.Exp).then_inc(gexp_ready, 1)
                    act.activation(et.rearrange("p c j -> p (c j)"), ps[:, 0, 18:36], ACT.Exp).then_inc(gexp_ready, 1)
                    act.activation(GL[:, 1, 0:8, :].rearrange("p c j -> p (c j)"), ps[:, 0, 36:52], ACT.Exp).then_inc(gexp_ready, 1)
                    act.activation(GLs[:, 1].rearrange("p j b -> p (j b)"), ps[:, 0, 54:70], ACT.Exp).then_inc(gexp_ready, 1)

                @block.tensor
                def _(pe):
                    pe.wait_ge(sqn_ready, 1)
                    for u in range(8):
                        i, (j, q) = u // 4, halves[u % 4]
                        pe.matmul(ps[:, u, 0:HN], C("head_mean"), ch(24 + i)[:, j, q * HN:(q + 1) * HN], start=True, stop=True).then_inc(mm_done, 1)
                    pe.wait_ge(g_ready, 1)
                    pe.wait_ge(root_ready, 9)
                    for hf in range(2):
                        p = slice(64 * hf, 64 * hf + 64)
                        gp, gs = g_[p, 0:8].rearrange("p c j -> p (c j)"), g_[p, 8]
                        for at_, mat, rhs in ((0, "U_p", gp), (16, "U_s", gs), (18, "SU_p", gp), (34, "SU_s", gs),
                                              (36, "ones", gp), (54, "ones", g8[p].rearrange("p j b -> p (j b)"))):
                            n = rhs.shape[1]
                            last = pe.matmul(ps[p, 0, at_:at_ + n], C(mat)[p], rhs, start=True, stop=True)
                    last.then_inc(gsum_done, 1)

            En_g, ATT, Kd_t, Vd_t, KB_t, Qg = 6, 16, 25, 24, 27, 19
            dkinds = [("turn", kd_, Kd_t), ("turn", vd_, Vd_t), ("Dts", None, 29), ("Dst", None, 30), ("row", None, 33),
                      ("KKn", kd_, kd_, En_g), ("KQ", kd_, qd_, ATT)]
            dunits = [(k, g) for k in dkinds for g in range(3)]
            on_act2 = lambda kind: kind in ("turn", "Dts", "Dst", "row")
            with stage(nc, "mm_done", "act_out", "dve_out", "v_steps") as (block, mm_done, act_out, dve_out, v_steps):
                su, gb = tm(26), tm(31)
                na = sum(on_act2(k[0]) for k, g in dunits)

                @block.tensor
                def _(pe):
                    for u, (k, g) in enumerate(dunits):
                        if u >= 8:
                            v = u - 8
                            if v < na:
                                pe.wait_ge(act_out, v + 1)
                            else:
                                pe.wait_ge(dve_out, v - na + 1)
                        Um = C("U_s" if g == 2 else "U_p")
                        for x, c, j, p in per_head(g):
                            tk = slice(c * CH, (c + 1) * CH)
                            lhsT, rhs = {"turn": lambda: (k[1][p, j, tk], C("id64")[p]), "Dts": lambda: (Um[p], su[p, c, j]),
                                         "Dst": lambda: (su[p, c, j], Um[p]), "row": lambda: (gb[p, c, j], Um[p]),
                                         "KKn": lambda: (k[1][p, j, tk], k[2][p, j, tk]), "KQ": lambda: (k[1][p, j, tk], k[2][p, j, tk])}[k[0]]()
                            last = pe.matmul(ps[p, u % 8, x:x + CH], lhsT, rhs, start=True, stop=True)
                        last.then_inc(mm_done, 1)

                @block.scalar
                def _(act):
                    for u, (k, g) in enumerate(dunits[:na]):
                        act.wait_ge(mm_done, u + 1)
                        act.activation(part3(k[-1], g), bank3(u % 8, g), ACT.Copy if k[0] == "turn" else ACT.Exp).then_inc(act_out, 1)

                @block.vector
                def _(dve):
                    st = Steps(dve, v_steps)
                    dve.wait_ge(act_out, 6)
                    whole = lambda i: tm(i).rearrange("p c j t -> p (c j) t")
                    per_row = lambda a: bc(a.rearrange("p c j -> p (c j)"), 2, CH)
                    st.did(dve.tensor_tensor(whole(KB_t), whole(Kd_t), per_row(beg), ALU.mult))
                    st.did(dve.tensor_tensor(whole(Vd_t), whole(Vd_t), per_row(beta), ALU.mult))
                    st.settle()
                    st.did(dve.tensor_tensor(whole(Kd_t), whole(Kd_t), per_row(et), ALU.mult))
                    dve.wait_ge(act_out, na)
                    for u, (k, g) in enumerate(dunits[na:]):
                        dve.wait_ge(mm_done, na + u + 1)
                        dve.tensor_tensor(part3(k[-1], g), bank3((na + u) % 8, g), part3(29 if k[0] == "KKn" else 30, g), ALU.mult).then_inc(dve_out, 1)
                    for j in range(2):
                        st.did(dve.tensor_tensor(ch(Qg)[:, j].rearrange("p (c t) -> p c t", t=CH), qd_[:, j].rearrange("p (c t) -> p c t", t=CH),
                                                 tm(33)[:, :, j], ALU.mult))
                    dve.wait_ge(dve_out, 6)
                    st.did(dve.tensor_tensor(whole(En_g), whole(En_g), per_row(beta), ALU.mult))
                    for g in range(3):
                        st.did(dve.tensor_tensor(part3(ATT, g), part3(ATT, g), mask3("U", g), ALU.mult))
                    st.settle()

            TM, TTm, P1, Em = (10, 11), (12, 13), (21, 22), (23, 26)
            En = (En_r, En_g)
            steps = [(lv, m, g) for lv in range(6) for m in range(2) for g in range(3 if lv < 3 else 2)]
            with stage(nc, "em_ready", "eye_ready", "p1_done", "p1_out", "tt_done", "t_ready") as (
                    block, em_ready, eye_ready, p1_done, p1_out, tt_done, t_ready):
                place = {s: n for n, s in enumerate(steps)}

                @block.gpsimd
                def _(pool):
                    for lv in range(6):
                        for m in range(2):
                            if lv:
                                pool.wait_ge(p1_done, place[(lv - 1, m, 1 if lv > 3 else 2)] + 1)
                            pool.tensor_tensor(tm(Em[m]).rearrange("p c j t -> p (c j) t"), tm(En[m]).rearrange("p c j t -> p (c j) t"),
                                               bc(C("lev", lv), 1, 2 * NCH), ALU.mult).then_inc(em_ready, 1)

                @block.tensor
                def _(pe):
                    pe.wait_ge(eye_ready, 4)
                    for lv in range(6):
                        ns = [n for n, s in enumerate(steps) if s[0] == lv]
                        for n in ns:
                            _, m, g = steps[n]
                            pe.wait_ge(em_ready, 2 * lv + m + 1)
                            if lv:
                                pe.wait_ge(t_ready, 2 * place[(lv - 1, m, g)] + 2)
                            if n >= 2:
                                pe.wait_ge(p1_out, n - 1)
                            for x, c, j, p in per_head(g):
                                last = pe.matmul(ps[p, n % 2, x:x + CH], tm(Em[m])[p, c, j], tm(TTm[m])[p, c, j], start=True, stop=True)
                            last.then_inc(p1_done, 1)
                        for n in ns:
                            _, m, g = steps[n]
                            pe.wait_ge(p1_out, n + 1)
                            if n >= 3:
                                pe.wait_ge(t_ready, 2 * (n - 2))
                            b = 2 + 2 * (n % 3)
                            for x, c, j, p in per_head(g):
                                pe.matmul(ps[p, b, x:x + CH], tm(P1[m])[p, c, j], tm(TM[m])[p, c, j], start=True, stop=True)
                            for x, c, j, p in per_head(g):
                                last = pe.matmul(ps[p, b + 1, x:x + CH], tm(TM[m])[p, c, j], tm(P1[m])[p, c, j], start=True, stop=True)
                            last.then_inc(tt_done, 1)

                @block.scalar
                def _(act):
                    for n, (lv, m, g) in enumerate(steps):
                        act.wait_ge(p1_done, n + 1)
                        if lv:
                            act.wait_ge(tt_done, place[(lv - 1, m, g)] + 1)
                        act.copy(part3(P1[m], g), bank3(n % 2, g)).then_inc(p1_out, 1)

                @block.vector
                def _(dve):
                    for i in TM + TTm:
                        dve.tensor_copy(tm(i).rearrange("p c j t -> p (c j) t"), bc(C("id64"), 1, 2 * NCH)).then_inc(eye_ready, 1)
                    dve.wait_ge(eye_ready, 4)
                    for n, (lv, m, g) in enumerate(steps):
                        dve.wait_ge(tt_done, n + 1)
                        b = 2 + 2 * (n % 3)
                        if lv:
                            dve.wait_ge(t_ready, 2 * place[(lv - 1, m, g)] + 2)
                        dve.tensor_tensor(part3(TM[m], g), part3(TM[m], g), bank3(b, g), ALU.subtract).then_inc(t_ready, 1)
                        dve.tensor_tensor(part3(TTm[m], g), part3(TTm[m], g), bank3(b + 1, g), ALU.subtract).then_inc(t_ready, 1)

            WT, UU = (29, 30), (31, 33)
            wu = [(k, m, g) for m in range(2) for k in range(2) for g in range(3)]
            with stage(nc, "mm_done", "act_out", "dve_out") as (block, mm_done, act_out, dve_out):
                @block.tensor
                def _(pe):
                    for u, (k, m, g) in enumerate(wu):
                        if u >= 8:
                            pe.wait_ge(dve_out if u % 2 else act_out, (u - 8) // 2 + 1)
                        for x, c, j, p in per_head(g):
                            tt = tm(TTm[m])[p, c, j]
                            lhsT, rhs = (tm((A_t, KB_t)[m])[p, c, j], tt) if k == 0 else (tt, tm((MV, Vd_t)[m])[p, c, j])
                            last = pe.matmul(ps[p, u % 8, x:x + CH], lhsT, rhs, start=True, stop=True)
                        last.then_inc(mm_done, 1)

                def target(u):
                    k, m, g = wu[u]
                    return part3((WT, UU)[k][m], g), bank3(u % 8, g)

                @block.scalar
                def _(act):
                    for u in range(0, len(wu), 2):
                        act.wait_ge(mm_done, u + 1)
                        act.copy(*target(u)).then_inc(act_out, 1)

                @block.vector
                def _(dve):
                    for u in range(1, len(wu), 2):
                        dve.wait_ge(mm_done, u + 1)
                        dve.tensor_copy(*target(u)).then_inc(dve_out, 1)

            S = S_sb[:, :].rearrange("p (m j n) -> p m j n", m=2, j=2)
            SA = slot(21)[:, 0:512].rearrange("p (s m j n) -> p s m j n", s=2, m=2, j=2)
            Y = (14, 27)
            Qx = (Qr, ch(Qg))
            Px = (PB, ATT)
            Kx = (B_t, Kd_t)
            mh = [(m, j, p) for m in range(2) for j, hf, p in heads4]
            S0 = slot(10, 2)[:, 0:2048].rearrange("p (m j b n) -> p m j b n", m=2, j=2, b=NSEQ)
            with stage(nc, "s_ready", "ws_done", "sa_ready", "out_done", "ds_done", "y_out", "scaled", "state_out", "s0_in") as (
                    block, s_ready, ws_done, sa_ready, out_done, ds_done, y_out, scaled, state_out, s0_in):
                @block.tensor
                def _(pe):
                    for c in range(8):
                        tk = slice(c * CH, (c + 1) * CH)
                        bw, bo, bd = c % 2, 2 + c % 2, 4 + c % 2
                        at_ = lambda m, j: slice((m * 2 + j) * CH, (m * 2 + j + 1) * CH)
                        pe.wait_ge(s_ready, c + 1)
                        if c >= 2:
                            pe.wait_ge(sa_ready, 2 * (c - 1))
                            pe.wait_ge(y_out, 2 * (c - 1))
                        for m, j, p in mh:
                            last = pe.matmul(ps[p, bw, at_(m, j)], tm(WT[m])[p, c, j], S[p, m, j], start=True, stop=True)
                        last.then_inc(ws_done, 1)
                        pe.wait_ge(sa_ready, 2 * (c + 1))
                        for m, j, p in mh:
                            pe.matmul(ps[p, bd, at_(m, j)], tm(Kx[m])[p, c, j], SA[p, c % 2, m, j], start=True, stop=(m == 1))
                            if m == 0:
                                pe.matmul(ps[p, bd, at_(m, j)], tm(K_t)[p, c, j], tm(V_t)[p, c, j], start=False, stop=True)
                        for m, j, p in mh:
                            o = ps[p, bo, at_(m, j)]
                            pe.matmul(o, S[p, m, j], Qx[m][p, j, tk], start=True, stop=False)
                            last = pe.matmul(o, SA[p, c % 2, m, j], tm(Px[m])[p, c, j], start=False, stop=(m == 1))
                            if m == 0:
                                last = pe.matmul(o, tm(V_t)[p, c, j], tm(PK)[p, c, j], start=False, stop=True)
                        last.then_inc(out_done, 1)

                @block.vector
                def _(dve):
                    dve.memset(S, 0.0).then_inc(s_ready, 1)
                    dve.wait_ge(s_ready, 1)
                    for c in range(8):
                        dve.wait_ge(ws_done, c + 1)
                        for m in range(2):
                            dve.tensor_tensor(SA[:, c % 2, m], tm(UU[m])[:, c], ps[:, c % 2, m * 128:(m + 1) * 128].rearrange("p (j n) -> p j n", j=2),
                                              ALU.add).then_inc(sa_ready, 1)
                        dve.wait_ge(out_done, c + 1)
                        dve.tensor_tensor(S, S, bc(GL[:, :, c], 3, HD), ALU.mult).then_inc(scaled, 1)
                        dve.wait_ge(scaled, c + 1)
                        dve.tensor_tensor(S, S, ps[:, 4 + c % 2, 0:256].rearrange("p (m j n) -> p m j n", m=2, j=2), ALU.add).then_inc(s_ready, 1)
                        dve.wait_ge(s_ready, c + 2)

                @block.scalar
                def _(act):
                    for c in range(8):
                        act.wait_ge(out_done, c + 1)
                        for m in range(2):
                            act.copy(ch(Y[m])[:, :, c * CH:(c + 1) * CH],
                                     ps[:, 2 + c % 2, m * 128:(m + 1) * 128].rearrange("p (j t) -> p j t", j=2)).then_inc(y_out, 1)

                @block.sync
                def _(sp):
                    sp.dma_start(slot(10, 2)[:, 0:2048], at("states")).then_inc(s0_in, 16)
                    sp.wait_ge(s_ready, 9)
                    sp.dma_start(at("o_state_p"), S_sb[:, :]).then_inc(state_out, 16)
                    sp.wait_ge(state_out, 16)
                    sp.wait_ge(s0_in, 16)

            SAT = slot(21)[:, 512:768].rearrange("p (x t) -> p x t", x=4)
            SA1 = slot(21)[:, 0:256].rearrange("p (m j n) -> p m j n", m=2, j=2)
            SAx = slot(12, 2)[:, 0:2048].rearrange("p (x b n) -> p x b n", x=4, b=NSEQ)
            Vx = slot(22)[:, 0:1024].rearrange("p (j b n) -> p j b n", j=2, b=NSEQ)
            with stage(nc, "sat_done", "sat_out", "sa_done", "sa_ready", "x_ready", "y_done", "y_out", "ds_done", "s_ready", "state_out") as (
                    block, sat_done, sat_out, sa_done, sa_ready, x_ready, y_done, y_out, ds_done, s_ready, state_out):
                tk = lambda b: slice(SEQ + b * NEW, SEQ + (b + 1) * NEW)

                @block.tensor
                def _(pe):
                    for m, j, p in mh:
                        for b in range(NSEQ):
                            last = pe.matmul(ps[p, 0, (m * 2 + j) * CH + b * NEW:(m * 2 + j) * CH + (b + 1) * NEW], S0[p, m, j, b],
                                             tm(WT[m])[p, 8, j, b * NEW:(b + 1) * NEW], start=True, stop=True)
                    last.then_inc(sat_done, 1)
                    pe.wait_ge(sat_out, 1)
                    for m, j, p in mh:
                        x = m * 2 + j
                        last = pe.matmul(ps[p, 1, x * CH:(x + 1) * CH], SAT[p, x], C("id64")[p], start=True, stop=True)
                    last.then_inc(sa_done, 1)
                    pe.wait_ge(sa_ready, 2)
                    for m, j, p in mh:
                        x = m * 2 + j
                        pe.matmul(ps[p, 2, x * CH:(x + 1) * CH], SA1[p, m, j], tm(Px[m])[p, 8, j], start=True, stop=False)
                        if m == 0:
                            pe.matmul(ps[p, 2, x * CH:(x + 1) * CH], tm(V_t)[p, 8, j], tm(PK)[p, 8, j], start=False, stop=False)
                        for b in range(NSEQ):
                            last = pe.matmul(ps[p, 2, x * CH + b * NEW:x * CH + (b + 1) * NEW], S0[p, m, j, b], Qx[m][p, j, tk(b)],
                                             start=False, stop=(b == NSEQ - 1))
                    last.then_inc(y_done, 1)
                    pe.wait_ge(x_ready, 6)
                    for m, j, p in mh:
                        x = m * 2 + j
                        last = pe.matmul(ps[p, 4 + x, :], tm(Kx[m])[p, 8, j], SAx[p, x].rearrange("p b n -> p (b n)"), start=True, stop=(m == 1))
                        if m == 0:
                            last = pe.matmul(ps[p, 4 + x, :], tm(K_t)[p, 8, j], Vx[p, j].rearrange("p b n -> p (b n)"), start=False, stop=True)
                    last.then_inc(ds_done, 1)

                @block.scalar
                def _(act):
                    act.wait_ge(sat_done, 1)
                    act.copy(SAT.rearrange("p x t -> p (x t)"), ps[:, 0, 0:256]).then_inc(sat_out, 1)
                    act.wait_ge(y_done, 1)
                    for m in range(2):
                        act.copy(ch(Y[m])[:, :, SEQ:TOK], ps[:, 2, m * 128:(m + 1) * 128].rearrange("p (j t) -> p j t", j=2)).then_inc(y_out, 1)

                @block.vector
                def _(dve):
                    of = bc(C("seq_of"), 2, HD)
                    for j in range(2):
                        dve.tensor_tensor(Vx[:, j], bc(tm(V_t)[:, 8, j], 1, NSEQ), of, ALU.mult).then_inc(x_ready, 1)
                    dve.wait_ge(sa_done, 1)
                    for m in range(2):
                        dve.tensor_tensor(SA1[:, m], tm(UU[m])[:, 8], ps[:, 1, m * 128:(m + 1) * 128].rearrange("p (j n) -> p j n", j=2),
                                          ALU.add).then_inc(sa_ready, 1)
                    dve.wait_ge(sa_ready, 2)
                    for x in range(4):
                        dve.tensor_tensor(SAx[:, x], bc(SA1[:, x // 2, x % 2], 1, NSEQ), of, ALU.mult).then_inc(x_ready, 1)
                    dve.wait_ge(y_done, 1)
                    for x in range(4):
                        s = S0[:, x // 2, x % 2]
                        dve.tensor_tensor(s, s, bc(GLs[:, x // 2, x % 2], 2, HD), ALU.mult).then_inc(s_ready, 1)
                    dve.wait_ge(ds_done, 1)
                    dve.wait_ge(s_ready, 4)
                    for x in range(4):
                        s = S0[:, x // 2, x % 2]
                        dve.tensor_tensor(s, s, ps[:, 4 + x, :].rearrange("p (b n) -> p b n", b=NSEQ), ALU.add).then_inc(s_ready, 1)

                @block.sync
                def _(sp):
                    sp.wait_ge(s_ready, 8)
                    sp.dma_start(at("o_state_s"), slot(10, 2)[:, 0:2048]).then_inc(state_out, 16)
                    sp.wait_ge(state_out, 16)

            yr, yg = ch(14), ch(27)
            sqr, rtr, sqg, rtg = ch(21), ch(22), ch(23), ch(24)
            sqc, rtc = slot(5, 2), slot(7, 2)
            wo = slot(9, 8)[:, 0:8192].rearrange("p (k n) -> p k n", k=KC)
            with stage(nc, "v_steps", "mean_done", "yc_ready", "sq_ready", "mm_done", "root_ready", "cat_ready") as (
                    block, v_steps, mean_done, yc_ready, sq_ready, mm_done, root_ready, cat_ready):
                vu = [("g", u) for u in range(4)] + [("c", u) for u in range(8)] + [("r", u) for u in range(4)]

                @block.tensor
                def _(pe):
                    for u, (j, q) in enumerate(halves):
                        pe.matmul(ps[:, u, 0:HN], C("head_mean"), yr[:, j, q * HN:(q + 1) * HN], start=True, stop=True).then_inc(mean_done, 1)
                    for n, (k, u) in enumerate(vu):
                        pe.wait_ge(sq_ready, {"g": 1, "c": 2, "r": 3}[k])
                        if n >= 4:
                            pe.wait_ge(root_ready, n - 3)
                        src = {"g": slot(23), "c": sqc, "r": slot(21)}[k][:, u * HN:(u + 1) * HN]
                        pe.matmul(ps[:, 4 + n % 4, 0:HN], C("all_mean" if k == "c" else "head_mean"), src, start=True, stop=True).then_inc(mm_done, 1)

                @block.scalar
                def _(act):
                    for n, (k, u) in enumerate(vu):
                        act.wait_ge(mm_done, n + 1)
                        d = {"g": slot(24), "c": rtc, "r": slot(22)}[k][:, u * HN:(u + 1) * HN]
                        act.activation(d, ps[:, 4 + n % 4, 0:HN], ACT.Copy, bias=64e-5 if k == "r" else EPS).then_inc(root_ready, 1)
                    act.wait_ge(root_ready, 16)
                    for n, d in enumerate((slot(24), rtc, slot(22))):
                        act.activation(d, d, ACT.Sqrt).then_inc(root_ready, 1)

                @block.vector
                def _(dve):
                    st = Steps(dve, v_steps)
                    OCf = slot(2, 2)
                    dve.tensor_tensor(flat(sqg), flat(yg), flat(yg), ALU.mult).then_inc(sq_ready, 1)
                    dve.tensor_tensor(sqc, OCf, OCf, ALU.mult).then_inc(sq_ready, 1)
                    for u, (j, q) in enumerate(halves):
                        dve.wait_ge(mean_done, u + 1)
                        v = yr[:, j, q * HN:(q + 1) * HN]
                        st.did(dve.tensor_tensor(v, v, ps[:, u, 0:HN], ALU.subtract))
                    st.settle()
                    dve.tensor_tensor(flat(sqr), flat(yr), flat(yr), ALU.mult).then_inc(sq_ready, 1)
                    st.link(dve.tensor_tensor(stat[:, 50:51], col("subln"), col("lam_rest"), ALU.mult))
                    dve.wait_ge(root_ready, 17)
                    st.link(dve.reciprocal(flat(rtg), flat(rtg)))
                    st.link(dve.tensor_tensor(flat(rtg), flat(rtg), flat(z_ch), ALU.mult))
                    st.link(dve.tensor_tensor(flat(rtg), flat(rtg), flat(yg), ALU.mult))
                    st.did(dve.tensor_scalar(slot(1), flat(rtg), col("dn_g"), None, ALU.mult))
                    dve.wait_ge(root_ready, 18)
                    st.link(dve.reciprocal(rtc, rtc))
                    st.did(dve.scalar_tensor_tensor(OCf, OCf, stat[:, 50:51], rtc, ALU.mult, ALU.mult))
                    dve.wait_ge(root_ready, 19)
                    st.link(dve.reciprocal(flat(rtr), flat(rtr)))
                    st.link(dve.tensor_tensor(flat(yr), flat(yr), flat(rtr), ALU.mult))
                    for j in range(2):
                        st.did(dve.tensor_scalar(yr[:, j], yr[:, j], col("ln_g", j), col("ln_b", j), ALU.mult, ALU.add))
                    st.settle()
                    st.link(dve.tensor_tensor(flat(yr), flat(yr), flat(yadd), ALU.add))
                    st.did(dve.tensor_tensor(slot(0), flat(yr), flat(gate), ALU.mult))
                    st.settle()

            with stage(nc, "wo_in", "mm_done", "x_steps") as (block, wo_in, mm_done, x_steps):
                ou = [(i, n) for i in range(TILES) for n in range(2)]

                @block.sync
                def _(sp):
                    sp.dma_start(wo, at("w_out").rearrange("(k p) n -> p k n", p=P)).then_inc(wo_in, 16)

                @block.tensor
                def _(pe):
                    pe.wait_ge(wo_in, 16)
                    for u, (i, n) in enumerate(ou):
                        if u >= 8:
                            pe.wait_ge(x_steps, u - 7)
                        w = min(P, TOK - i * P)
                        for k in range(KC):
                            last = pe.matmul(ps[0:w, u % 8, :], cat[:, k, i * P:i * P + w], wo[:, k, n * 512:(n + 1) * 512], start=(k == 0), stop=(k == KC - 1))
                        last.then_inc(mm_done, 1)

                @block.vector
                def _(dve):
                    for u, (i, n) in enumerate(ou):
                        w = min(P, TOK - i * P)
                        dve.wait_ge(mm_done, u + 1)
                        d = x_sb[0:w, i, n * 512:(n + 1) * 512]
                        dve.tensor_tensor(d, d, ps[0:w, u % 8, :], ALU.add).then_inc(x_steps, 1)

            norm_transposed("ffn_g")
            qT = slot(0, 8).rearrange("p (c t) -> p c t", c=16)
            keys = slot(8, 2)[:, 0:2048].rearrange("p (c n) -> p c n", c=16)
            qu = [(c, q) for c in range(16) for q in range(2)]
            with stage(nc, "keys_in", "wq_in0", "wq_in1", "mm_done", "act_out", "dve_out") as (
                    block, keys_in, wq_in0, wq_in1, mm_done, act_out, dve_out):
                wq_in = (wq_in0, wq_in1)
                wqv = at("pk_wq").rearrange("(k p) n -> p k n", p=P)

                @block.sync
                def _(sp):
                    for g in range(4):
                        if g >= 2:
                            sp.wait_ge(mm_done, 8 * (g - 1))
                        sp.dma_start(W2[:, g % 2], wqv[:, :, g * 512:(g + 1) * 512]).then_inc(wq_in[g % 2], 16)
                    sp.dma_start(keys, at("pk_keys")).then_inc(keys_in, 16)
                    sp.wait_ge(keys_in, 16)

                @block.tensor
                def _(pe):
                    for u, (c, q) in enumerate(qu):
                        g = c // 4
                        if u % 8 == 0:
                            pe.wait_ge(wq_in[g % 2], 16 * (g // 2 + 1))
                        if u >= 8:
                            pe.wait_ge(dve_out if u % 2 else act_out, (u - 8) // 2 + 1)
                        for k in range(KC):
                            last = pe.matmul(ps[:, u % 8, 0:HN], W2[:, g % 2, k, (c % 4) * P:(c % 4 + 1) * P], xnT[:, k, q * HN:(q + 1) * HN],
                                             start=(k == 0), stop=(k == KC - 1))
                        last.then_inc(mm_done, 1)

                @block.scalar
                def _(act):
                    for u in range(0, 32, 2):
                        act.wait_ge(mm_done, u + 1)
                        act.copy(qT[:, qu[u][0], 0:HN], ps[:, u % 8, 0:HN]).then_inc(act_out, 1)

                @block.vector
                def _(dve):
                    for u in range(1, 32, 2):
                        dve.wait_ge(mm_done, u + 1)
                        dve.tensor_copy(qT[:, qu[u][0], HN:TOK], ps[:, u % 8, 0:HN]).then_inc(dve_out, 1)

            SC = slot(10, 4)[:, 0:4096].rearrange("p (s c n) -> p s c n", s=2, c=16)
            SC2 = slot(14, 2)[:, 0:2048].rearrange("p (c n) -> p c n", c=16)
            cand = slot(16, 2)[:, 0:2048].rearrange("p (h n) -> p h n", h=PK_HEADS)
            cand2 = slot(18, 2)[:, 0:2048].rearrange("p (h n) -> p h n", h=PK_HEADS)
            rt = slot(26, 3)
            SV = rt[:, 0:256].rearrange("p (c n) -> p c n", c=16)
            SI = rt[:, 256:512].bitcast(U32).rearrange("p (c n) -> p c n", c=16)
            SIf = rt[:, 512:768].rearrange("p (h c n) -> p h c n", h=PK_HEADS, c=2)
            TV = rt[:, 768:896].rearrange("p (h n) -> p h n", h=PK_HEADS)
            TI = rt[:, 896:1024].bitcast(U32).rearrange("p (h n) -> p h n", h=PK_HEADS)
            TA = rt[:, 1024:1280].bitcast(U32).rearrange("p (c n) -> p c n", c=2)
            TAf = rt[:, 1280:1536].rearrange("p (c n) -> p c n", c=2)
            route = rt[:, 1536:1920].rearrange("p (k n) -> p k n", k=3)
            ex = rt[:, 1920:2048].rearrange("p (h n) -> p h n", h=PK_HEADS)
            sums = rt[:, 2048:2064]
            routeT = slot(32, 2)[:, 0:3 * TOKP].rearrange("p (k t) -> p k t", k=3)
            with stage(nc, "s_done", "s_out", "v_steps", "shifted", "exp_done", "route_ready", "t_done", "t_out", "sc_free") as (
                    block, s_done, s_out, v_steps, shifted, exp_done, route_ready, t_done, t_out, sc_free):
                @block.tensor
                def _(pe):
                    for i in range(TILES + 1):
                        if i < TILES:
                            w = min(P, TOK - i * P)
                            if i >= 1:
                                pe.wait_ge(s_out, 4 * i)
                            for b in range(4):
                                for n in range(4):
                                    c = b * 4 + n
                                    last = pe.matmul(ps[0:w, b, n * P:(n + 1) * P], qT[:, c, i * P:i * P + w], keys[:, c, :], start=True, stop=True)
                                last.then_inc(s_done, 1)
                        if i >= 1:
                            w = min(P, TOK - (i - 1) * P)
                            pe.wait_ge(route_ready, i)
                            for k in range(3):
                                last = pe.transpose(ps[:, 4 + i % 2, k * P:k * P + w], route[0:w, k, :], C("ident")[0:w, 0:w])
                            last.then_inc(t_done, 1)

                @block.scalar
                def _(act):
                    for i in range(TILES + 1):
                        if i < TILES:
                            w = min(P, TOK - i * P)
                            if i >= 2:
                                act.wait_ge(sc_free, i - 1)
                            for b in range(4):
                                act.wait_ge(s_done, 4 * i + b + 1)
                                act.copy(SC[0:w, i % 2, 4 * b:4 * b + 4], ps[0:w, b, :].rearrange("p (c n) -> p c n", c=4)).then_inc(s_out, 1)
                        if i >= 1:
                            w = min(P, TOK - (i - 1) * P)
                            act.wait_ge(shifted, i)
                            act.activation(ex[0:w], ex[0:w], ACT.Exp).then_inc(exp_done, 1)
                            act.wait_ge(t_done, i)
                            act.copy(routeT[:, :, (i - 1) * P:(i - 1) * P + w],
                                     ps[:, 4 + i % 2, 0:3 * P].rearrange("p (k t) -> p k t", k=3)[:, :, 0:w]).then_inc(t_out, 1)

                @block.vector
                def _(dve):
                    st = Steps(dve, v_steps)
                    for i in range(TILES):
                        w = min(P, TOK - i * P)
                        r = slice(0, w)
                        sc = SC[r, i % 2]
                        dve.wait_ge(s_out, 4 * (i + 1))
                        if i:
                            dve.wait_ge(t_done, i)

                        def best16(n, vals, idx, src, rest):
                            for c in range(n):
                                st.did(dve.max(vals[r, c, 0:8], src[:, c]))
                            st.settle()
                            for c in range(n):
                                st.did(dve.max_index(idx[r, c, 0:8], vals[r, c, 0:8], src[:, c]))
                                st.did(dve.match_replace(rest[r, c], vals[r, c, 0:8], src[:, c], -3.0e38))
                            st.settle()
                            for c in range(n):
                                st.did(dve.max(vals[r, c, 8:16], rest[r, c]))
                            st.settle()
                            for c in range(n):
                                st.did(dve.max_index(idx[r, c, 8:16], vals[r, c, 8:16], rest[r, c]))
                            st.settle()
                        best16(16, SV, SI, sc, SC2)
                        dve.sem_inc(sc_free, 1)
                        v = SV.rearrange("p (h c) n -> p h c n", c=2)[r]
                        st.did(dve.tensor_tensor(cand[r].rearrange("p h (a b) -> p h a b", a=TOPK), bc(v[:, :, 0], 3, TOPK), bc(v[:, :, 1], 2, TOPK), ALU.add))
                        st.did(dve.tensor_copy(SIf[r].rearrange("p h c n -> p (h c n)"), SI[r].rearrange("p c n -> p (c n)")))
                        st.settle()
                        best16(PK_HEADS, TV, TI, cand[r], cand2)
                        dve.tensor_tensor(ex[r], TV[r], TV[r, :, 0:1].broadcast_to([w, PK_HEADS, TOPK]), ALU.subtract).then_inc(shifted, 1)
                        ti = TI[r].rearrange("p h n -> p (h n)")
                        st.did(dve.tensor_scalar(TA[r, 0], ti, 4, None, ALU.logical_shift_right))
                        st.did(dve.tensor_scalar(TA[r, 1], ti, 15, None, ALU.bitwise_and))
                        st.settle()
                        st.link(dve.tensor_copy(TAf[r], TA[r]))
                        for c in range(2):
                            e = (cand, cand2)[c][r].rearrange("p h (j a) -> p (h j) a", a=TOPK)
                            st.did(dve.tensor_tensor(e, bc(C("iota")[r, 0:TOPK], 1, P), bc(TAf[r, c], 2, TOPK), ALU.is_equal))
                        st.settle()
                        for c in range(2):
                            e = (cand, cand2)[c][r].rearrange("p h (j a) -> p h j a", a=TOPK)
                            st.did(dve.tensor_tensor(e, e, bc(SIf[r, :, c], 2, TOPK), ALU.mult))
                        st.settle()
                        for c in range(2):
                            e = (cand, cand2)[c][r].rearrange("p h (j a) -> p (h j) a", a=TOPK)
                            st.did(dve.tensor_reduce(route[r, c], e, AX.X, ALU.add))
                        dve.wait_ge(exp_done, i + 1)
                        st.link(dve.tensor_reduce(sums[r, 0:8], ex[r], AX.X, ALU.add))
                        st.link(dve.reciprocal(sums[r, 8:16], sums[r, 0:8]))
                        dve.tensor_tensor(route[r, 2].rearrange("p (h n) -> p h n", h=PK_HEADS), ex[r], bc(sums[r, 8:16], 2, TOPK), ALU.mult).then_inc(route_ready, 1)
                    dve.wait_ge(t_out, TILES)

            TG = 32
            NTG = TOK // TG
            OCT = 8
            stg = slot(4, 8)[:, 0:2 * P * TG].rearrange("p (s e t) -> p s e t", s=2, e=P)
            A1 = slot(12, 2)[:, 0:2 * OCT * P].rearrange("p (s t n) -> p s t n", s=2, t=OCT)
            B1 = slot(14, 2)[:, 0:2 * OCT * P].rearrange("p (s t n) -> p s t n", s=2, t=OCT)
            cur = stat[:, 0:48].rearrange("p (s k t) -> p s k t", s=2, k=3)
            gd = t["g_scratch"]
            with stage(nc, "cur_ready", "ab_free", "ab_ready", "bank_free", "g_done", "g_out", "g_saved0", "g_saved1") as (
                    block, cur_ready, ab_free, ab_ready, bank_free, g_done, g_out, g_saved0, g_saved1):
                g_saved = (g_saved0, g_saved1)
                PER = TG // OCT

                @block.vector
                def _(dve):
                    dve.sem_inc(ab_free, 2)
                    with dve.Fori(0, TOK // (2 * OCT)) as o2:
                        for s in range(2):
                            o = o2 * 2 + s
                            dve.wait_ge(ab_free, o + 1)
                            dve.tensor_copy(cur[:, s], routeT[:, :, bass.ds(o * OCT, OCT)]).then_inc(cur_ready, 1)
                            dve.wait_ge(cur_ready, o + 1)
                            for k in range(OCT):
                                dve.tensor_scalar(A1[:, s, k], C("iota"), cur[:, s, 0, k:k + 1], None, ALU.is_equal).then_inc(ab_ready, 1)
                                dve.tensor_scalar(B1[:, s, k], C("iota"), cur[:, s, 1, k:k + 1], cur[:, s, 2, k:k + 1], ALU.is_equal,
                                                  ALU.mult).then_inc(ab_ready, 1)

                @block.tensor
                def _(pe):
                    pe.sem_inc(bank_free, 2)
                    with pe.Fori(0, TOK // (2 * OCT)) as o2:
                        for s in range(2):
                            o = o2 * 2 + s
                            pe.wait_ge(bank_free, o + 1)
                            pe.wait_ge(ab_ready, (o + 1) * 2 * OCT)
                            for k in range(OCT):
                                last = pe.matmul(ps[:, 2 * s + k // 4, (k % 4) * P:(k % 4 + 1) * P], A1[:, s, k], B1[:, s, k], start=True, stop=True)
                                if k % 4 == 3:
                                    last.then_inc(g_done, 1)
                            pe.wait_ge(g_done, (o + 1) * 2)
                            pe.sem_inc(ab_free, 1)

                @block.scalar
                def _(act):
                    for sg in range(2):
                        act.sem_inc(g_saved[sg], 16)
                    with act.Fori(0, NTG // 2) as it:
                        for sg in range(2):
                            act.wait_ge(g_saved[sg], it * 16 + 16)
                            for n in range(2 * PER):
                                s = (n // 2) % 2
                                act.wait_ge(g_done, it * (4 * PER) + sg * 2 * PER + n + 1)
                                act.copy(stg[:, sg, :, n * 4:n * 4 + 4], ps[:, 2 * s + n % 2, :].rearrange("p (t e) -> p e t", t=4)).then_inc(g_out, 1)
                                if n % 2:
                                    act.wait_ge(g_out, it * (4 * PER) + sg * 2 * PER + n + 1)
                                    act.sem_inc(bank_free, 1)

                @block.sync
                def _(sp):
                    with sp.Fori(0, NTG // 2) as it:
                        for sg in range(2):
                            sp.wait_ge(g_out, it * (4 * PER) + (sg + 1) * 2 * PER)
                            sp.dma_start(gd[:, bass.ds(it * 2 + sg, 1)].rearrange("p g e t -> p (g e t)"),
                                         stg[:, sg].rearrange("p e t -> p (e t)")).then_inc(g_saved[sg], 16)
                    for sg in range(2):
                        sp.wait_ge(g_saved[sg], NTG // 2 * 16 + 16)

            PAIRS = PK_KEYS // 2
            acc = slot(0, 4).rearrange("p (d q t) -> p d q t", d=KC, q=2)
            ub = slot(4, 4)[:, 0:4096].rearrange("p (s e k n) -> p s e k n", s=2, e=2, k=KC)
            vb = slot(8, 4)[:, 0:4096].rearrange("p (s e n) -> p s e n", s=2, e=2)
            Gt = slot(12, 2).rearrange("p (s g e t) -> p s g e t", s=2, g=NTG, e=2)
            GH = slot(14, 2).rearrange("p (s e t) -> p s e t", s=2, e=2)
            uv = at("pk_u").rearrange("(n e) p x -> n p e x", e=2)
            vv = at("pk_v").rearrange("(p n e) d -> n p (e d)", p=P, e=2)
            with stage(nc, "u_in0", "u_in1", "vg_in0", "vg_in1", "h_done", "gelu_done", "c_ready", "o_done", "o_free", "pair_done", "zeroed") as (
                    block, u_in0, u_in1, vg_in0, vg_in1, h_done, gelu_done, c_ready, o_done, o_free, pair_done, zeroed):
                u_in, vg_in = (u_in0, u_in1), (vg_in0, vg_in1)

                @block.sync
                def _(sp):
                    def load_u(k, s):
                        sp.dma_start(ub[:, s].rearrange("p e k n -> p e (k n)"), uv[bass.ds(k, 1)].rearrange("o p e x -> (o p) e x")).then_inc(u_in[s], 16)

                    def load_vg(k, s):
                        sp.dma_start(vb[:, s].rearrange("p e n -> p (e n)"), vv[bass.ds(k, 1)].rearrange("o p x -> (o p) x")).then_inc(vg_in[s], 16)
                        sp.dma_start(Gt[:, s].rearrange("p g e t -> p g (e t)"),
                                     gd[:, :, bass.ds(k * 2, 2)].rearrange("p g e t -> p g (e t)")).then_inc(vg_in[s], 16)
                    for k in range(2):
                        load_u(k, k)
                        load_vg(k, k)
                    with sp.Fori(0, PAIRS // 2 - 1) as i:
                        for s in range(2):
                            sp.wait_ge(h_done, i * 8 + 4 * (s + 1))
                            load_u(i * 2 + (2 + s), s)
                        for s in range(2):
                            sp.wait_ge(pair_done, i * 2 + (s + 3))
                            load_vg(i * 2 + (2 + s), s)

                @block.tensor
                def _(pe):
                    pe.sem_inc(pair_done, 2)
                    pe.wait_ge(zeroed, 1)

                    def hidden(k, half, s):
                        pe.wait_ge(u_in[s], half * 16 + 16)
                        pe.wait_ge(gelu_done, k * 4 + 4)
                        for e in range(2):
                            for q in range(2):
                                for c in range(KC):
                                    last = pe.matmul(ps[:, 2 * e + q, 0:HN], ub[:, s, e, c], xnT[:, c, q * HN:(q + 1) * HN],
                                                     start=(c == 0), stop=(c == KC - 1))
                                last.then_inc(h_done, 1)

                    def output(k, half, s):
                        pe.wait_ge(vg_in[s], half * 32 + 32)
                        pe.wait_ge(c_ready, k * 2 + 2)
                        for u in range(16):
                            d, q = u // 2, u % 2
                            pe.wait_ge(o_free, k * 16 + (u + 1))
                            for e in range(2):
                                last = pe.matmul(ps[:, 4 + u % 4, 0:HN], vb[:, s, e, d * P:(d + 1) * P], GH[:, s, e, q * HN:(q + 1) * HN],
                                                 start=(e == 0), stop=(e == 1))
                            last.then_inc(o_done, 1)
                        pe.wait_ge(o_done, k * 16 + 16)
                        pe.sem_inc(pair_done, 1)
                    hidden(0, 0, 0)
                    with pe.Fori(0, PAIRS // 2 - 1) as i:
                        hidden(i * 2 + 1, i, 1)
                        output(i * 2, i, 0)
                        hidden(i * 2 + 2, i + 1, 0)
                        output(i * 2 + 1, i, 1)
                    n = PAIRS // 2 - 1
                    hidden(2 * n + 1, n, 1)
                    output(2 * n, n, 0)
                    output(2 * n + 1, n, 1)

                @block.scalar
                def _(act):
                    act.sem_inc(gelu_done, 4)
                    with act.Fori(0, PAIRS // 2) as i:
                        for s in range(2):
                            k = i * 2 + s
                            act.wait_ge(pair_done, k + 1)
                            for n in range(4):
                                e, q = n // 2, n % 2
                                act.wait_ge(h_done, k * 4 + (n + 1))
                                act.activation(GH[:, s, e, q * HN:(q + 1) * HN], ps[:, n, 0:HN], ACT.Gelu).then_inc(gelu_done, 1)

                @block.vector
                def _(dve):
                    dve.sem_inc(o_free, 4)
                    dve.memset(slot(0, 4), 0.0).then_inc(zeroed, 1)
                    dve.wait_ge(zeroed, 1)
                    with dve.Fori(0, PAIRS // 2) as i:
                        for s in range(2):
                            k = i * 2 + s
                            dve.wait_ge(vg_in[s], i * 32 + 32)
                            for e in range(2):
                                dve.wait_ge(gelu_done, k * 4 + (2 * e + 6))
                                h = GH[:, s, e].rearrange("p (g t) -> p g t", t=TG)
                                dve.tensor_tensor(h, h, Gt[:, s, :, e], ALU.mult).then_inc(c_ready, 1)
                            dve.wait_ge(o_free, k * 16 + 4)
                            for u in range(16):
                                d, q = u // 2, u % 2
                                dve.wait_ge(o_done, k * 16 + (u + 1))
                                dve.tensor_tensor(acc[:, d, q], acc[:, d, q], ps[:, 4 + u % 4, 0:HN], ALU.add).then_inc(o_free, 1)

            with stage(nc, "t_done", "x_ready") as (block, t_done, x_ready):
                accT = slot(0, 4).rearrange("p (d t) -> p d t", d=KC)

                @block.tensor
                def _(pe):
                    for u in range(2 * TILES):
                        i, n = u // 2, u % 2
                        w = min(P, TOK - i * P)
                        if u >= 8:
                            pe.wait_ge(x_ready, u - 7)
                        for d in range(4):
                            last = pe.transpose(ps[0:w, u % 8, d * P:(d + 1) * P], accT[:, n * 4 + d, i * P:i * P + w], C("ident"))
                        last.then_inc(t_done, 1)

                @block.vector
                def _(dve):
                    for u in range(2 * TILES):
                        i, n = u // 2, u % 2
                        w = min(P, TOK - i * P)
                        dve.wait_ge(t_done, u + 1)
                        d = x_sb[0:w, i, n * 512:(n + 1) * 512]
                        dve.tensor_tensor(d, d, ps[0:w, u % 8, :], ALU.add).then_inc(x_ready, 1)


        with stage(nc, "y_out") as (block, y_out):
            @block.sync
            def _(sp):
                sp.dma_start(t["o_y"].rearrange("(i p) d -> p i d", p=P), x_sb[:, :, :]).then_inc(y_out, 16)
                sp.wait_ge(y_out, 16)


_OUTS = [("o_y", (TOKP, D)), ("o_kp", (DEPTH, SEQ, 512)), ("o_vp", (DEPTH, SEQ, 512)),
         ("o_ks", (DEPTH, SAMP, 512)), ("o_vs", (DEPTH, SAMP, 512)),
         ("o_state_p", (DEPTH, P, 256)), ("o_state_s", (DEPTH, P, 2048)), ("o_tails", (DEPTH, P, 234))]

_SCRATCH = [("rel_scratch", (P, H * (REL + 1))), ("g_scratch", (P, TOK // 32, P, 32))]


def lay_out(i):
    f = lambda n: np.ascontiguousarray(np.asarray(i[n], dtype=None))
    a = {}
    a["x_prompt"] = f("x_prompt").reshape(SEQ, D)
    a["x_sample"] = f("x_sample").reshape(SAMP, D)
    a["cache_k"], a["cache_v"] = f("cache_k"), f("cache_v")
    a["page_table"] = f("page_table")
    a["w_in"], a["w_out"], a["rel_bias"] = f("w_in"), f("w_out"), f("rel_bias")
    per = lambda n: f(n).reshape(DEPTH, -1, P).transpose(0, 2, 1)
    cols = np.zeros((DEPTH, P, NCOL), np.float32)

    def put(name, v):
        o, n = COLS[name]
        cols[:, :, o:o + n] = v
    for name, src in (("mix_g", "rms_mix_g"), ("ffn_g", "rms_ffn_g"), ("mu", "rw_mu"), ("w0", "rw_w0"), ("a0", "rw_a0"),
                      ("kk", "rw_kk"), ("ka", "rw_ka"), ("rk", "rw_rk"), ("ln_g", "rw_ln_g"), ("ln_b", "rw_ln_b"),
                      ("conv", "dn_conv_w"), ("subln", "df_subln_g")):
        put(name, per(src))
    put("dn_g", np.tile(f("dn_norm_g"), (1, 2))[:, :, None])
    halves = lambda n: np.repeat(f(n).reshape(DEPTH, 2, 2).transpose(0, 2, 1), 64, axis=1)
    put("a_log", halves("dn_a_log"))
    put("dt", halves("dn_dt_bias"))
    init = np.array([0.8 - 0.6 * math.exp(-0.3 * l) for l in range(DEPTH)], np.float32)
    put("lam_init", init[:, None, None])
    put("lam_rest", np.array([1.0 - (0.8 - 0.6 * math.exp(-0.3 * l)) for l in range(DEPTH)], np.float32)[:, None, None])
    a["cols"] = cols
    a["rows"] = np.concatenate([f("df_qn_g").reshape(DEPTH, P), f("df_kn_g").reshape(DEPTH, P)]
                               + [f(n) for n in ("df_lq1", "df_lk1", "df_lq2", "df_lk2")], axis=1)
    a["lora"] = np.concatenate([np.concatenate([f("rw_w2"), f("rw_a2")], axis=1), f("rw_g2")], axis=2)
    shift = f("state_rwkv_shift").reshape(DEPTH, NSEQ, 8, P).transpose(0, 3, 2, 1).reshape(DEPTH, P, 64)
    conv = f("state_dn_conv").reshape(DEPTH, NSEQ, 3, 6, P).transpose(0, 4, 3, 1, 2).reshape(DEPTH, P, 144)
    a["tails"] = np.concatenate([shift, conv], axis=2)
    sr = f("state_rwkv").reshape(DEPTH, NSEQ, 2, 2, HD, HD).transpose(0, 3, 5, 2, 1, 4).reshape(DEPTH, P, 1024)
    sd = f("state_dn").reshape(DEPTH, NSEQ, 2, 2, HD, HD).transpose(0, 3, 4, 2, 1, 5).reshape(DEPTH, P, 1024)
    a["states"] = np.concatenate([sr, sd], axis=2)
    a["pk_wq"] = f("pk_wq")
    a["pk_keys"] = f("pk_keys").transpose(0, 4, 1, 2, 3).reshape(DEPTH, P, 16 * P)
    a["pk_u"] = f("pk_u").reshape(DEPTH, P, P, KC, P).transpose(0, 2, 4, 3, 1).reshape(DEPTH, P, P, D)
    a["pk_v"] = f("pk_v")
    a["consts"], a["buckets"], a["future"] = constants()
    return {k: np.ascontiguousarray(v) for k, v in a.items()}


def results_of(r):
    y = r["o_y"]
    kp, vp = (r[n].reshape(1, DEPTH, SEQ, H, 2 * HD) for n in ("o_kp", "o_vp"))
    ks, vs = (r[n].reshape(DEPTH, NSEQ, NEW, H, 2 * HD).transpose(1, 0, 2, 3, 4) for n in ("o_ks", "o_vs"))
    sp = r["o_state_p"].reshape(DEPTH, 2, HD, 2, 2, HD)
    ap = sp[:, :, :, 0].transpose(0, 3, 1, 4, 2).reshape(DEPTH, 1, H, HD, HD)
    bp = sp[:, :, :, 1].transpose(0, 3, 1, 2, 4).reshape(DEPTH, 1, H, HD, HD)
    ss = r["o_state_s"].reshape(DEPTH, 2, HD, 2, 2, NSEQ, HD)
    as_ = ss[:, :, :, 0].transpose(0, 4, 3, 1, 5, 2).reshape(DEPTH, NSEQ, H, HD, HD)
    bs = ss[:, :, :, 1].transpose(0, 4, 3, 1, 2, 5).reshape(DEPTH, NSEQ, H, HD, HD)
    tl = r["o_tails"]
    shp = tl[:, :, 0:8].transpose(0, 2, 1).reshape(DEPTH, 1, A_COLS)
    shs = tl[:, :, 8:72].reshape(DEPTH, P, 8, NSEQ).transpose(0, 3, 2, 1).reshape(DEPTH, NSEQ, A_COLS)
    cvp = tl[:, :, 72:90].reshape(DEPTH, P, 6, 3).transpose(0, 3, 2, 1).reshape(DEPTH, 1, 3, 768)
    cvs = tl[:, :, 90:234].reshape(DEPTH, P, 6, NSEQ, 3).transpose(0, 3, 4, 2, 1).reshape(DEPTH, NSEQ, 3, 768)
    out = (y[:SEQ].reshape(1, SEQ, D), y[SEQ:TOK].reshape(NSEQ, NEW, D), kp, vp, ks, vs, ap, as_, shp, shs, bp, bs, cvp, cvs)
    return tuple(np.ascontiguousarray(o) for o in out)


def kernel(**inputs):
    import concourse.bacc as bacc
    from concourse.bass_utils import run_bass_kernel_spmd

    nc = bacc.Bacc("TRN2", target_bir_lowering=False, num_devices=1)
    arrays = lay_out(inputs)
    t = {n: nc.dram_tensor(n, a.shape, mybir.dt.from_np(a.dtype), kind="ExternalInput").ap() for n, a in arrays.items()}
    for n, shape in _OUTS:
        t[n] = nc.dram_tensor(n, shape, F32, kind="ExternalOutput").ap()
    for n, shape in _SCRATCH:
        t[n] = nc.dram_tensor(n, shape, F32, kind="Internal").ap()
    trunk(nc, t)
    r = run_bass_kernel_spmd(nc, [arrays], core_ids=[0])
    return results_of(r.results[0])
```

```python
import math
from contextlib import ExitStack, contextmanager

import numpy as np

import concourse.bass as bass
from concourse import mybir

F32 = mybir.dt.float32
F32R = mybir.dt.float32r
U32 = mybir.dt.uint32
ALU = mybir.AluOpType
ACT = mybir.ActivationFunctionType
AX = mybir.AxisListType

P = 128
D = 1024
KC = D // P
SEQ = 512
DEPTH = 2
NSEQ = 8
NEW = 8
SAMP = NSEQ * NEW
TOK = SEQ + SAMP
TILES = 5
TOKP = TILES * P
PAST = 256
PAGE = 128
PAGES = PAST // PAGE
H = 4
HD = 64
CH = 64
NCH = TOK // CH
A_COLS, B_COLS, C_W = 1024, 1032, 512
COL_B, COL_AB, COL_Z, COL_C = 1024, 1792, 1800, 2056
EPS = 1e-6
KAPPA = math.exp(-0.5)
NEG = -1e30
BUCKETS = 32
REL = 639
PK_HEADS, PK_KEYS, TOPK = 8, 128, 16
SLOT = 2 * TOK
XW = KC * TOK + CH
WCH = 2 * P
X_AT = 14 * SLOT + TILES * 3 * C_W
W_AT = X_AT + 2 * XW
ARENA = W_AT + 4 * KC * WCH

COLS = {}
for _name, _n in (("mix_g", 8), ("ffn_g", 8), ("mu", 8), ("w0", 2), ("a0", 2), ("kk", 2), ("ka", 2),
                  ("rk", 2), ("ln_g", 2), ("ln_b", 2), ("conv", 24), ("subln", 1), ("dn_g", 1),
                  ("a_log", 2), ("dt", 2), ("lam_init", 1), ("lam_rest", 1)):
    COLS[_name] = (sum(n for _, n in COLS.values()), _n)
NCOL = sum(n for _, n in COLS.values())

CONST = {}
for _name, _n in (("ident", 128), ("head_mean", 128), ("all_mean", 128), ("iota", 128), ("id64", 64),
                  ("U_p", 64), ("SU_p", 64), ("SUt_p", 64), ("U_s", 64), ("SU_s", 64), ("SUt_s", 64),
                  ("lev", 6 * 64), ("seq_of", 8), ("ones", 64), ("is_c0", 1), ("is_c1", 1), ("last", 8)):
    CONST[_name] = (sum(n for _, n in CONST.values()), _n)
NCONST = sum(n for _, n in CONST.values())


def constants():
    c = np.zeros((P, NCONST), np.float32)

    def put(name, a):
        o, n = CONST[name]
        c[:, o:o + n] = a
    i = np.arange(64)
    s, t = i[:, None], i[None, :]
    same = (s // NEW) == (t // NEW)
    dup = lambda m: np.concatenate([m, m], 0).astype(np.float32)
    put("ident", np.eye(P))
    put("head_mean", np.kron(np.eye(2), np.full((64, 64), 1 / 64)))
    put("all_mean", np.full((P, P), 1 / P))
    put("iota", np.tile(np.arange(P), (P, 1)))
    put("id64", dup(np.eye(64)))
    put("U_p", dup(s <= t)); put("SU_p", dup(s > t)); put("SUt_p", dup(s < t))
    put("U_s", dup((s <= t) & same)); put("SU_s", dup((s > t) & same)); put("SUt_s", dup((s < t) & same))
    lev = [((s // (2 * b)) == (t // (2 * b))) & (s % (2 * b) >= b) & (t % (2 * b) < b) for b in (1, 2, 4, 8, 16, 32)]
    put("lev", np.concatenate([dup(m) for m in lev], 1))
    put("seq_of", dup((i[:, None] // NEW) == np.arange(8)[None, :]))
    put("ones", 1.0)
    row = np.arange(P)
    put("is_c0", ((row // 8) % 2 == 0)[:, None]); put("is_c1", ((row // 8) % 2 == 1)[:, None])
    dist = 511 - np.arange(REL)
    n = np.maximum(dist, 0)
    nf = np.maximum(n, 1).astype(np.float32)
    big = 16 + (np.log(nf / np.float32(16)) / np.float32(math.log(8)) * np.float32(16)).astype(np.int32)
    bucket = np.where(n < 16, n, np.minimum(big, 31))
    buckets = ((np.arange(BUCKETS)[:, None] == bucket[None]) & (dist >= 0)[None]).astype(np.float32)
    future = np.where(dist < 0, NEG, 0.0).astype(np.float32)[None].repeat(P, 0)
    return c, buckets, future


@contextmanager
def stage(nc, *names):
    with ExitStack() as ctx:
        sems = [ctx.enter_context(nc.semaphore(n)) for n in names]
        with nc.Block() as block:
            yield (block, *sems)
        for s in sems:
            nc.gpsimd.sem_clear(s)
        nc.all_engine_barrier()


class Steps:

    def __init__(self, eng, sem):
        self.eng, self.sem, self.n = eng, sem, 0

    def did(self, ins):
        self.n += 1
        ins.then_inc(self.sem, 1)

    def settle(self):
        self.eng.wait_ge(self.sem, self.n)

    def link(self, ins):
        self.did(ins)
        self.settle()


def split_products(pe, out, terms):
    for n, ((lhi, llo), (rhi, rlo)) in enumerate(terms):
        pe.matmul(out, lhi, rhi, start=(n == 0), stop=False)
        pe.matmul(out, lhi, rlo, start=False, stop=False)
        last = pe.matmul(out, llo, rhi, start=False, stop=(n == len(terms) - 1))
    return last


def bc(ap, axis, n):
    shape = list(ap.shape)
    shape.insert(axis, n)
    return ap.unsqueeze(axis).broadcast_to(shape)


def trunk(nc, t):
    ctx = ExitStack()
    with ctx:
        def sb(name, shape, dt=F32):
            return ctx.enter_context(nc.sbuf_tensor(name, shape, dt))

        arena_at = nc.sbuf_base + (-nc.sbuf_base) % 32
        arena = sb("arena", [P, ARENA])
        x_sb = sb("x_sb", [P, TILES, D])
        cst = sb("cst", [P, NCONST])
        cols = sb("cols_sb", [P, NCOL])
        rows = sb("rows_sb", [P, 512])
        bias_p = sb("bias_p", [P, H, 512])
        bias_s = sb("bias_s", [64, PAST + NEW])
        bias_own = sb("bias_own", [64, NSEQ, SAMP])
        work_s = sb("work_s", [64, 2 * (PAST + SAMP)])
        S_sb = sb("S_sb", [P, 256])
        small = sb("small", [P, 736])

        def split_at(name, at, size):
            return nc.alloc_sbuf_tensor_at(name, [P, size], F32R, offset=arena_at + 4 * at)

        x_split = split_at("x_split", X_AT, 2 * XW)
        w_split = split_at("w_split", W_AT, 4 * KC * WCH)
        u_split = split_at("u_split", 4 * SLOT, 4 * D)
        c_split = split_at("c_split", 8 * SLOT, 4 * SLOT)
        ps = ctx.enter_context(nc.psum_tensor("ps", [P, 8, 512], F32))

        def C(name, i=None):
            o, n = CONST[name]
            return cst[:, o:o + n] if i is None else cst[:, o + i * 64:o + (i + 1) * 64]

        def col(name, i=0, p=slice(0, P)):
            o, _ = COLS[name]
            return cols[p, o + i:o + i + 1]

        def slot(i, n=1):
            return arena[:, i * SLOT:(i + n) * SLOT]

        def ch(i):
            return slot(i).rearrange("p (j t) -> p j t", j=2)

        def tm(i):
            return slot(i).rearrange("p (c j t) -> p c j t", c=NCH, j=2)

        small_at = [0]

        def sm(n):
            small_at[0] += n
            assert small_at[0] <= 736
            return small[:, small_at[0] - n:small_at[0]]

        cat = slot(0, 4).rearrange("p (c t) -> p c t", c=KC)
        z_ch = ch(4)
        hA = slot(5, 5)
        hAp = hA[:, 0:8 * 513].rearrange("p (c t) -> p c t", c=8)
        hAs = hA[:, 8 * 513:8 * 513 + 576].rearrange("p (c b t) -> p c b t", c=8, b=8)
        hB = slot(10, 4)
        hBp = hB[:, 0:6 * 515].rearrange("p (c t) -> p c t", c=6)
        hBs = hB[:, 6 * 515:6 * 515 + 528].rearrange("p (c b t) -> p c b t", c=6, b=8)
        hC = slot(14, 7)[:, 0:TILES * 1536].rearrange("p (i n) -> p i n", i=TILES)
        def x_part(h):
            return x_split[:, h * XW:h * XW + KC * TOK].rearrange("p (k t) -> p k t", k=KC)

        def x_tile(k, i):
            return tuple(x_split[:, h * XW + k * TOK + i * P:h * XW + k * TOK + (i + 1) * P] for h in range(2))

        def w_part(s, h):
            return w_split[:, (2 * s + h) * KC * WCH:(2 * s + h + 1) * KC * WCH].rearrange("p (k n) -> p k n", k=KC)

        def w_raw(i):
            return slot(i, 4)[:, 0:2 * KC * WCH].rearrange("p (s k n) -> p s k n", s=2, k=KC)

        beta_g = sm(36).rearrange("p (k c j) -> p k c j", k=2, c=NCH)
        lam = sm(8)
        stat = sm(64)
        GL = sm(36).rearrange("p (m c j) -> p m c j", m=2, c=NCH)
        GLs = sm(32).rearrange("p (m j b) -> p m j b", m=2, j=2)
        gcol = sm(108).rearrange("p (k c j) -> p k c j", k=6, c=NCH)
        tails_o = sm(234)
        tails_i = sm(208)

        RP = REL + 1
        relb = slot(0)[0:32, 0:4]
        relb_bc = slot(0)[0:32, 128:128 + H * P].rearrange("b (h p) -> b h p", h=H)
        onehot = slot(1)[0:32, 0:REL]
        fut = slot(2)[:, 0:REL]
        r4 = slot(3, 3)[:, 0:H * RP].rearrange("p (h n) -> p h n", h=H)
        with stage(nc, "consts_in", "x_in", "steps", "rel_copied", "rel_mm", "rel_row", "rel_out", "rel_in", "own_ready") as (
                block, consts_in, x_in, steps_, rel_copied, rel_mm, rel_row, rel_out, rel_in, own_ready):
            rd = t["rel_scratch"]

            @block.sync
            def _(sp):
                sp.dma_start(relb, t["rel_bias"]).then_inc(consts_in, 16)
                sp.dma_start(onehot, t["buckets"]).then_inc(consts_in, 16)
                sp.dma_start(fut, t["future"]).then_inc(consts_in, 16)
                sp.dma_start(cst[:, :], t["consts"]).then_inc(consts_in, 16)
                sp.dma_start(x_sb[:, 0:4, :], t["x_prompt"].rearrange("(i p) d -> p i d", p=P)).then_inc(x_in, 16)
                sp.dma_start(x_sb[0:64, 4, :], t["x_sample"]).then_inc(x_in, 16)
                sp.wait_ge(rel_row, 2 * H)
                sp.dma_start(rd, r4.rearrange("p h n -> p (h n)")).then_inc(rel_out, 16)
                sp.wait_ge(rel_out, 16)
                for h in range(H):
                    sp.dma_start(bias_p[:, h, :], bass.AP(rd.tensor, h * RP + 127, [[H * RP - 1, P], [1, 512]])).then_inc(rel_in, 16)
                    for c in range(2):
                        r = h * 16 + c * 8
                        sp.dma_start(bias_s[r:r + 8, :], bass.AP(rd.tensor, h * RP + 255, [[H * RP - 1, 8], [1, PAST + NEW]])).then_inc(rel_in, 16)
                sp.wait_ge(rel_in, 12 * 16)
                sp.wait_ge(x_in, 32)

            @block.vector
            def _(dve):
                st = Steps(dve, steps_)
                st.did(dve.memset(x_sb[64:P, 4, :], 0.0))
                st.did(dve.memset(r4[:, :, REL:RP], 0.0))
                st.did(dve.memset(bias_own[:, :, :], NEG))
                st.settle()
                dve.wait_ge(consts_in, 64)
                dve.tensor_copy(relb_bc, bc(relb, 2, P)).then_inc(rel_copied, 1)
                for h in range(H):
                    dve.wait_ge(rel_mm, h + 1)
                    dve.tensor_tensor(r4[:, h, 0:512], ps[:, 2 * h, :], fut[:, 0:512], ALU.add).then_inc(rel_row, 1)
                    dve.tensor_tensor(r4[:, h, 512:REL], ps[:, 2 * h + 1, 0:REL - 512], fut[:, 512:REL], ALU.add).then_inc(rel_row, 1)
                dve.wait_ge(rel_in, 12 * 16)
                for b in range(NSEQ):
                    last = dve.tensor_copy(bias_own[:, b, b * NEW:(b + 1) * NEW], bias_s[:, PAST:PAST + NEW])
                last.then_inc(own_ready, 1)

            @block.tensor
            def _(pe):
                pe.wait_ge(consts_in, 64)
                pe.wait_ge(rel_copied, 1)
                for h in range(H):
                    pe.matmul(ps[:, 2 * h, :], relb_bc[:, h], onehot[:, 0:512], start=True, stop=True)
                    pe.matmul(ps[:, 2 * h + 1, 0:REL - 512], relb_bc[:, h], onehot[:, 512:REL], start=True, stop=True).then_inc(rel_mm, 1)

        with nc.Fori(0, DEPTH) as layer:
            L = bass.ds(layer, 1)

            def at(name):
                a = t[name][L]
                n = len(a.shape)
                names = " ".join("abcdefg"[:n - 1])
                return a.rearrange(f"o {names} -> (o a) {names[2:]}" if n > 2 else f"o {names} -> o {names}")

            def norm_transposed(gain):
                junk = slot(5)[:, 0:D]
                xn = slot(0, 5).rearrange("p (i n) -> p i n", n=SLOT)[:, :, 0:D]
                xg = slot(6, 5)[:, 0:10 * 512].rearrange("p (u k t) -> p u k t", u=10, k=4)
                with stage(nc, "par_in", "ssq_ready", "root_ready", "inv_steps", "xn_ready", "tr_done", "xg_ready", "hi_ready", "lo_ready") as (
                        block, par_in, ssq_ready, root_ready, inv_steps, xn_ready, tr_done, xg_ready, hi_ready, lo_ready):
                    def part(h, u):
                        i, hf = u // 2, u % 2
                        return x_part(h)[:, 4 * hf:4 * hf + 4, i * P:min(TOK, (i + 1) * P)]

                    def gained(u):
                        return xg[:, u, :, 0:min(P, TOK - (u // 2) * P)]

                    @block.sync
                    def _(sp):
                        sp.dma_start(cols[:, :], at("cols")).then_inc(par_in, 16)
                        sp.dma_start(rows[:, :], t["rows"][L].broadcast_to([P, 512])).then_inc(par_in, 16)

                    @block.scalar
                    def _(act):
                        sq = Steps(act, ssq_ready)
                        for i in range(TILES):
                            sq.link(act.activation(junk, x_sb[:, i, :], ACT.Square, accum_out=stat[:, i:i + 1]))
                        act.wait_ge(inv_steps, 1)
                        act.activation(stat[:, 16:21], stat[:, 8:13], ACT.Sqrt).then_inc(root_ready, 1)
                        for u in range(TILES * 2):
                            act.wait_ge(xg_ready, u + 1)
                            act.copy(part(0, u), gained(u)).then_inc(hi_ready, 1)

                    @block.gpsimd
                    def _(pool):
                        for h in range(2):
                            pool.tensor_copy(x_split[:, h * XW + KC * TOK:(h + 1) * XW], C("ones")).then_inc(lo_ready, 1)
                        for u in range(TILES * 2):
                            pool.wait_ge(hi_ready, u + 1)
                            pool.tensor_tensor(part(1, u), gained(u), part(0, u).bitcast(F32), ALU.subtract).then_inc(lo_ready, 1)

                    @block.vector
                    def _(dve):
                        st = Steps(dve, inv_steps)
                        dve.wait_ge(ssq_ready, TILES)
                        st.link(dve.tensor_scalar(stat[:, 8:13], stat[:, 0:5], 1.0 / D, EPS, ALU.mult, ALU.add))
                        dve.wait_ge(root_ready, 1)
                        st.link(dve.reciprocal(stat[:, 24:29], stat[:, 16:21]))
                        for i in range(TILES):
                            dve.tensor_scalar(xn[:, i, :], x_sb[:, i, :], stat[:, 24 + i:25 + i], None, ALU.mult).then_inc(xn_ready, 1)
                        dve.wait_ge(par_in, 32)
                        o, _ = COLS[gain]
                        for u in range(TILES * 2):
                            w, hf = min(P, TOK - (u // 2) * P), u % 2
                            dve.wait_ge(tr_done, u + 1)
                            dve.tensor_tensor(gained(u), ps[:, u % 8, :].rearrange("p (k t) -> p k t", k=4)[:, :, 0:w],
                                              bc(cols[:, o + 4 * hf:o + 4 * hf + 4], 2, w), ALU.mult).then_inc(xg_ready, 1)

                    @block.tensor
                    def _(pe):
                        for u in range(TILES * 2):
                            i, hf = u // 2, u % 2
                            pe.wait_ge(xn_ready, i + 1)
                            if u >= 8:
                                pe.wait_ge(xg_ready, u - 7)
                            for k in range(4):
                                kc = hf * 4 + k
                                last = pe.transpose(ps[:, u % 8, k * P:(k + 1) * P], xn[:, i, kc * P:(kc + 1) * P], C("ident"))
                            last.then_inc(tr_done, 1)

            def hi_of(act, g, raw, w_in, hi_ready, width=WCH):
                s = g % 2
                act.wait_ge(w_in[s], 16 * (g // 2 + 1))
                act.copy(w_part(s, 0)[:, :, 0:width], raw[:, s, :, 0:width]).then_inc(hi_ready, 1)

            def lo_of(pool, g, raw, hi_ready, lo_ready, width=WCH):
                s = g % 2
                pool.wait_ge(hi_ready, g + 1)
                pool.tensor_tensor(w_part(s, 1)[:, :, 0:width], raw[:, s, :, 0:width], w_part(s, 0)[:, :, 0:width].bitcast(F32),
                                   ALU.subtract).then_inc(lo_ready, 1)

            norm_transposed("mix_g")

            groups = ([("A", c, WCH) for c in range(0, A_COLS, WCH)] + [("ab", COL_AB, P)]
                      + [("B", c, WCH) for c in range(COL_B, COL_AB, WCH)] + [("z", COL_Z, WCH)]
                      + [("C", c, WCH) for c in range(COL_C, COL_C + 3 * C_W, WCH)])
            units = []
            for g, (kind, c0, w) in enumerate(groups):
                if kind == "C":
                    units += [(g, kind, c0, i) for i in range(TILES)]
                else:
                    units += [(g, kind, c0 + m * P, part) for m in range(w // P) for part in (0, 1)]
            rows_u = len(units)
            units += [(len(groups) - 1, "ab_rows", COL_AB, 0)]
            abT = work_s[0:8, 0:TOK]
            raw = w_raw(0)
            group_last = [max(u for u, un in enumerate(units) if un[0] == g) for g in range(len(groups))]
            with stage(nc, "w_in0", "w_in1", "hi_ready", "lo_ready", "tails_in", "proj_done", "out_act", "out_dve", "tails_steps",
                       "tail_ready", "tail_out") as (block, w_s0, w_s1, hi_ready, lo_ready, tails_in, proj_done, out_act, out_dve,
                                                     tails_steps, tail_ready, tail_out):
                w_sem = [w_s0, w_s1]
                wv = at("w_in").rearrange("(k p) n -> p k n", p=P)

                @block.sync
                def _(sp):
                    sp.dma_start(tails_i, at("tails")).then_inc(tails_in, 16)
                    for g, (kind, c0, w) in enumerate(groups):
                        if g >= 2:
                            sp.wait_ge(lo_ready, g - 1)
                        sp.dma_start(raw[:, g % 2, :, 0:w], wv[:, :, c0:c0 + w]).then_inc(w_sem[g % 2], 16)
                    sp.wait_ge(tail_ready, 1)
                    sp.dma_start(at("o_tails"), tails_o).then_inc(tail_out, 16)
                    sp.wait_ge(tail_out, 16)

                def copies(u):
                    g, kind, c0, part = units[u]
                    b = ps[:, u % 8, :]
                    if kind == "C":
                        return [(hC[:, part, c0 - COL_C:c0 - COL_C + WCH], b[:, 0:WCH])]
                    if kind == "ab":
                        return [(abT[:, 0:SEQ], b[0:8])] if part == 0 else [(abT[:, SEQ:TOK], b[0:8, 0:SAMP])]
                    if kind == "ab_rows":
                        v = b[:, 0:NCH * 8].rearrange("p (c k j h) -> p h k c j", c=NCH, k=2, j=2)
                        return [(beta_g[64 * hf:64 * hf + 64, k], v[64 * hf:64 * hf + 64, hf, k]) for hf in range(2) for k in range(2)]
                    if kind == "z":
                        j = (c0 - COL_Z) // P
                        return [(z_ch[:, j, 0:SEQ], b)] if part == 0 else [(z_ch[:, j, SEQ:TOK], b[:, 0:SAMP])]
                    base, dp, ds_, lead = (0, hAp, hAs, 1) if kind == "A" else (COL_B, hBp, hBs, 3)
                    c = (c0 - base) // P
                    if part == 0:
                        return [(dp[:, c, lead:lead + SEQ], b)]
                    return [(ds_[:, c, :, lead:lead + NEW], b[:, 0:SAMP].rearrange("p (b t) -> p b t", b=NSEQ))]

                @block.scalar
                def _(act):
                    for g in range(2):
                        hi_of(act, g, raw, w_sem, hi_ready, groups[g][2])
                    for u in range(len(units)):
                        g = units[u][0]
                        if u and units[u - 1][0] < g < len(groups) - 1:
                            act.wait_ge(proj_done, group_last[g - 1] + 1)
                            hi_of(act, g + 1, raw, w_sem, hi_ready, groups[g + 1][2])
                        if u % 2 == 0:
                            act.wait_ge(proj_done, u + 1)
                            for d, s in copies(u):
                                last = act.copy(d, s)
                            last.then_inc(out_act, 1)

                @block.gpsimd
                def _(pool):
                    for g in range(len(groups)):
                        lo_of(pool, g, raw, hi_ready, lo_ready, groups[g][2])

                @block.vector
                def _(dve):
                    st = Steps(dve, tails_steps)
                    st.did(dve.memset(hAp[:, :, 0:1], 0.0))
                    st.did(dve.memset(hBp[:, :, 0:3], 0.0))
                    dve.wait_ge(tails_in, 16)
                    st.did(dve.tensor_copy(hAs[:, :, :, 0:1], tails_i[:, 0:64].rearrange("p (c b o) -> p c b o", c=8, b=8)))
                    st.did(dve.tensor_copy(hBs[:, :, :, 0:3], tails_i[:, 64:208].rearrange("p (c b k) -> p c b k", c=6, b=8)))
                    for u in range(1, len(units), 2):
                        dve.wait_ge(proj_done, u + 1)
                        for d, s in copies(u):
                            last = dve.tensor_copy(d, s)
                        last.then_inc(out_dve, 1)
                    dve.wait_ge(out_act, (len(units) + 1) // 2)
                    dve.wait_ge(out_dve, len(units) // 2)
                    st.did(dve.tensor_copy(tails_o[:, 0:8].unsqueeze(2), hAp[:, :, SEQ:SEQ + 1]))
                    st.did(dve.tensor_copy(tails_o[:, 8:72].rearrange("p (c b o) -> p c b o", c=8, b=8), hAs[:, :, :, NEW:NEW + 1]))
                    st.did(dve.tensor_copy(tails_o[:, 72:90].rearrange("p (c k) -> p c k", c=6), hBp[:, :, SEQ:SEQ + 3]))
                    st.link(dve.tensor_copy(tails_o[:, 90:234].rearrange("p (c b k) -> p c b k", c=6, b=8), hBs[:, :, :, NEW:NEW + 3]))
                    dve.sem_inc(tail_ready, 1)

                @block.tensor
                def _(pe):
                    for u, (g, kind, c0, part) in enumerate(units):
                        wh, wl = w_part(g % 2, 0), w_part(g % 2, 1)
                        if u == 0 or units[u - 1][0] != g:
                            pe.wait_ge(lo_ready, g + 1)
                        if u >= 8:
                            pe.wait_ge(out_dve if u % 2 else out_act, (u - 8) // 2 + 1)
                        m = c0 - groups[g][1]
                        if kind == "ab_rows":
                            for c in range(NCH):
                                for hf in range(2):
                                    last = pe.matmul(ps[64 * hf:64 * hf + 64, u % 8, c * 8:c * 8 + 8], abT[:, c * CH:(c + 1) * CH],
                                                     C("ident")[0:8, 0:8], start=True, stop=True)
                        elif kind == "C":
                            last = split_products(pe, ps[:, u % 8, 0:WCH], [(x_tile(k, part), (wh[:, k, :], wl[:, k, :])) for k in range(KC)])
                        else:
                            t0, n = (0, SEQ) if part == 0 else (SEQ, SAMP)
                            last = split_products(pe, ps[:, u % 8, 0:n], [((wh[:, k, m:m + P], wl[:, k, m:m + P]),
                                                                          (x_part(0)[:, k, t0:t0 + n], x_part(1)[:, k, t0:t0 + n]))
                                                                         for k in range(KC)])
                        last.then_inc(proj_done, 1)

            QT = slot(21, 5)[:, 0:2560].rearrange("p (h t) -> p h t", h=H)
            KT = slot(21, 5)[:, 2560:5120].rearrange("p (h t) -> p h t", h=H)
            room = slot(26, 8)
            sq2 = room[:, 0:2048].rearrange("p (s n) -> p s n", s=2)
            ssq = room[:, 2048:2128].rearrange("p (i n) -> p i n", i=TILES)
            root = room[:, 2128:2208]
            rinv = room[:, 2208:2288].rearrange("p (i n) -> p i n", i=TILES)
            lprod = room[:, 2304:2432].rearrange("p (a n) -> p a n", a=2)
            coef = lam[0:64, 4:5]
            with stage(nc, "sq_ready", "ssq_steps", "mean_ready", "root_ready", "lam_sum", "lam_exp", "qk_ready", "t_done", "q_out",
                       "k_out", "rows_out") as (block, sq_ready, ssq_steps, mean_ready, root_ready, lam_sum, lam_exp, qk_ready,
                                                t_done, q_out, k_out, rows_out):
                @block.scalar
                def _(act):
                    for i in range(TILES):
                        if i >= 2:
                            act.wait_ge(ssq_steps, i - 1)
                        act.activation(sq2[:, i % 2, :], hC[:, i, 0:1024], ACT.Square).then_inc(sq_ready, 1)
                    act.wait_ge(mean_ready, 1)
                    act.activation(root, root, ACT.Sqrt).then_inc(root_ready, 1)
                    act.wait_ge(lam_sum, 1)
                    act.activation(lam[:, 0:2], lam[:, 0:2], ACT.Exp).then_inc(lam_exp, 1)
                    for i in range(TILES):
                        act.wait_ge(t_done, 2 * i + 1)
                        act.copy(QT[:, :, i * P:(i + 1) * P], ps[:, (2 * i) % 8, :].rearrange("p (h t) -> p h t", h=H)).then_inc(q_out, 1)

                @block.vector
                def _(dve):
                    st = Steps(dve, ssq_steps)
                    for i in range(TILES):
                        dve.wait_ge(sq_ready, i + 1)
                        st.did(dve.tensor_reduce(ssq[:, i, :], sq2[:, i % 2, :].rearrange("p (g n) -> p g n", n=HD), AX.X, ALU.add))
                    st.settle()
                    st.did(dve.tensor_tensor(lprod, rows[:, 256:512].rearrange("p (a b n) -> p b a n", a=2, b=2)[:, 0],
                                             rows[:, 256:512].rearrange("p (a b n) -> p b a n", a=2, b=2)[:, 1], ALU.mult))
                    dve.tensor_scalar(root.rearrange("p (i n) -> p i n", i=TILES), ssq, 1.0 / HD, EPS, ALU.mult, ALU.add).then_inc(mean_ready, 1)
                    st.settle()
                    dve.tensor_reduce(lam[:, 0:2], lprod, AX.X, ALU.add).then_inc(lam_sum, 1)
                    dve.wait_ge(root_ready, 1)
                    st.link(dve.reciprocal(rinv.rearrange("p i n -> p (i n)"), root))
                    for i in range(TILES):
                        v = hC[:, i, 0:1024].rearrange("p (g n) -> p g n", n=HD)
                        st.link(dve.tensor_tensor(v, v, bc(rinv[:, i, :], 2, HD), ALU.mult))
                        v = hC[:, i, 0:1024].rearrange("p (a h n) -> p a h n", a=2, h=H)
                        g = bc(rows[:, 0:256].rearrange("p (a n) -> p a n", a=2), 2, H)
                        dve.tensor_tensor(v, v, g, ALU.mult).then_inc(qk_ready, 1)
                    dve.wait_ge(lam_exp, 1)
                    st.link(dve.tensor_tensor(lam[:, 2:3], lam[:, 0:1], lam[:, 1:2], ALU.subtract))
                    st.link(dve.tensor_tensor(lam[:, 2:3], lam[:, 2:3], col("lam_init"), ALU.add))
                    st.link(dve.tensor_scalar(lam[:, 3:4], lam[:, 2:3], -1.0, None, ALU.mult))
                    st.link(dve.scalar_tensor_tensor(coef, C("is_c1")[0:64], lam[0:64, 3:4], C("is_c0")[0:64], ALU.mult, ALU.add))
                    for i in range(TILES):
                        dve.wait_ge(t_done, 2 * i + 2)
                        dve.tensor_copy(KT[:, :, i * P:(i + 1) * P], ps[:, (2 * i + 1) % 8, :].rearrange("p (h t) -> p h t", h=H)).then_inc(k_out, 1)

                @block.tensor
                def _(pe):
                    for i in range(TILES):
                        pe.wait_ge(qk_ready, i + 1)
                        if i == 4:
                            pe.wait_ge(q_out, 1)
                            pe.wait_ge(k_out, 1)
                        for a in range(2):
                            for h in range(H):
                                last = pe.transpose(ps[:, (2 * i + a) % 8, h * P:(h + 1) * P], hC[:, i, a * C_W + h * P:a * C_W + (h + 1) * P], C("ident"))
                            last.then_inc(t_done, 1)

                @block.sync
                def _(sp):
                    sp.dma_start(at("o_vp").rearrange("(i p) n -> p i n", p=P), hC[:, 0:4, 1024:1536]).then_inc(rows_out, 16)
                    sp.dma_start(at("o_vs"), hC[0:SAMP, 4, 1024:1536]).then_inc(rows_out, 16)
                    sp.wait_ge(qk_ready, TILES)
                    sp.dma_start(at("o_kp").rearrange("(i p) n -> p i n", p=P), hC[:, 0:4, 512:1024]).then_inc(rows_out, 16)
                    sp.dma_start(at("o_ks"), hC[0:SAMP, 4, 512:1024]).then_inc(rows_out, 16)
                    sp.wait_ge(rows_out, 64)

            Sb = room[:, 0:2048].rearrange("p (s c k) -> p s c k", s=2, c=2)
            pd = room[:, 2048:3072].rearrange("p (s k) -> p s k", s=2)
            PT = room[:, 3072:4096].rearrange("p (s k) -> p s k", s=2)
            st4 = room[:, 4096:4096 + 16].rearrange("p (s n) -> p s n", s=2)
            au = [(i, h) for i in range(4) for h in range(H)]
            OC = cat[:, 4:8, :]
            with stage(nc, "s_done", "biased", "max_ready", "exp_done", "fin_steps", "pd_ready", "pt_done", "pt_ready", "pv_done", "oc_ready") as (
                    block, s_done, biased, max_ready, exp_done, fin_steps, pd_ready, pt_done, pt_ready, pv_done, oc_ready):
                @block.tensor
                def _(pe):
                    def scores(u):
                        i, h = au[u]
                        if u >= 2:
                            pe.wait_ge(biased, u - 1)
                        for c in range(2):
                            last = pe.matmul(ps[:, 2 * (u % 2) + c, 0:(i + 1) * P], QT[64 * c:64 * c + 64, h, i * P:(i + 1) * P],
                                             KT[64 * c:64 * c + 64, h, 0:(i + 1) * P], start=True, stop=True)
                        last.then_inc(s_done, 1)

                    def turn(u):
                        i, h = au[u]
                        pe.wait_ge(pd_ready, u + 1)
                        if u >= 2:
                            pe.wait_ge(pt_ready, u - 1)
                        for j in range(i + 1):
                            last = pe.transpose(ps[:, 4 + u % 2, j * P:(j + 1) * P], pd[:, u % 2, j * P:(j + 1) * P], C("ident"))
                        last.then_inc(pt_done, 1)

                    def values(u):
                        i, h = au[u]
                        pe.wait_ge(pt_ready, u + 1)
                        if u >= 2:
                            pe.wait_ge(oc_ready, u - 1)
                        for j in range(i + 1):
                            last = pe.matmul(ps[:, 6 + u % 2, 0:P], hC[:, j, 1024 + h * P:1024 + (h + 1) * P], PT[:, u % 2, j * P:(j + 1) * P],
                                             start=(j == 0), stop=(j == i))
                        last.then_inc(pv_done, 1)
                    n = len(au)
                    for u in range(n + 2):
                        if u < n:
                            scores(u)
                        if 1 <= u <= n:
                            turn(u - 1)
                        if u >= 2:
                            values(u - 2)

                def copy_out(act, u):
                    i, h = au[u]
                    act.wait_ge(pt_done, u + 1)
                    if u >= 2:
                        act.wait_ge(pv_done, u - 1)
                    act.copy(PT[:, u % 2, 0:(i + 1) * P], ps[:, 4 + u % 2, 0:(i + 1) * P]).then_inc(pt_ready, 1)
                    act.wait_ge(pv_done, u + 1)
                    act.copy(OC[:, h, i * P:(i + 1) * P], ps[:, 6 + u % 2, 0:P]).then_inc(oc_ready, 1)

                @block.scalar
                def _(act):
                    for u, (i, h) in enumerate(au):
                        k, s, m = (i + 1) * P, Sb[:, u % 2], st4[:, u % 2]
                        act.wait_ge(max_ready, u + 1)
                        for c in range(2):
                            last = act.activation(s[:, c, 0:k], s[:, c, 0:k], ACT.Exp, bias=m[:, c:c + 1], accum_out=m[:, 2 + c:3 + c])
                        last.then_inc(exp_done, 1)
                        if u >= 1:
                            copy_out(act, u - 1)
                    copy_out(act, len(au) - 1)

                @block.vector
                def _(dve):
                    st = Steps(dve, fin_steps)

                    def finish(u):
                        i, h = au[u]
                        k, s, m = (i + 1) * P, Sb[:, u % 2], st4[:, u % 2]
                        dve.wait_ge(exp_done, u + 1)
                        st.link(dve.reciprocal(m[:, 4:6], m[:, 2:4]))
                        st.link(dve.tensor_tensor(m[:, 5:6], m[:, 5:6], lam[:, 3:4], ALU.mult))
                        if u >= 2:
                            dve.wait_ge(pt_done, u - 1)
                        st.link(dve.tensor_scalar(pd[:, u % 2, 0:k], s[:, 0, 0:k], m[:, 4:5], None, ALU.mult))
                        dve.scalar_tensor_tensor(pd[:, u % 2, 0:k], s[:, 1, 0:k], m[:, 5:6], pd[:, u % 2, 0:k],
                                                 ALU.mult, ALU.add).then_inc(pd_ready, 1)

                    for u, (i, h) in enumerate(au):
                        k, s, m = (i + 1) * P, Sb[:, u % 2], st4[:, u % 2]
                        dve.wait_ge(s_done, u + 1)
                        if u >= 2:
                            dve.wait_ge(pd_ready, u - 1)
                        dve.scalar_tensor_tensor(s[:, :, 0:k], ps[:, 2 * (u % 2):2 * (u % 2) + 2, 0:k], HD ** -0.5,
                                                 bc(bias_p[:, h, 512 - k:512], 1, 2), ALU.mult, ALU.add).then_inc(biased, 1)
                        dve.wait_ge(biased, u + 1)
                        dve.tensor_reduce(m[:, 0:2], s[:, :, 0:k], AX.X, ALU.max, negate=True).then_inc(max_ready, 1)
                        if u >= 1:
                            finish(u - 1)
                    finish(len(au) - 1)

            QX = room[:, 0:2048].rearrange("p (b h r) -> p b h r", b=NSEQ, h=H)
            NPG = 4
            pages = [a[:, 0:2048].rearrange("p (m j n) -> p m j n", m=2, j=PAGES)
                     for a in (room[:, 2048:4096], room[:, 4096:6144], slot(0, 2), arena[:, 34 * SLOT:ARENA])]
            KTb = room[:, 6144:8192].rearrange("p (s h t) -> p s h t", s=2, h=H)
            W_ = PAST + SAMP
            Ss = work_s[:, 0:2 * W_].rearrange("p (s k) -> p s k", s=2)
            PTa = room[:, 8192:8384].rearrange("p (j r) -> p j r", j=3)
            PTs = room[:, 8384:8384 + 192].rearrange("p (s j h q) -> p s j h q", s=2, j=3, h=H)
            ms = stat[0:64, 32:48].rearrange("p (s n) -> p s n", s=2)
            with stage(nc, "pages_in0", "pages_in1", "pages_in2", "pages_in3", "qx_steps", "kt_done", "kt_a", "kt_v", "s_done", "biased", "max_ready", "exp_done",
                       "p_steps", "p_ready", "pt_done", "pta_steps", "pt_ready", "pv_done", "oc_ready", "pid_in") as (
                    block, pages_in0, pages_in1, pages_in2, pages_in3, qx_steps, kt_done, kt_a, kt_v, s_done, biased, max_ready, exp_done,
                    p_steps, p_ready, pt_done, pta_steps, pt_ready, pv_done, oc_ready, pid_in):
                pages_in = [pages_in0, pages_in1, pages_in2, pages_in3]

                @block.sync
                def _(sp):
                    for b in range(NSEQ):
                        if b >= NPG:
                            sp.wait_ge(kt_done, 2 * (b - NPG + 1))
                            sp.wait_ge(pv_done, b - NPG + 1)
                        for j in range(PAGES):
                            pid = sp.value_load(t["page_table"][b:b + 1, j:j + 1], min_val=0, max_val=t["cache_k"].shape[0] - 1)
                            for m, name in enumerate(("cache_k", "cache_v")):
                                src = t[name][bass.ds(pid, 1), L].rearrange("o a t h n -> (o a t) (h n)")
                                sp.dma_start(pages[b % NPG][:, m, j, :], src).then_inc(pages_in[b % NPG], 16)

                @block.tensor
                def _(pe):
                    def keys(b):
                        pe.wait_ge(pages_in[b % NPG], 64 * (b // NPG + 1))
                        for j in range(PAGES):
                            if b >= 1:
                                pe.wait_ge(kt_v if j else kt_a, b)
                            for h in range(H):
                                last = pe.transpose(ps[:, j, h * P:(h + 1) * P], pages[b % NPG][:, 0, j, h * P:(h + 1) * P], C("ident"))
                            last.then_inc(kt_done, 1)

                    def scores(b):
                        pe.wait_ge(kt_a, b + 1)
                        pe.wait_ge(kt_v, b + 1)
                        if b == 0:
                            pe.wait_ge(qx_steps, 9)
                        if b >= 2:
                            pe.wait_ge(biased, 2 * (b - 1))
                        for h in range(H):
                            pe.matmul(ps[0:64, 2 + b % 2, 0:PAST], QX[:, b, h, :], KTb[:, b % 2, h, :], start=(h == 0), stop=(h == 3))
                        for h in range(H):
                            last = pe.matmul(ps[0:64, 2 + b % 2, PAST:W_], QX[:, b, h, :], KT[:, h, SEQ:TOK], start=(h == 0), stop=(h == 3))
                        last.then_inc(s_done, 1)

                    def turn(b):
                        pe.wait_ge(p_ready, b + 1)
                        if b >= 2:
                            pe.wait_ge(pt_ready, b - 1)
                        for j in range(3):
                            k = min(P, W_ - j * P)
                            last = pe.transpose(ps[0:k, 4 + b % 2, j * 64:j * 64 + 64], Ss[:, b % 2, j * P:j * P + k], C("ident")[0:64, 0:64])
                        last.then_inc(pt_done, 1)

                    def values(b):
                        pe.wait_ge(pt_ready, b + 1)
                        for h in range(H):
                            o = ps[:, 6, h * 64 + b * NEW:h * 64 + (b + 1) * NEW]
                            for j in range(PAGES):
                                pe.matmul(o, pages[b % NPG][:, 1, j, h * P:(h + 1) * P], PTs[:, b % 2, j, h, :], start=(j == 0), stop=False)
                            last = pe.matmul(o, hC[0:64, 4, 1024 + h * P:1024 + (h + 1) * P], PTs[0:64, b % 2, 2, h, :], start=False, stop=True)
                        last.then_inc(pv_done, 1)
                    for b in range(NSEQ + 3):
                        if b < NSEQ:
                            keys(b)
                        if 1 <= b <= NSEQ:
                            scores(b - 1)
                        if 2 <= b <= NSEQ + 1:
                            turn(b - 2)
                        if b >= 3:
                            values(b - 3)

                @block.scalar
                def _(act):
                    for b in range(NSEQ + 1):
                        if b < NSEQ:
                            act.wait_ge(kt_done, 2 * b + 1)
                            if b >= 2:
                                act.wait_ge(s_done, b - 1)
                            act.copy(KTb[:, b % 2, :, 0:P], ps[:, 0, :].rearrange("p (h t) -> p h t", h=H)).then_inc(kt_a, 1)
                        if b >= 1:
                            u = b - 1
                            act.wait_ge(max_ready, u + 1)
                            act.activation(Ss[:, u % 2, :], Ss[:, u % 2, :], ACT.Exp, bias=ms[:, u % 2, 0:1], accum_out=ms[:, u % 2, 1:2]).then_inc(exp_done, 1)
                    act.wait_ge(pv_done, NSEQ)
                    act.copy(OC[:, :, SEQ:TOK], ps[:, 6, 0:256].rearrange("p (h t) -> p h t", h=H)).then_inc(oc_ready, 1)

                @block.vector
                def _(dve):
                    q = Steps(dve, qx_steps)
                    q.link(dve.memset(QX, 0.0))
                    for h in range(H):
                        for c in range(2):
                            p = slice(64 * c, 64 * c + 64)
                            q.did(dve.tensor_copy(QX[p, :, h, h * 16 + c * 8:h * 16 + c * 8 + 8],
                                                  QT[p, h, SEQ:TOK].rearrange("p (b t) -> p b t", b=NSEQ)))
                    st = Steps(dve, p_steps)
                    pt = Steps(dve, pta_steps)

                    def scaled(b):
                        s, m = Ss[:, b % 2], ms[:, b % 2]
                        dve.wait_ge(s_done, b + 1)
                        if b >= 2:
                            dve.wait_ge(pt_done, b - 1)
                        dve.scalar_tensor_tensor(s[:, 0:PAST], ps[0:64, 2 + b % 2, 0:PAST], HD ** -0.5, bias_s[:, 0:PAST],
                                                 ALU.mult, ALU.add).then_inc(biased, 1)
                        dve.scalar_tensor_tensor(s[:, PAST:W_], ps[0:64, 2 + b % 2, PAST:W_], HD ** -0.5, bias_own[:, b, :],
                                                 ALU.mult, ALU.add).then_inc(biased, 1)
                        dve.wait_ge(biased, 2 * b + 2)
                        dve.tensor_reduce(m[:, 0:1], s, AX.X, ALU.max, negate=True).then_inc(max_ready, 1)

                    def weights(b):
                        s, m = Ss[:, b % 2], ms[:, b % 2]
                        dve.wait_ge(exp_done, b + 1)
                        st.link(dve.reciprocal(m[:, 2:3], m[:, 1:2]))
                        st.link(dve.tensor_tensor(m[:, 2:3], m[:, 2:3], coef, ALU.mult))
                        dve.tensor_scalar(s, s, m[:, 2:3], None, ALU.mult).then_inc(p_ready, 1)

                    def differences(b):
                        dve.wait_ge(pt_done, b + 1)
                        if b >= 2:
                            dve.wait_ge(pv_done, b - 1)
                        for p, js in ((slice(0, P), slice(0, 2)), (slice(0, 64), slice(2, 3))):
                            n = js.stop - js.start
                            raw = ps[p, 4 + b % 2, js.start * 64:js.stop * 64]
                            pt.link(dve.tensor_copy(PTa[p, js, :], raw.rearrange("p (j r) -> p j r", j=n)))
                            v = PTa[p, js, :].rearrange("p j (h c q) -> p c j h q", h=H, c=2)
                            for j in range(n):
                                last = dve.tensor_tensor(PTs[p, b % 2, js.start + j], v[:, 0, j], v[:, 1, j], ALU.add)
                                pt.did(last)
                        pt.settle()
                        dve.sem_inc(pt_ready, 1)
                    for b in range(NSEQ + 2):
                        if b < NSEQ:
                            dve.wait_ge(kt_done, 2 * b + 2)
                            if b >= 2:
                                dve.wait_ge(s_done, b - 1)
                            dve.tensor_copy(KTb[:, b % 2, :, P:PAST], ps[:, 1, :].rearrange("p (h t) -> p h t", h=H)).then_inc(kt_v, 1)
                        if b >= 2:
                            weights(b - 2)
                        if 1 <= b <= NSEQ:
                            scaled(b - 1)
                        if b >= 2:
                            differences(b - 2)

            hs = slot(14, 4).rearrange("p (c t) -> p c t", c=8)
            r_, k_, v_, lora = ch(14), ch(15), ch(16), ch(17)
            sig, a_, gate, kkn = ch(18), ch(19), ch(20), ch(21)
            t1, t2, cumA, cumB = ch(22), ch(23), ch(24), ch(25)
            Gd, Gi = ch(26), ch(27)
            Qr, Ar, Kr, Br, yadd = ch(28), ch(29), ch(30), ch(31), ch(32)
            lw = slot(33)[:, 0:512]
            halves = [(j, q) for j in range(2) for q in range(2)]
            HN = TOK // 2

            def chunked(a):
                return (a[:, :, 0:SEQ].rearrange("p j (c t) -> p j c t", t=CH), a[:, :, SEQ:TOK].rearrange("p j (b t) -> p j b t", t=NEW))

            def flat(a):
                return a.rearrange("p j t -> p (j t)")

            with stage(nc, "lora_in", "v_steps", "lora_ready", "lora_act", "mm_done", "act_out", "sq_ready", "kk_mm", "root_ready",
                       "rk_ready", "rk_mm", "rk_out", "cum_ready", "exp_ready") as (
                    block, lora_in, v_steps, lora_ready, lora_act, mm_done, act_out, sq_ready, kk_mm, root_ready,
                    rk_ready, rk_mm, rk_out, cum_ready, exp_ready):
                @block.sync
                def _(sp):
                    sp.dma_start(lw, at("lora")).then_inc(lora_in, 16)

                @block.tensor
                def _(pe):
                    pe.wait_ge(lora_in, 16)
                    pe.wait_ge(lora_act, 2)
                    for u in range(12):
                        kind, (j, q) = u // 4, halves[u % 4]
                        if u >= 8:
                            pe.wait_ge(act_out, u - 7)
                        w, x = [(lw[0:64, j * P:(j + 1) * P], lora[0:64, 0]), (lw[64:P, j * P:(j + 1) * P], lora[64:P, 0]),
                                (lw[:, 256 + j * P:256 + (j + 1) * P], lora[:, 1])][kind]
                        pe.matmul(ps[:, u % 8, 0:HN], w, x[:, q * HN:(q + 1) * HN], start=True, stop=True).then_inc(mm_done, 1)
                    pe.wait_ge(sq_ready, 1)
                    pe.wait_ge(act_out, 12)
                    for u, (j, q) in enumerate(halves):
                        pe.matmul(ps[:, u, 0:HN], C("head_mean"), t1[:, j, q * HN:(q + 1) * HN], start=True, stop=True).then_inc(kk_mm, 1)
                    pe.wait_ge(rk_ready, 2)
                    for u, (j, q) in enumerate(halves):
                        pe.matmul(ps[:, 4 + u, 0:HN], C("head_mean"), t1[:, j, q * HN:(q + 1) * HN], start=True, stop=True).then_inc(rk_mm, 1)

                @block.scalar
                def _(act):
                    act.wait_ge(lora_ready, 4)
                    act.activation(lora[0:64, 0], lora[0:64, 0], ACT.Tanh).then_inc(lora_act, 1)
                    act.activation(lora[:, 1], lora[:, 1], ACT.Sigmoid).then_inc(lora_act, 1)
                    for u in range(12):
                        kind, (j, q) = u // 4, halves[u % 4]
                        act.wait_ge(mm_done, u + 1)
                        src = ps[:, u % 8, 0:HN]
                        d = (sig, a_, gate)[kind][:, j, q * HN:(q + 1) * HN]
                        if kind == 2:
                            act.copy(d, src).then_inc(act_out, 1)
                        else:
                            act.activation(d, src, ACT.Sigmoid, bias=col("w0" if kind == 0 else "a0", j)).then_inc(act_out, 1)
                    for u, (j, q) in enumerate(halves):
                        act.wait_ge(kk_mm, u + 1)
                        act.activation(t2[:, j, q * HN:(q + 1) * HN], ps[:, u, 0:HN], ACT.Copy, scale=float(HD), bias=EPS).then_inc(root_ready, 1)
                    act.wait_ge(root_ready, 4)
                    act.activation(flat(t2), flat(t2), ACT.Sqrt).then_inc(root_ready, 1)
                    act.wait_ge(cum_ready, 1)
                    act.activation(flat(Gd), flat(cumB), ACT.Exp, scale=-KAPPA).then_inc(exp_ready, 1)
                    act.activation(flat(Gi), flat(cumB), ACT.Exp, scale=KAPPA).then_inc(exp_ready, 1)
                    act.wait_ge(cum_ready, 2)
                    act.activation(flat(cumA), flat(sig), ACT.Exp, scale=-KAPPA).then_inc(exp_ready, 1)

                @block.vector
                def _(dve):
                    st = Steps(dve, v_steps)
                    hsp, hss = hs[:, :, 0:SEQ], hs[:, :, SEQ:TOK].rearrange("p c (b t) -> p c b t", b=NSEQ)
                    for c in range(8):
                        st.did(dve.tensor_tensor(hsp[:, c], hAp[:, c, 0:SEQ], hAp[:, c, 1:SEQ + 1], ALU.subtract))
                    st.did(dve.tensor_tensor(hss, hAs[:, :, :, 0:NEW], hAs[:, :, :, 1:NEW + 1], ALU.subtract))
                    st.settle()
                    for n, c in enumerate((6, 7, 2, 3, 0, 1, 4, 5)):
                        sem = lora_ready if n < 2 else v_steps
                        dve.scalar_tensor_tensor(hsp[:, c], hsp[:, c], col("mu", c), hAp[:, c, 1:SEQ + 1], ALU.mult, ALU.add).then_inc(sem, 1)
                        dve.scalar_tensor_tensor(hss[:, c], hss[:, c], col("mu", c), hAs[:, c, :, 1:NEW + 1], ALU.mult, ALU.add).then_inc(sem, 1)
                    st.n += 12
                    st.settle()
                    for j in range(2):
                        st.did(dve.tensor_scalar(kkn[:, j], k_[:, j], col("kk", j), None, ALU.mult))
                    st.settle()
                    dve.tensor_tensor(flat(t1), flat(kkn), flat(kkn), ALU.mult).then_inc(sq_ready, 1)
                    dve.wait_ge(root_ready, 5)
                    st.link(dve.reciprocal(flat(t2), flat(t2)))
                    st.did(dve.tensor_tensor(flat(kkn), flat(kkn), flat(t2), ALU.mult))
                    for j in range(2):
                        st.did(dve.tensor_scalar(t1[:, j], a_[:, j], -1.0, col("ka", j), ALU.add, ALU.mult))
                    st.settle()
                    st.link(dve.scalar_tensor_tensor(flat(k_), flat(t1), 1.0, flat(k_), ALU.add, ALU.mult))
                    st.link(dve.tensor_tensor(flat(t1), flat(r_), flat(k_), ALU.mult))
                    for j in range(2):
                        dve.tensor_scalar(t1[:, j], t1[:, j], col("rk", j), None, ALU.mult).then_inc(rk_ready, 1)
                    for u, (j, q) in enumerate(halves):
                        dve.wait_ge(rk_mm, u + 1)
                        dve.scalar_tensor_tensor(yadd[:, j, q * HN:(q + 1) * HN], ps[:, 4 + u, 0:HN], float(HD), v_[:, j, q * HN:(q + 1) * HN],
                                                 ALU.mult, ALU.mult).then_inc(rk_out, 1)
                    src, dst = sig, cumA
                    for n in range(6):
                        w = 1 << n
                        (sp_, ss_), (dp_, ds_) = chunked(src), chunked(dst)
                        st.did(dve.tensor_tensor(dp_[:, :, :, w:], sp_[:, :, :, w:], sp_[:, :, :, :-w], ALU.add))
                        st.did(dve.tensor_copy(dp_[:, :, :, 0:w], sp_[:, :, :, 0:w]))
                        if n < 3:
                            st.did(dve.tensor_tensor(ds_[:, :, :, w:], ss_[:, :, :, w:], ss_[:, :, :, :-w], ALU.add))
                            st.did(dve.tensor_copy(ds_[:, :, :, 0:w], ss_[:, :, :, 0:w]))
                        elif n == 3:
                            st.did(dve.tensor_copy(ds_, ss_))
                        st.settle()
                        src, dst = dst, (cumB if dst is cumA else cumA)
                    assert src is cumB
                    dve.sem_inc(cum_ready, 1)
                    dve.tensor_tensor(flat(sig), flat(cumB), flat(sig), ALU.subtract).then_inc(cum_ready, 1)
                    dve.wait_ge(exp_ready, 2)
                    st.did(dve.tensor_tensor(flat(Qr), flat(r_), flat(Gd), ALU.mult))
                    st.did(dve.tensor_tensor(flat(Kr), flat(k_), flat(Gi), ALU.mult))
                    dve.wait_ge(rk_out, 4)
                    st.link(dve.tensor_tensor(flat(t1), flat(kkn), flat(a_), ALU.mult))
                    st.did(dve.tensor_tensor(flat(Br), flat(t1), flat(Gi), ALU.mult))
                    dve.wait_ge(exp_ready, 3)
                    st.did(dve.scalar_tensor_tensor(flat(Ar), flat(kkn), -1.0, flat(cumA), ALU.mult, ALU.mult))
                    (gp, gs) = chunked(Gd)
                    st.did(dve.tensor_copy(GL[:, 0, 0:8, :].rearrange("p c j -> p j c").unsqueeze(3), gp[:, :, :, CH - 1:CH]))
                    st.did(dve.tensor_copy(GLs[:, 0].unsqueeze(3), gs[:, :, :, NEW - 1:NEW]))
                    st.settle()
                    for d, s in ((t1, Kr), (t2, Br)):
                        (dp_, ds_), (sp_, ss_) = chunked(d), chunked(s)
                        for j in range(2):
                            st.did(dve.tensor_tensor(dp_[:, j], sp_[:, j], gp[:, j, :, CH - 1:CH].broadcast_to([P, 8, CH]), ALU.mult))
                            st.did(dve.tensor_tensor(ds_[:, j], ss_[:, j], gs[:, j, :, NEW - 1:NEW].broadcast_to([P, NSEQ, NEW]), ALU.mult))
                    st.settle()

            cg = [range(0, 4), range(4, 8), range(8, 9)]
            heads4 = [(j, hf, slice(64 * hf, 64 * hf + 64)) for j in range(2) for hf in range(2)]

            def per_head(g):
                return [((n * 2 + j) * CH, c, j, p) for n, c in enumerate(cg[g]) for j, hf, p in heads4]

            def bank3(b, g, n=CH):
                w = len(cg[g]) * 2
                return ps[:, b, 0:w * n].rearrange("p (x t) -> p x t", t=n)

            def part3(i, g):
                return tm(i)[:, cg[g].start:cg[g].stop].rearrange("p c j t -> p (c j) t")

            def mask3(m, g):
                return bc(C(m + ("_s" if g == 2 else "_p")), 1, len(cg[g]) * 2)

            En_r, MT, PB, PK, V_t, A_t, K_t, B_t, MV = 5, 6, 7, 8, 9, 14, 15, 17, 18
            rkinds = [("turn", v_, V_t), ("turn", Ar, A_t), ("turn", t1, K_t), ("turn", t2, B_t),
                      ("En", Ar, Br, En_r), ("MT", Kr, Ar, MT), ("PB", Br, Qr, PB), ("PK", Kr, Qr, PK), ("MV", MT, V_t, MV)]
            runits = [(k, g) for k in rkinds for g in range(3)]
            on_act = lambda kind: kind in ("turn", "En", "MV", "KK")
            with stage(nc, "mm_done", "act_out", "dve_out") as (block, mm_done, act_out, dve_out):
                def counts(units):
                    n, out = {True: 0, False: 0}, []
                    for k, g in units:
                        n[on_act(k[0])] += 1
                        out.append((on_act(k[0]), n[on_act(k[0])]))
                    return out
                cnt = counts(runits)

                @block.tensor
                def _(pe):
                    for u, (k, g) in enumerate(runits):
                        if u >= 8:
                            a, n = cnt[u - 8]
                            pe.wait_ge(act_out if a else dve_out, n)
                        if k[0] == "MV" and g == 0:
                            pe.wait_ge(dve_out, cnt[u - 1][1])
                            pe.wait_ge(act_out, 3)
                        for x, c, j, p in per_head(g):
                            tk = slice(c * CH, (c + 1) * CH)
                            if k[0] == "turn":
                                lhsT, rhs = k[1][p, j, tk], C("id64")[p]
                            elif k[0] == "MV":
                                lhsT, rhs = tm(MT)[p, c, j], tm(V_t)[p, c, j]
                            else:
                                lhsT, rhs = k[1][p, j, tk], k[2][p, j, tk]
                            last = pe.matmul(ps[p, u % 8, x:x + CH], lhsT, rhs, start=True, stop=True)
                        last.then_inc(mm_done, 1)

                @block.scalar
                def _(act):
                    for u, (k, g) in enumerate(runits):
                        if on_act(k[0]):
                            act.wait_ge(mm_done, u + 1)
                            act.activation(part3(k[-1], g), bank3(u % 8, g), ACT.Copy, scale=-1.0 if k[0] == "En" else 1.0).then_inc(act_out, 1)

                @block.vector
                def _(dve):
                    for u, (k, g) in enumerate(runits):
                        if not on_act(k[0]):
                            dve.wait_ge(mm_done, u + 1)
                            dve.tensor_tensor(part3(k[-1], g), bank3(u % 8, g), mask3("SUt" if k[0] == "MT" else "U", g), ALU.mult).then_inc(dve_out, 1)

            cv = slot(21, 3).rearrange("p (c t) -> p c t", c=6)
            sg3 = slot(24, 3).rearrange("p (c t) -> p c t", c=6)
            qd_, kd_, vd_ = ch(21), ch(22), ch(23)
            nq, nk = ch(24), ch(25)
            nrm2 = slot(24, 2)
            rt2 = slot(29, 2)
            g_, beta = beta_g[:, 0], beta_g[:, 1]
            sp_m, sp_a, sp_e = gcol[:, 3], gcol[:, 4], gcol[:, 5]
            eg, et, beg = gcol[:, 0], gcol[:, 1], gcol[:, 2]
            alog = stat[:, 48:50]
            g8 = stat[:, 0:16].rearrange("p (j b) -> p j b", j=2)
            with stage(nc, "v_steps", "conv_ready", "sig_ready", "sqn_ready", "mm_done", "root_ready", "ab_ready", "sp_exp", "g_ready",
                       "gsum_done", "gexp_ready") as (block, v_steps, conv_ready, sig_ready, sqn_ready, mm_done, root_ready, ab_ready,
                                                      sp_exp, g_ready, gsum_done, gexp_ready):
                @block.vector
                def _(dve):
                    st = Steps(dve, v_steps)
                    st.link(dve.tensor_tensor(g_, g_, bc(cols[:, COLS["dt"][0]:COLS["dt"][0] + 2], 1, NCH), ALU.add))
                    st.link(dve.tensor_scalar(sp_m, g_, 0.0, None, ALU.max))
                    dve.scalar_tensor_tensor(sp_a, sp_m, 2.0, g_, ALU.mult, ALU.subtract).then_inc(ab_ready, 1)
                    for n in range(4):
                        for c in range(6):
                            xp, xs = hBp[:, c, n:n + SEQ], hBs[:, c, :, n:n + NEW]
                            dp_, ds_ = cv[:, c, 0:SEQ], cv[:, c, SEQ:TOK].rearrange("p (b t) -> p b t", b=NSEQ)
                            w = col("conv", n * 6 + c)
                            for d, x in ((dp_, xp), (ds_, xs)):
                                if n == 0:
                                    i = dve.tensor_scalar(d, x, w, None, ALU.mult)
                                else:
                                    i = dve.scalar_tensor_tensor(d, x, w, d, ALU.mult, ALU.add)
                                if n == 3:
                                    i.then_inc(conv_ready, 1)
                                else:
                                    st.did(i)
                        if n < 3:
                            st.settle()
                    dve.wait_ge(conv_ready, 12)
                    dve.wait_ge(sig_ready, 3)
                    st.link(dve.tensor_tensor(slot(21, 3), slot(21, 3), slot(24, 3), ALU.mult))
                    dve.tensor_tensor(nrm2, slot(21, 2), slot(21, 2), ALU.mult).then_inc(sqn_ready, 1)
                    dve.wait_ge(sig_ready, 4)
                    st.did(dve.tensor_tensor(flat(z_ch), flat(z_ch), slot(27), ALU.mult))
                    dve.wait_ge(sp_exp, 3)
                    st.link(dve.tensor_tensor(sp_m, sp_m, sp_e, ALU.add))
                    st.link(dve.scalar_tensor_tensor(g_, sp_m, -1.0, bc(alog, 1, NCH), ALU.mult, ALU.mult))
                    st.did(dve.tensor_tensor(g8, bc(g_[:, 8], 2, NSEQ), bc(C("seq_of"), 1, 2), ALU.mult))
                    su, gb = tm(26), tm(31)
                    for m, a, b in (("_p", 0, 8), ("_s", 8, 9)):
                        for j in range(2):
                            st.did(dve.tensor_tensor(su[:, a:b, j], bc(C("SU" + m), 1, b - a), bc(g_[:, a:b, j], 2, CH), ALU.mult))
                    st.did(dve.tensor_copy(gb.rearrange("p c j t -> p (c j) t"), bc(g_.rearrange("p c j -> p (c j)"), 2, CH)))
                    st.settle()
                    dve.sem_inc(g_ready, 1)
                    dve.wait_ge(root_ready, 10)
                    st.link(dve.reciprocal(rt2, rt2))
                    st.did(dve.scalar_tensor_tensor(flat(qd_), flat(qd_), HD ** -0.5, slot(29), ALU.mult, ALU.mult))
                    st.did(dve.tensor_tensor(flat(kd_), flat(kd_), slot(30), ALU.mult))
                    dve.wait_ge(gexp_ready, 4)
                    st.did(dve.scalar_tensor_tensor(beg, eg, -1.0, beta, ALU.mult, ALU.mult))
                    st.settle()

                @block.scalar
                def _(act):
                    act.wait_ge(conv_ready, 12)
                    for n in range(3):
                        act.activation(slot(24 + n), slot(21 + n), ACT.Sigmoid).then_inc(sig_ready, 1)
                    act.activation(slot(27), flat(z_ch), ACT.Sigmoid).then_inc(sig_ready, 1)
                    act.activation(beta, beta, ACT.Sigmoid).then_inc(sp_exp, 1)
                    act.wait_ge(ab_ready, 1)
                    act.activation(sp_e, sp_a, ACT.Exp, scale=-1.0).then_inc(root_ready, 1)
                    act.activation(alog, cols[:, COLS["a_log"][0]:COLS["a_log"][0] + 2], ACT.Exp).then_inc(sp_exp, 1)
                    act.wait_ge(root_ready, 1)
                    act.activation(sp_e, sp_e, ACT.Ln, bias=1.0).then_inc(sp_exp, 1)
                    for u in range(8):
                        act.wait_ge(mm_done, u + 1)
                        i, (j, q) = u // 4, halves[u % 4]
                        act.activation(ch(29 + i)[:, j, q * HN:(q + 1) * HN], ps[:, u, 0:HN], ACT.Copy, scale=float(HD), bias=EPS).then_inc(root_ready, 1)
                    act.wait_ge(root_ready, 9)
                    act.activation(rt2, rt2, ACT.Sqrt).then_inc(root_ready, 1)
                    act.wait_ge(gsum_done, 1)
                    act.activation(eg.rearrange("p c j -> p (c j)"), ps[:, 0, 0:18], ACT.Exp).then_inc(gexp_ready, 1)
                    act.activation(et.rearrange("p c j -> p (c j)"), ps[:, 0, 18:36], ACT.Exp).then_inc(gexp_ready, 1)
                    act.activation(GL[:, 1, 0:8, :].rearrange("p c j -> p (c j)"), ps[:, 0, 36:52], ACT.Exp).then_inc(gexp_ready, 1)
                    act.activation(GLs[:, 1].rearrange("p j b -> p (j b)"), ps[:, 0, 54:70], ACT.Exp).then_inc(gexp_ready, 1)

                @block.tensor
                def _(pe):
                    pe.wait_ge(sqn_ready, 1)
                    for u in range(8):
                        i, (j, q) = u // 4, halves[u % 4]
                        pe.matmul(ps[:, u, 0:HN], C("head_mean"), ch(24 + i)[:, j, q * HN:(q + 1) * HN], start=True, stop=True).then_inc(mm_done, 1)
                    pe.wait_ge(g_ready, 1)
                    pe.wait_ge(root_ready, 9)
                    for hf in range(2):
                        p = slice(64 * hf, 64 * hf + 64)
                        gp, gs = g_[p, 0:8].rearrange("p c j -> p (c j)"), g_[p, 8]
                        for at_, mat, rhs in ((0, "U_p", gp), (16, "U_s", gs), (18, "SU_p", gp), (34, "SU_s", gs),
                                              (36, "ones", gp), (54, "ones", g8[p].rearrange("p j b -> p (j b)"))):
                            n = rhs.shape[1]
                            last = pe.matmul(ps[p, 0, at_:at_ + n], C(mat)[p], rhs, start=True, stop=True)
                    last.then_inc(gsum_done, 1)

            En_g, ATT, Kd_t, Vd_t, KB_t, Qg = 6, 16, 25, 24, 27, 19
            dkinds = [("turn", kd_, Kd_t), ("turn", vd_, Vd_t), ("Dts", None, 29), ("Dst", None, 30), ("row", None, 33),
                      ("KKn", kd_, kd_, En_g), ("KQ", kd_, qd_, ATT)]
            dunits = [(k, g) for k in dkinds for g in range(3)]
            on_act2 = lambda kind: kind in ("turn", "Dts", "Dst", "row")
            with stage(nc, "mm_done", "act_out", "dve_out", "v_steps") as (block, mm_done, act_out, dve_out, v_steps):
                su, gb = tm(26), tm(31)
                na = sum(on_act2(k[0]) for k, g in dunits)

                @block.tensor
                def _(pe):
                    for u, (k, g) in enumerate(dunits):
                        if u >= 8:
                            v = u - 8
                            if v < na:
                                pe.wait_ge(act_out, v + 1)
                            else:
                                pe.wait_ge(dve_out, v - na + 1)
                        Um = C("U_s" if g == 2 else "U_p")
                        for x, c, j, p in per_head(g):
                            tk = slice(c * CH, (c + 1) * CH)
                            lhsT, rhs = {"turn": lambda: (k[1][p, j, tk], C("id64")[p]), "Dts": lambda: (Um[p], su[p, c, j]),
                                         "Dst": lambda: (su[p, c, j], Um[p]), "row": lambda: (gb[p, c, j], Um[p]),
                                         "KKn": lambda: (k[1][p, j, tk], k[2][p, j, tk]), "KQ": lambda: (k[1][p, j, tk], k[2][p, j, tk])}[k[0]]()
                            last = pe.matmul(ps[p, u % 8, x:x + CH], lhsT, rhs, start=True, stop=True)
                        last.then_inc(mm_done, 1)

                @block.scalar
                def _(act):
                    for u, (k, g) in enumerate(dunits[:na]):
                        act.wait_ge(mm_done, u + 1)
                        act.activation(part3(k[-1], g), bank3(u % 8, g), ACT.Copy if k[0] == "turn" else ACT.Exp).then_inc(act_out, 1)

                @block.vector
                def _(dve):
                    st = Steps(dve, v_steps)
                    dve.wait_ge(act_out, 6)
                    whole = lambda i: tm(i).rearrange("p c j t -> p (c j) t")
                    per_row = lambda a: bc(a.rearrange("p c j -> p (c j)"), 2, CH)
                    st.did(dve.tensor_tensor(whole(KB_t), whole(Kd_t), per_row(beg), ALU.mult))
                    st.did(dve.tensor_tensor(whole(Vd_t), whole(Vd_t), per_row(beta), ALU.mult))
                    st.settle()
                    st.did(dve.tensor_tensor(whole(Kd_t), whole(Kd_t), per_row(et), ALU.mult))
                    dve.wait_ge(act_out, na)
                    for u, (k, g) in enumerate(dunits[na:]):
                        dve.wait_ge(mm_done, na + u + 1)
                        dve.tensor_tensor(part3(k[-1], g), bank3((na + u) % 8, g), part3(29 if k[0] == "KKn" else 30, g), ALU.mult).then_inc(dve_out, 1)
                    for j in range(2):
                        st.did(dve.tensor_tensor(ch(Qg)[:, j].rearrange("p (c t) -> p c t", t=CH), qd_[:, j].rearrange("p (c t) -> p c t", t=CH),
                                                 tm(33)[:, :, j], ALU.mult))
                    dve.wait_ge(dve_out, 6)
                    st.did(dve.tensor_tensor(whole(En_g), whole(En_g), per_row(beta), ALU.mult))
                    for g in range(3):
                        st.did(dve.tensor_tensor(part3(ATT, g), part3(ATT, g), mask3("U", g), ALU.mult))
                    st.settle()

            TM, TTm, P1, Em = (10, 11), (12, 13), (21, 22), (23, 26)
            En = (En_r, En_g)
            steps = [(lv, m, g) for lv in range(6) for m in range(2) for g in range(3 if lv < 3 else 2)]
            with stage(nc, "em_ready", "eye_ready", "p1_done", "p1_out", "tt_done", "t_ready") as (
                    block, em_ready, eye_ready, p1_done, p1_out, tt_done, t_ready):
                place = {s: n for n, s in enumerate(steps)}

                @block.gpsimd
                def _(pool):
                    for lv in range(6):
                        for m in range(2):
                            if lv:
                                pool.wait_ge(p1_done, place[(lv - 1, m, 1 if lv > 3 else 2)] + 1)
                            pool.tensor_tensor(tm(Em[m]).rearrange("p c j t -> p (c j) t"), tm(En[m]).rearrange("p c j t -> p (c j) t"),
                                               bc(C("lev", lv), 1, 2 * NCH), ALU.mult).then_inc(em_ready, 1)

                @block.tensor
                def _(pe):
                    pe.wait_ge(eye_ready, 4)
                    for lv in range(6):
                        ns = [n for n, s in enumerate(steps) if s[0] == lv]
                        for n in ns:
                            _, m, g = steps[n]
                            pe.wait_ge(em_ready, 2 * lv + m + 1)
                            if lv:
                                pe.wait_ge(t_ready, 2 * place[(lv - 1, m, g)] + 2)
                            if n >= 2:
                                pe.wait_ge(p1_out, n - 1)
                            for x, c, j, p in per_head(g):
                                last = pe.matmul(ps[p, n % 2, x:x + CH], tm(Em[m])[p, c, j], tm(TTm[m])[p, c, j], start=True, stop=True)
                            last.then_inc(p1_done, 1)
                        for n in ns:
                            _, m, g = steps[n]
                            pe.wait_ge(p1_out, n + 1)
                            if n >= 3:
                                pe.wait_ge(t_ready, 2 * (n - 2))
                            b = 2 + 2 * (n % 3)
                            for x, c, j, p in per_head(g):
                                pe.matmul(ps[p, b, x:x + CH], tm(P1[m])[p, c, j], tm(TM[m])[p, c, j], start=True, stop=True)
                            for x, c, j, p in per_head(g):
                                last = pe.matmul(ps[p, b + 1, x:x + CH], tm(TM[m])[p, c, j], tm(P1[m])[p, c, j], start=True, stop=True)
                            last.then_inc(tt_done, 1)

                @block.scalar
                def _(act):
                    for n, (lv, m, g) in enumerate(steps):
                        act.wait_ge(p1_done, n + 1)
                        if lv:
                            act.wait_ge(tt_done, place[(lv - 1, m, g)] + 1)
                        act.copy(part3(P1[m], g), bank3(n % 2, g)).then_inc(p1_out, 1)

                @block.vector
                def _(dve):
                    for i in TM + TTm:
                        dve.tensor_copy(tm(i).rearrange("p c j t -> p (c j) t"), bc(C("id64"), 1, 2 * NCH)).then_inc(eye_ready, 1)
                    dve.wait_ge(eye_ready, 4)
                    for n, (lv, m, g) in enumerate(steps):
                        dve.wait_ge(tt_done, n + 1)
                        b = 2 + 2 * (n % 3)
                        if lv:
                            dve.wait_ge(t_ready, 2 * place[(lv - 1, m, g)] + 2)
                        dve.tensor_tensor(part3(TM[m], g), part3(TM[m], g), bank3(b, g), ALU.subtract).then_inc(t_ready, 1)
                        dve.tensor_tensor(part3(TTm[m], g), part3(TTm[m], g), bank3(b + 1, g), ALU.subtract).then_inc(t_ready, 1)

            WT, UU = (29, 30), (31, 33)
            wu = [(k, m, g) for m in range(2) for k in range(2) for g in range(3)]
            with stage(nc, "mm_done", "act_out", "dve_out") as (block, mm_done, act_out, dve_out):
                @block.tensor
                def _(pe):
                    for u, (k, m, g) in enumerate(wu):
                        if u >= 8:
                            pe.wait_ge(dve_out if u % 2 else act_out, (u - 8) // 2 + 1)
                        for x, c, j, p in per_head(g):
                            tt = tm(TTm[m])[p, c, j]
                            lhsT, rhs = (tm((A_t, KB_t)[m])[p, c, j], tt) if k == 0 else (tt, tm((MV, Vd_t)[m])[p, c, j])
                            last = pe.matmul(ps[p, u % 8, x:x + CH], lhsT, rhs, start=True, stop=True)
                        last.then_inc(mm_done, 1)

                def target(u):
                    k, m, g = wu[u]
                    return part3((WT, UU)[k][m], g), bank3(u % 8, g)

                @block.scalar
                def _(act):
                    for u in range(0, len(wu), 2):
                        act.wait_ge(mm_done, u + 1)
                        act.copy(*target(u)).then_inc(act_out, 1)

                @block.vector
                def _(dve):
                    for u in range(1, len(wu), 2):
                        dve.wait_ge(mm_done, u + 1)
                        dve.tensor_copy(*target(u)).then_inc(dve_out, 1)

            S = S_sb[:, :].rearrange("p (m j n) -> p m j n", m=2, j=2)
            SA = slot(21)[:, 0:512].rearrange("p (s m j n) -> p s m j n", s=2, m=2, j=2)
            Y = (14, 27)
            Qx = (Qr, ch(Qg))
            Px = (PB, ATT)
            Kx = (B_t, Kd_t)
            mh = [(m, j, p) for m in range(2) for j, hf, p in heads4]
            S0 = slot(10, 2)[:, 0:2048].rearrange("p (m j b n) -> p m j b n", m=2, j=2, b=NSEQ)
            with stage(nc, "s_ready", "ws_done", "sa_ready", "out_done", "ds_done", "y_out", "scaled", "state_out", "s0_in") as (
                    block, s_ready, ws_done, sa_ready, out_done, ds_done, y_out, scaled, state_out, s0_in):
                @block.tensor
                def _(pe):
                    for c in range(8):
                        tk = slice(c * CH, (c + 1) * CH)
                        bw, bo, bd = c % 2, 2 + c % 2, 4 + c % 2
                        at_ = lambda m, j: slice((m * 2 + j) * CH, (m * 2 + j + 1) * CH)
                        pe.wait_ge(s_ready, c + 1)
                        if c >= 2:
                            pe.wait_ge(sa_ready, 2 * (c - 1))
                            pe.wait_ge(y_out, 2 * (c - 1))
                        for m, j, p in mh:
                            last = pe.matmul(ps[p, bw, at_(m, j)], tm(WT[m])[p, c, j], S[p, m, j], start=True, stop=True)
                        last.then_inc(ws_done, 1)
                        pe.wait_ge(sa_ready, 2 * (c + 1))
                        for m, j, p in mh:
                            pe.matmul(ps[p, bd, at_(m, j)], tm(Kx[m])[p, c, j], SA[p, c % 2, m, j], start=True, stop=(m == 1))
                            if m == 0:
                                pe.matmul(ps[p, bd, at_(m, j)], tm(K_t)[p, c, j], tm(V_t)[p, c, j], start=False, stop=True)
                        for m, j, p in mh:
                            o = ps[p, bo, at_(m, j)]
                            pe.matmul(o, S[p, m, j], Qx[m][p, j, tk], start=True, stop=False)
                            last = pe.matmul(o, SA[p, c % 2, m, j], tm(Px[m])[p, c, j], start=False, stop=(m == 1))
                            if m == 0:
                                last = pe.matmul(o, tm(V_t)[p, c, j], tm(PK)[p, c, j], start=False, stop=True)
                        last.then_inc(out_done, 1)

                @block.vector
                def _(dve):
                    dve.memset(S, 0.0).then_inc(s_ready, 1)
                    dve.wait_ge(s_ready, 1)
                    for c in range(8):
                        dve.wait_ge(ws_done, c + 1)
                        for m in range(2):
                            dve.tensor_tensor(SA[:, c % 2, m], tm(UU[m])[:, c], ps[:, c % 2, m * 128:(m + 1) * 128].rearrange("p (j n) -> p j n", j=2),
                                              ALU.add).then_inc(sa_ready, 1)
                        dve.wait_ge(out_done, c + 1)
                        dve.tensor_tensor(S, S, bc(GL[:, :, c], 3, HD), ALU.mult).then_inc(scaled, 1)
                        dve.wait_ge(scaled, c + 1)
                        dve.tensor_tensor(S, S, ps[:, 4 + c % 2, 0:256].rearrange("p (m j n) -> p m j n", m=2, j=2), ALU.add).then_inc(s_ready, 1)
                        dve.wait_ge(s_ready, c + 2)

                @block.scalar
                def _(act):
                    for c in range(8):
                        act.wait_ge(out_done, c + 1)
                        for m in range(2):
                            act.copy(ch(Y[m])[:, :, c * CH:(c + 1) * CH],
                                     ps[:, 2 + c % 2, m * 128:(m + 1) * 128].rearrange("p (j t) -> p j t", j=2)).then_inc(y_out, 1)

                @block.sync
                def _(sp):
                    sp.dma_start(slot(10, 2)[:, 0:2048], at("states")).then_inc(s0_in, 16)
                    sp.wait_ge(s_ready, 9)
                    sp.dma_start(at("o_state_p"), S_sb[:, :]).then_inc(state_out, 16)
                    sp.wait_ge(state_out, 16)
                    sp.wait_ge(s0_in, 16)

            SAT = slot(21)[:, 512:768].rearrange("p (x t) -> p x t", x=4)
            SA1 = slot(21)[:, 0:256].rearrange("p (m j n) -> p m j n", m=2, j=2)
            SAx = slot(12, 2)[:, 0:2048].rearrange("p (x b n) -> p x b n", x=4, b=NSEQ)
            Vx = slot(22)[:, 0:1024].rearrange("p (j b n) -> p j b n", j=2, b=NSEQ)
            with stage(nc, "sat_done", "sat_out", "sa_done", "sa_ready", "x_ready", "y_done", "y_out", "ds_done", "s_ready", "state_out") as (
                    block, sat_done, sat_out, sa_done, sa_ready, x_ready, y_done, y_out, ds_done, s_ready, state_out):
                tk = lambda b: slice(SEQ + b * NEW, SEQ + (b + 1) * NEW)

                @block.tensor
                def _(pe):
                    for m, j, p in mh:
                        for b in range(NSEQ):
                            last = pe.matmul(ps[p, 0, (m * 2 + j) * CH + b * NEW:(m * 2 + j) * CH + (b + 1) * NEW], S0[p, m, j, b],
                                             tm(WT[m])[p, 8, j, b * NEW:(b + 1) * NEW], start=True, stop=True)
                    last.then_inc(sat_done, 1)
                    pe.wait_ge(sat_out, 1)
                    for m, j, p in mh:
                        x = m * 2 + j
                        last = pe.matmul(ps[p, 1, x * CH:(x + 1) * CH], SAT[p, x], C("id64")[p], start=True, stop=True)
                    last.then_inc(sa_done, 1)
                    pe.wait_ge(sa_ready, 2)
                    for m, j, p in mh:
                        x = m * 2 + j
                        pe.matmul(ps[p, 2, x * CH:(x + 1) * CH], SA1[p, m, j], tm(Px[m])[p, 8, j], start=True, stop=False)
                        if m == 0:
                            pe.matmul(ps[p, 2, x * CH:(x + 1) * CH], tm(V_t)[p, 8, j], tm(PK)[p, 8, j], start=False, stop=False)
                        for b in range(NSEQ):
                            last = pe.matmul(ps[p, 2, x * CH + b * NEW:x * CH + (b + 1) * NEW], S0[p, m, j, b], Qx[m][p, j, tk(b)],
                                             start=False, stop=(b == NSEQ - 1))
                    last.then_inc(y_done, 1)
                    pe.wait_ge(x_ready, 6)
                    for m, j, p in mh:
                        x = m * 2 + j
                        last = pe.matmul(ps[p, 4 + x, :], tm(Kx[m])[p, 8, j], SAx[p, x].rearrange("p b n -> p (b n)"), start=True, stop=(m == 1))
                        if m == 0:
                            last = pe.matmul(ps[p, 4 + x, :], tm(K_t)[p, 8, j], Vx[p, j].rearrange("p b n -> p (b n)"), start=False, stop=True)
                    last.then_inc(ds_done, 1)

                @block.scalar
                def _(act):
                    act.wait_ge(sat_done, 1)
                    act.copy(SAT.rearrange("p x t -> p (x t)"), ps[:, 0, 0:256]).then_inc(sat_out, 1)
                    act.wait_ge(y_done, 1)
                    for m in range(2):
                        act.copy(ch(Y[m])[:, :, SEQ:TOK], ps[:, 2, m * 128:(m + 1) * 128].rearrange("p (j t) -> p j t", j=2)).then_inc(y_out, 1)

                @block.vector
                def _(dve):
                    of = bc(C("seq_of"), 2, HD)
                    for j in range(2):
                        dve.tensor_tensor(Vx[:, j], bc(tm(V_t)[:, 8, j], 1, NSEQ), of, ALU.mult).then_inc(x_ready, 1)
                    dve.wait_ge(sa_done, 1)
                    for m in range(2):
                        dve.tensor_tensor(SA1[:, m], tm(UU[m])[:, 8], ps[:, 1, m * 128:(m + 1) * 128].rearrange("p (j n) -> p j n", j=2),
                                          ALU.add).then_inc(sa_ready, 1)
                    dve.wait_ge(sa_ready, 2)
                    for x in range(4):
                        dve.tensor_tensor(SAx[:, x], bc(SA1[:, x // 2, x % 2], 1, NSEQ), of, ALU.mult).then_inc(x_ready, 1)
                    dve.wait_ge(y_done, 1)
                    for x in range(4):
                        s = S0[:, x // 2, x % 2]
                        dve.tensor_tensor(s, s, bc(GLs[:, x // 2, x % 2], 2, HD), ALU.mult).then_inc(s_ready, 1)
                    dve.wait_ge(ds_done, 1)
                    dve.wait_ge(s_ready, 4)
                    for x in range(4):
                        s = S0[:, x // 2, x % 2]
                        dve.tensor_tensor(s, s, ps[:, 4 + x, :].rearrange("p (b n) -> p b n", b=NSEQ), ALU.add).then_inc(s_ready, 1)

                @block.sync
                def _(sp):
                    sp.wait_ge(s_ready, 8)
                    sp.dma_start(at("o_state_s"), slot(10, 2)[:, 0:2048]).then_inc(state_out, 16)
                    sp.wait_ge(state_out, 16)

            yr, yg = ch(14), ch(27)
            sqr, rtr, sqg, rtg = ch(21), ch(22), ch(23), ch(24)
            sqc, rtc = slot(5, 2), slot(7, 2)
            with stage(nc, "v_steps", "mean_done", "yc_ready", "sq_ready", "mm_done", "root_ready", "cat_ready") as (
                    block, v_steps, mean_done, yc_ready, sq_ready, mm_done, root_ready, cat_ready):
                vu = [("g", u) for u in range(4)] + [("c", u) for u in range(8)] + [("r", u) for u in range(4)]

                @block.tensor
                def _(pe):
                    for u, (j, q) in enumerate(halves):
                        pe.matmul(ps[:, u, 0:HN], C("head_mean"), yr[:, j, q * HN:(q + 1) * HN], start=True, stop=True).then_inc(mean_done, 1)
                    for n, (k, u) in enumerate(vu):
                        pe.wait_ge(sq_ready, {"g": 1, "c": 2, "r": 3}[k])
                        if n >= 4:
                            pe.wait_ge(root_ready, n - 3)
                        src = {"g": slot(23), "c": sqc, "r": slot(21)}[k][:, u * HN:(u + 1) * HN]
                        pe.matmul(ps[:, 4 + n % 4, 0:HN], C("all_mean" if k == "c" else "head_mean"), src, start=True, stop=True).then_inc(mm_done, 1)

                @block.scalar
                def _(act):
                    for n, (k, u) in enumerate(vu):
                        act.wait_ge(mm_done, n + 1)
                        d = {"g": slot(24), "c": rtc, "r": slot(22)}[k][:, u * HN:(u + 1) * HN]
                        act.activation(d, ps[:, 4 + n % 4, 0:HN], ACT.Copy, bias=64e-5 if k == "r" else EPS).then_inc(root_ready, 1)
                    act.wait_ge(root_ready, 16)
                    for n, d in enumerate((slot(24), rtc, slot(22))):
                        act.activation(d, d, ACT.Sqrt).then_inc(root_ready, 1)

                @block.vector
                def _(dve):
                    st = Steps(dve, v_steps)
                    OCf = slot(2, 2)
                    dve.tensor_tensor(flat(sqg), flat(yg), flat(yg), ALU.mult).then_inc(sq_ready, 1)
                    dve.tensor_tensor(sqc, OCf, OCf, ALU.mult).then_inc(sq_ready, 1)
                    for u, (j, q) in enumerate(halves):
                        dve.wait_ge(mean_done, u + 1)
                        v = yr[:, j, q * HN:(q + 1) * HN]
                        st.did(dve.tensor_tensor(v, v, ps[:, u, 0:HN], ALU.subtract))
                    st.settle()
                    dve.tensor_tensor(flat(sqr), flat(yr), flat(yr), ALU.mult).then_inc(sq_ready, 1)
                    st.link(dve.tensor_tensor(stat[:, 50:51], col("subln"), col("lam_rest"), ALU.mult))
                    dve.wait_ge(root_ready, 17)
                    st.link(dve.reciprocal(flat(rtg), flat(rtg)))
                    st.link(dve.tensor_tensor(flat(rtg), flat(rtg), flat(z_ch), ALU.mult))
                    st.link(dve.tensor_tensor(flat(rtg), flat(rtg), flat(yg), ALU.mult))
                    st.did(dve.tensor_scalar(slot(1), flat(rtg), col("dn_g"), None, ALU.mult))
                    dve.wait_ge(root_ready, 18)
                    st.link(dve.reciprocal(rtc, rtc))
                    st.did(dve.scalar_tensor_tensor(OCf, OCf, stat[:, 50:51], rtc, ALU.mult, ALU.mult))
                    dve.wait_ge(root_ready, 19)
                    st.link(dve.reciprocal(flat(rtr), flat(rtr)))
                    st.link(dve.tensor_tensor(flat(yr), flat(yr), flat(rtr), ALU.mult))
                    for j in range(2):
                        st.did(dve.tensor_scalar(yr[:, j], yr[:, j], col("ln_g", j), col("ln_b", j), ALU.mult, ALU.add))
                    st.settle()
                    st.link(dve.tensor_tensor(flat(yr), flat(yr), flat(yadd), ALU.add))
                    st.did(dve.tensor_tensor(slot(0), flat(yr), flat(gate), ALU.mult))
                    st.settle()

            with stage(nc, "wo_in0", "wo_in1", "hi_ready", "lo_ready", "cat_hi", "cat_ready", "mm_done", "x_steps") as (
                    block, wo_in0, wo_in1, hi_ready, lo_ready, cat_hi, cat_ready, mm_done, x_steps):
                ou = [(g, i) for g in range(D // WCH) for i in range(TILES)]
                wo_in = (wo_in0, wo_in1)
                raw = w_raw(4)

                @block.sync
                def _(sp):
                    wv = at("w_out").rearrange("(k p) n -> p k n", p=P)
                    for g in range(D // WCH):
                        if g >= 2:
                            sp.wait_ge(lo_ready, g - 1)
                        sp.dma_start(raw[:, g % 2], wv[:, :, g * WCH:(g + 1) * WCH]).then_inc(wo_in[g % 2], 16)

                @block.tensor
                def _(pe):
                    for u, (g, i) in enumerate(ou):
                        if i == 0:
                            pe.wait_ge(lo_ready, g + 1)
                        if u == 0:
                            pe.wait_ge(cat_ready, KC + 2)
                        if u >= 8:
                            pe.wait_ge(x_steps, u - 7)
                        wh, wl = w_part(g % 2, 0), w_part(g % 2, 1)
                        split_products(pe, ps[:, u % 8, 0:WCH], [(x_tile(k, i), (wh[:, k, :], wl[:, k, :])) for k in range(KC)]).then_inc(mm_done, 1)

                @block.scalar
                def _(act):
                    for k in range(KC):
                        act.copy(x_part(0)[:, k], cat[:, k]).then_inc(cat_hi, 1)
                    for g in range(D // WCH):
                        if g >= 2:
                            act.wait_ge(mm_done, TILES * (g - 1))
                        hi_of(act, g, raw, wo_in, hi_ready)

                @block.gpsimd
                def _(pool):
                    for h in range(2):
                        pool.tensor_copy(x_split[:, h * XW + KC * TOK:(h + 1) * XW], C("ones")).then_inc(cat_ready, 1)
                    for g in range(D // WCH):
                        lo_of(pool, g, raw, hi_ready, lo_ready)

                @block.vector
                def _(dve):
                    for k in range(KC):
                        dve.wait_ge(cat_hi, k + 1)
                        dve.tensor_tensor(x_part(1)[:, k], cat[:, k], x_part(0)[:, k].bitcast(F32), ALU.subtract).then_inc(cat_ready, 1)
                    for u, (g, i) in enumerate(ou):
                        w = min(P, TOK - i * P)
                        dve.wait_ge(mm_done, u + 1)
                        d = x_sb[0:w, i, g * WCH:(g + 1) * WCH]
                        dve.tensor_tensor(d, d, ps[0:w, u % 8, 0:WCH], ALU.add).then_inc(x_steps, 1)

            norm_transposed("ffn_g")
            qT = slot(0, 8).rearrange("p (c t) -> p c t", c=16)
            keys = slot(8, 2)[:, 0:2048].rearrange("p (c n) -> p c n", c=16)
            qu = [(c, q) for c in range(16) for q in range(2)]
            with stage(nc, "keys_in", "wq_in0", "wq_in1", "hi_ready", "lo_ready", "mm_done", "act_out", "dve_out") as (
                    block, keys_in, wq_in0, wq_in1, hi_ready, lo_ready, mm_done, act_out, dve_out):
                wq_in = (wq_in0, wq_in1)
                raw = w_raw(10)
                wqv = at("pk_wq").rearrange("(k p) n -> p k n", p=P)

                @block.sync
                def _(sp):
                    for g in range(8):
                        if g >= 2:
                            sp.wait_ge(lo_ready, g - 1)
                        sp.dma_start(raw[:, g % 2], wqv[:, :, g * WCH:(g + 1) * WCH]).then_inc(wq_in[g % 2], 16)
                    sp.dma_start(keys, at("pk_keys")).then_inc(keys_in, 16)
                    sp.wait_ge(keys_in, 16)

                @block.tensor
                def _(pe):
                    for u, (c, q) in enumerate(qu):
                        g, m = c // 2, (c % 2) * P
                        if u % 4 == 0:
                            pe.wait_ge(lo_ready, g + 1)
                        if u >= 8:
                            pe.wait_ge(dve_out if u % 2 else act_out, (u - 8) // 2 + 1)
                        wh, wl = w_part(g % 2, 0), w_part(g % 2, 1)
                        tq = slice(q * HN, (q + 1) * HN)
                        last = split_products(pe, ps[:, u % 8, 0:HN], [((wh[:, k, m:m + P], wl[:, k, m:m + P]), (x_part(0)[:, k, tq], x_part(1)[:, k, tq]))
                                                                      for k in range(KC)])
                        last.then_inc(mm_done, 1)

                @block.scalar
                def _(act):
                    for g in range(2):
                        hi_of(act, g, raw, wq_in, hi_ready)
                    for u in range(0, 32, 2):
                        if u and u % 4 == 0 and u < 28:
                            act.wait_ge(mm_done, u)
                            hi_of(act, u // 4 + 1, raw, wq_in, hi_ready)
                        act.wait_ge(mm_done, u + 1)
                        act.copy(qT[:, qu[u][0], 0:HN], ps[:, u % 8, 0:HN]).then_inc(act_out, 1)

                @block.gpsimd
                def _(pool):
                    for g in range(8):
                        lo_of(pool, g, raw, hi_ready, lo_ready)

                @block.vector
                def _(dve):
                    for u in range(1, 32, 2):
                        dve.wait_ge(mm_done, u + 1)
                        dve.tensor_copy(qT[:, qu[u][0], HN:TOK], ps[:, u % 8, 0:HN]).then_inc(dve_out, 1)

            SC = slot(10, 2)[:, 0:2048].rearrange("p (c n) -> p c n", c=16)
            cand = slot(12, 2)[:, 0:2048].rearrange("p (h n) -> p h n", h=PK_HEADS)
            cand2 = slot(14, 2)[:, 0:2048].rearrange("p (h n) -> p h n", h=PK_HEADS)
            TG = 32
            NTG = TOK // TG
            OCT = 8
            stg = slot(16, 4)[:, 0:P * TG].rearrange("p (e t) -> p e t", e=P)
            rest = arena[:, W_AT:ARENA]
            rt = rest[:, 0:2064]
            SV = rt[:, 0:256].rearrange("p (c n) -> p c n", c=16)
            SI = rt[:, 256:512].bitcast(U32).rearrange("p (c n) -> p c n", c=16)
            SIf = rt[:, 512:768].rearrange("p (h c n) -> p h c n", h=PK_HEADS, c=2)
            TV = rt[:, 768:896].rearrange("p (h n) -> p h n", h=PK_HEADS)
            TI = rt[:, 896:1024].bitcast(U32).rearrange("p (h n) -> p h n", h=PK_HEADS)
            TA = rt[:, 1024:1280].bitcast(U32).rearrange("p (c n) -> p c n", c=2)
            TAf = rt[:, 1280:1536].rearrange("p (c n) -> p c n", c=2)
            route = rt[:, 1536:1920].rearrange("p (k n) -> p k n", k=3)
            ex = rt[:, 1920:2048].rearrange("p (h n) -> p h n", h=PK_HEADS)
            sums = rt[:, 2048:2064]
            routeT = rest[:, 2064:2064 + 3 * TOKP].rearrange("p (k t) -> p k t", k=3)
            AB = rest[:, 2064 + 3 * TOKP:2064 + 3 * TOKP + 4 * OCT * P].rearrange("p (s m t n) -> p s m t n", s=2, m=2, t=OCT)
            gd = t["g_scratch"]
            octets = lambda i: (min(P, TOK - i * P)) // OCT
            with stage(nc, "s_done", "s_out", "v_steps", "sc_free", "halves_ready", "cand_ready", "shifted", "exp_done", "eq_ready", "looked_up", "route_ready", "t_done", "t_out", "onehots_ready", "b_ready", "g_done", "g_out", "g_saved") as (
                    block, s_done, s_out, v_steps, sc_free, halves_ready, cand_ready, shifted, exp_done, eq_ready,
                    looked_up, route_ready, t_done, t_out, onehots_ready, b_ready, g_done, g_out, g_saved):
                @block.tensor
                def _(pe):
                    def scores(i):
                        w = min(P, TOK - i * P)
                        if i >= 1:
                            pe.wait_ge(s_out, 4 * i)
                        if i >= 2:
                            pe.wait_ge(t_out, i - 1)
                        for b in range(4):
                            for n in range(4):
                                c = b * 4 + n
                                last = pe.matmul(ps[0:w, b, n * P:(n + 1) * P], qT[:, c, i * P:i * P + w], keys[:, c, :], start=True, stop=True)
                            last.then_inc(s_done, 1)

                    def turn(i):
                        w = min(P, TOK - i * P)
                        pe.wait_ge(route_ready, i + 1)
                        if i + 1 < TILES:
                            pe.wait_ge(s_out, 4 * (i + 2))
                        for k in range(3):
                            last = pe.transpose(ps[:, 0, k * P:k * P + w], route[0:w, k, :], C("ident")[0:w, 0:w])
                        last.then_inc(t_done, 1)

                    def spread(i, first, n):
                        with pe.Fori(0, n // 2) as o2:
                            for s in range(2):
                                o = o2 * 2 + (i * P // OCT + first + s)
                                pe.wait_ge(g_out, o * 2 + 2)
                                pe.wait_ge(b_ready, o + 1)
                                for k in range(OCT):
                                    last = pe.matmul(ps[:, 4 + 2 * s + k // 4, (k % 4) * P:(k % 4 + 1) * P], AB[:, s, 0, k], AB[:, s, 1, k],
                                                     start=True, stop=True)
                                    if k % 4 == 3:
                                        last.then_inc(g_done, 1)
                    pe.sem_inc(g_out, 4)
                    scores(0)
                    scores(1)
                    turn(0)
                    for i in range(TILES):
                        spread(i, 0, octets(i) - 4)
                        if i + 2 < TILES:
                            scores(i + 2)
                        spread(i, octets(i) - 4, 4)
                        if i + 1 < TILES:
                            turn(i + 1)

                @block.scalar
                def _(act):
                    def scores_out(i):
                        w = min(P, TOK - i * P)
                        if i >= 1:
                            act.wait_ge(sc_free, i)
                        for b in range(4):
                            act.wait_ge(s_done, 4 * i + b + 1)
                            act.copy(SC[0:w, 4 * b:4 * b + 4], ps[0:w, b, :].rearrange("p (c n) -> p c n", c=4)).then_inc(s_out, 1)

                    def routes_out(i):
                        w = min(P, TOK - i * P)
                        act.wait_ge(shifted, i + 1)
                        act.activation(ex[0:w], ex[0:w], ACT.Exp).then_inc(exp_done, 1)
                        act.wait_ge(t_done, i + 1)
                        act.copy(routeT[:, :, i * P:i * P + w], ps[:, 0, 0:3 * P].rearrange("p (k t) -> p k t", k=3)[:, :, 0:w]).then_inc(t_out, 1)

                    def gates_out(i, first, n):
                        with act.Fori(0, n) as it:
                            g = it + (i * P // TG + first)
                            act.wait_ge(g_saved, g * 16 + 16)
                            for q in range(TG // 4):
                                act.wait_ge(g_done, g * (TG // 4) + (q + 1))
                                act.copy(stg[:, :, q * 4:q * 4 + 4], ps[:, 4 + q % 4, :].rearrange("p (t e) -> p e t", t=4)).then_inc(g_out, 1)
                    act.sem_inc(g_saved, 16)
                    scores_out(0)
                    scores_out(1)
                    routes_out(0)
                    for i in range(TILES):
                        n = octets(i) * OCT // TG
                        gates_out(i, 0, n - 1)
                        if i + 2 < TILES:
                            scores_out(i + 2)
                        gates_out(i, n - 1, 1)
                        if i + 1 < TILES:
                            routes_out(i + 1)

                @block.gpsimd
                def _(pool):
                    def gated(i, first, n):
                        if i < 0:
                            return
                        for o in range(i * P // OCT + first, i * P // OCT + min(first + n, octets(i))):
                            pool.wait_ge(onehots_ready, o + 1)
                            pool.tensor_tensor(AB[:, o % 2, 1], AB[:, o % 2, 1], bc(routeT[:, 2, o * OCT:(o + 1) * OCT], 2, P),
                                               ALU.mult).then_inc(b_ready, 1)
                    for i in range(TILES):
                        w = min(P, TOK - i * P)
                        r = slice(0, w)
                        v = SV.rearrange("p (h c) n -> p h c n", c=2)[r]
                        gated(i - 1, 0, 9)
                        pool.wait_ge(halves_ready, i + 1)
                        pool.tensor_tensor(cand[r].rearrange("p h (a b) -> p h a b", a=TOPK), bc(v[:, :, 0], 3, TOPK), bc(v[:, :, 1], 2, TOPK),
                                           ALU.add).then_inc(cand_ready, 1)
                        gated(i - 1, 9, 6)
                        for c in range(2):
                            e = (cand, cand2)[c][r].rearrange("p h (j a) -> p h j a", a=TOPK)
                            pool.wait_ge(eq_ready, 2 * i + c + 1)
                            pool.tensor_tensor(e, e, bc(SIf[r, :, c], 2, TOPK), ALU.mult).then_inc(looked_up, 1)
                        gated(i - 1, 15, 1)
                    gated(TILES - 1, 0, 16)

                @block.vector
                def _(dve):
                    st = Steps(dve, v_steps)

                    def onehots(i, first, n):
                        if i < 0:
                            return
                        if first == 0:
                            dve.wait_ge(t_out, i + 1)
                        for o in range(i * P // OCT + first, i * P // OCT + min(first + n, octets(i))):
                            if o >= 2:
                                dve.wait_ge(g_done, 2 * (o - 1))
                            dve.tensor_tensor(AB[:, o % 2], bc(bc(C("iota"), 1, OCT), 1, 2), bc(routeT[:, 0:2, o * OCT:(o + 1) * OCT], 3, P),
                                              ALU.is_equal).then_inc(onehots_ready, 1)
                    for i in range(TILES):
                        w = min(P, TOK - i * P)
                        r = slice(0, w)
                        dve.wait_ge(s_out, 4 * (i + 1))
                        if i:
                            dve.wait_ge(t_done, i)

                        def best16(n, vals, idx, src, octs):
                            steps_of = (lambda c: dve.max(vals[r, c, 0:8], src[:, c]),
                                        lambda c: dve.max_index(idx[r, c, 0:8], vals[r, c, 0:8], src[:, c]),
                                        lambda c: dve.match_replace(src[:, c], vals[r, c, 0:8], src[:, c], -3.0e38),
                                        lambda c: dve.max(vals[r, c, 8:16], src[:, c]),
                                        lambda c: dve.max_index(idx[r, c, 8:16], vals[r, c, 8:16], src[:, c]))
                            for step in steps_of:
                                for c in range(n):
                                    st.did(step(c))
                                    if c % 8 == 7 and octs:
                                        onehots(i - 1, octs.pop(0), 1)
                                st.settle()
                        best16(16, SV, SI, SC[r], list(range(9)))
                        dve.sem_inc(sc_free, 1)
                        dve.sem_inc(halves_ready, 1)
                        st.did(dve.tensor_copy(SIf[r].rearrange("p h c n -> p (h c n)"), SI[r].rearrange("p c n -> p (c n)")))
                        onehots(i - 1, 9, 2)
                        dve.wait_ge(cand_ready, i + 1)
                        best16(PK_HEADS, TV, TI, cand[r], list(range(11, 15)))
                        dve.tensor_tensor(ex[r], TV[r], TV[r, :, 0:1].broadcast_to([w, PK_HEADS, TOPK]), ALU.subtract).then_inc(shifted, 1)
                        ti = TI[r].rearrange("p h n -> p (h n)")
                        st.did(dve.tensor_scalar(TA[r, 0], ti, 4, None, ALU.logical_shift_right))
                        st.did(dve.tensor_scalar(TA[r, 1], ti, 15, None, ALU.bitwise_and))
                        st.settle()
                        st.link(dve.tensor_copy(TAf[r], TA[r]))
                        for c in range(2):
                            e = (cand, cand2)[c][r].rearrange("p h (j a) -> p (h j) a", a=TOPK)
                            dve.tensor_tensor(e, bc(C("iota")[r, 0:TOPK], 1, P), bc(TAf[r, c], 2, TOPK), ALU.is_equal).then_inc(eq_ready, 1)
                        onehots(i - 1, 15, 1)
                        for c in range(2):
                            dve.wait_ge(looked_up, 2 * i + c + 1)
                            e = (cand, cand2)[c][r].rearrange("p h (j a) -> p (h j) a", a=TOPK)
                            st.did(dve.tensor_reduce(route[r, c], e, AX.X, ALU.add))
                        dve.wait_ge(exp_done, i + 1)
                        st.link(dve.tensor_reduce(sums[r, 0:8], ex[r], AX.X, ALU.add))
                        st.link(dve.reciprocal(sums[r, 8:16], sums[r, 0:8]))
                        dve.tensor_tensor(route[r, 2].rearrange("p (h n) -> p h n", h=PK_HEADS), ex[r], bc(sums[r, 8:16], 2, TOPK), ALU.mult).then_inc(route_ready, 1)
                    onehots(TILES - 1, 0, 16)

                @block.sync
                def _(sp):
                    with sp.Fori(0, NTG) as g:
                        sp.wait_ge(g_out, g * (TG // 4) + (TG // 4 + 4))
                        sp.dma_start(gd[:, bass.ds(g, 1)].rearrange("p g e t -> p (g e t)"), stg.rearrange("p e t -> p (e t)")).then_inc(g_saved, 16)
                    sp.wait_ge(g_saved, NTG * 16 + 16)

            PAIRS = PK_KEYS // 2
            acc = slot(0, 4).rearrange("p (d q t) -> p d q t", d=KC, q=2)
            u_raw = slot(12, 2)[:, 0:2 * D].rearrange("p (e n) -> p e n", e=2)
            v_raw = slot(14, 2)[:, 0:2 * D].rearrange("p (e n) -> p e n", e=2)
            Gt = slot(16, 2).rearrange("p (s g e t) -> p s g e t", s=2, g=NTG, e=2)
            gh = slot(18).rearrange("p (e t) -> p e t", e=2)
            us = u_split[:, :].rearrange("p (e h n) -> p e h n", e=2, h=2)
            vs = w_split[:, :].rearrange("p (s e h n) -> p s e h n", s=2, e=2, h=2)
            cs = c_split[:, :].rearrange("p (s e h t) -> p s e h t", s=2, e=2, h=2)
            uv = at("pk_u")
            vv = at("pk_v").rearrange("(p n e) d -> n e p d", p=P, e=2)
            with stage(nc, "u_in0", "u_in1", "v_in0", "v_in1", "g_in0", "g_in1", "u_hi", "u_ready", "v_hi", "v_ready", "h_done", "gelu_done",
                       "c_steps", "o_done", "o_free", "pair_done", "zeroed") as (
                    block, u_in0, u_in1, v_in0, v_in1, g_in0, g_in1, u_hi, u_ready, v_hi, v_ready, h_done, gelu_done, c_steps, o_done,
                    o_free, pair_done, zeroed):
                u_in, v_in, g_in = (u_in0, u_in1), (v_in0, v_in1), (g_in0, g_in1)

                @block.sync
                def _(sp):
                    def load_u(k, e):
                        sp.dma_start(u_raw[:, e], uv[bass.ds(k * 2 + e, 1)].rearrange("o p x -> (o p) x")).then_inc(u_in[e], 16)

                    def load_v(k, e):
                        sp.dma_start(v_raw[:, e], vv[bass.ds(k, 1), e].rearrange("o p d -> (o p) d")).then_inc(v_in[e], 16)

                    def load_g(k, s):
                        sp.dma_start(Gt[:, s].rearrange("p g e t -> p g (e t)"),
                                     gd[:, :, bass.ds(k * 2, 2)].rearrange("p g e t -> p g (e t)")).then_inc(g_in[s], 16)

                    def loads(k, s):
                        for e in range(2):
                            sp.wait_ge(u_ready, k * 2 + (e - 1))
                            load_u(k, e)
                        for e in range(2):
                            sp.wait_ge(v_ready, k * 2 + (e - 1))
                            load_v(k, e)
                        sp.wait_ge(c_steps, k * 6)
                        load_g(k, s)
                    for e in range(2):
                        load_u(0, e)
                        load_v(0, e)
                    load_g(0, 0)
                    sp.sem_inc(c_steps, 6)
                    loads(1, 1)
                    with sp.Fori(0, PAIRS // 2 - 1) as i:
                        for s in range(2):
                            loads(i * 2 + (2 + s), s)

                @block.scalar
                def _(act):
                    def u_hi_of(k, e):
                        act.wait_ge(u_in[e], k * 16 + 16)
                        act.copy(us[:, e, 0], u_raw[:, e]).then_inc(u_hi, 1)

                    def v_hi_of(k, s, e):
                        act.wait_ge(v_in[e], k * 16 + 16)
                        act.copy(vs[:, s, e, 0], v_raw[:, e]).then_inc(v_hi, 1)

                    def steps(k, s, more):
                        for e in range(2):
                            act.wait_ge(c_steps, k * 6 + (3 * e + 3))
                            for q in range(2):
                                act.wait_ge(h_done, k * 4 + (2 * e + q + 1))
                                act.activation(gh[:, e, q * HN:(q + 1) * HN], ps[:, 2 * e + q, 0:HN], ACT.Gelu).then_inc(gelu_done, 1)
                            if more:
                                u_hi_of(k + 1, e)
                        if more:
                            act.wait_ge(pair_done, k + 2)
                            for e in range(2):
                                v_hi_of(k + 1, 1 - s, e)
                    act.sem_inc(gelu_done, 4)
                    for e in range(2):
                        u_hi_of(0, e)
                        v_hi_of(0, 0, e)
                    with act.Fori(0, PAIRS // 2 - 1) as i:
                        for s in range(2):
                            steps(i * 2 + s, s, True)
                    steps(PAIRS - 2, 0, True)
                    steps(PAIRS - 1, 1, False)

                @block.gpsimd
                def _(pool):
                    def lo_parts(k, s):
                        for e in range(2):
                            pool.wait_ge(u_hi, k * 2 + (e + 1))
                            pool.tensor_tensor(us[:, e, 1], u_raw[:, e], us[:, e, 0].bitcast(F32), ALU.subtract).then_inc(u_ready, 1)
                        for e in range(2):
                            pool.wait_ge(v_hi, k * 2 + (e + 1))
                            pool.tensor_tensor(vs[:, s, e, 1], v_raw[:, e], vs[:, s, e, 0].bitcast(F32), ALU.subtract).then_inc(v_ready, 1)
                    with pool.Fori(0, PAIRS // 2) as i:
                        for s in range(2):
                            lo_parts(i * 2 + s, s)

                @block.tensor
                def _(pe):
                    def hidden(k):
                        for e in range(2):
                            pe.wait_ge(u_ready, k * 2 + (e + 1))
                            for q in range(2):
                                pe.wait_ge(gelu_done, k * 4 + (2 * e + q + 1))
                                tq = slice(q * HN, (q + 1) * HN)
                                split_products(pe, ps[:, 2 * e + q, 0:HN],
                                               [((us[:, e, 0, c * P:(c + 1) * P], us[:, e, 1, c * P:(c + 1) * P]),
                                                 (x_part(0)[:, c, tq], x_part(1)[:, c, tq])) for c in range(KC)]).then_inc(h_done, 1)

                    def output(k, s):
                        pe.wait_ge(v_ready, k * 2 + 2)
                        pe.wait_ge(c_steps, k * 6 + 12)
                        for u in range(16):
                            d, q = u // 2, u % 2
                            tq = slice(q * HN, (q + 1) * HN)
                            pe.wait_ge(o_free, k * 16 + (u + 1))
                            split_products(pe, ps[:, 4 + u % 4, 0:HN],
                                           [((vs[:, s, e, 0, d * P:(d + 1) * P], vs[:, s, e, 1, d * P:(d + 1) * P]),
                                             (cs[:, s, e, 0, tq], cs[:, s, e, 1, tq])) for e in range(2)]).then_inc(o_done, 1)
                        pe.wait_ge(o_done, k * 16 + 16)
                        pe.sem_inc(pair_done, 1)
                    pe.sem_inc(pair_done, 2)
                    hidden(0)
                    with pe.Fori(0, PAIRS // 2 - 1) as i:
                        for s in range(2):
                            hidden(i * 2 + (s + 1))
                            output(i * 2 + s, s)
                    hidden(PAIRS - 1)
                    output(PAIRS - 2, 0)
                    output(PAIRS - 1, 1)

                @block.vector
                def _(dve):
                    def product(k, s, e, n):
                        dve.wait_ge(g_in[s], n)
                        dve.wait_ge(gelu_done, k * 4 + (2 * e + 6))
                        h = gh[:, e].rearrange("p (g t) -> p g t", t=TG)
                        dve.tensor_tensor(h, h, Gt[:, s, :, e], ALU.mult).then_inc(c_steps, 1)

                    def hi(k, s, e):
                        dve.wait_ge(c_steps, k * 6 + (3 * e + 7))
                        dve.wait_ge(pair_done, k + 1)
                        dve.tensor_copy(cs[:, s, e, 0], gh[:, e]).then_inc(c_steps, 1)

                    def lo(k, s, e):
                        dve.wait_ge(c_steps, k * 6 + (3 * e + 8))
                        dve.tensor_tensor(cs[:, s, e, 1], gh[:, e], cs[:, s, e, 0].bitcast(F32), ALU.subtract).then_inc(c_steps, 1)

                    def add(k, units):
                        for u in units:
                            d, q = u // 2, u % 2
                            dve.wait_ge(o_done, k * 16 + (u + 1))
                            dve.tensor_tensor(acc[:, d, q], acc[:, d, q], ps[:, 4 + u % 4, 0:HN], ALU.add).then_inc(o_free, 1)

                    def steps(k, s, n):
                        product(k, s, 0, n)
                        hi(k, s, 0)
                        lo(k, s, 0)
                        dve.wait_ge(o_free, k * 16 - 12)
                        add(k - 1, range(0, 3))
                        product(k, s, 1, n)
                        add(k - 1, range(3, 6))
                        hi(k, s, 1)
                        add(k - 1, range(6, 9))
                        lo(k, s, 1)
                        add(k - 1, range(9, 16))
                    dve.sem_inc(o_free, 4)
                    dve.memset(slot(0, 4), 0.0).then_inc(zeroed, 1)
                    dve.wait_ge(zeroed, 1)
                    for e in range(2):
                        product(0, 0, e, 16)
                        hi(0, 0, e)
                        lo(0, 0, e)
                    with dve.Fori(0, PAIRS // 2 - 1) as i:
                        steps(i * 2 + 1, 1, i * 16 + 16)
                        steps(i * 2 + 2, 0, i * 16 + 32)
                    steps(PAIRS - 1, 1, PAIRS // 2 * 16)
                    dve.wait_ge(o_free, (PAIRS - 1) * 16 + 4)
                    add(PAIRS - 1, range(16))

            with stage(nc, "t_done", "x_ready") as (block, t_done, x_ready):
                accT = slot(0, 4).rearrange("p (d t) -> p d t", d=KC)

                @block.tensor
                def _(pe):
                    for u in range(2 * TILES):
                        i, n = u // 2, u % 2
                        w = min(P, TOK - i * P)
                        if u >= 8:
                            pe.wait_ge(x_ready, u - 7)
                        for d in range(4):
                            last = pe.transpose(ps[0:w, u % 8, d * P:(d + 1) * P], accT[:, n * 4 + d, i * P:i * P + w], C("ident"))
                        last.then_inc(t_done, 1)

                @block.vector
                def _(dve):
                    for u in range(2 * TILES):
                        i, n = u // 2, u % 2
                        w = min(P, TOK - i * P)
                        dve.wait_ge(t_done, u + 1)
                        d = x_sb[0:w, i, n * 512:(n + 1) * 512]
                        dve.tensor_tensor(d, d, ps[0:w, u % 8, :], ALU.add).then_inc(x_ready, 1)


        with stage(nc, "y_out") as (block, y_out):
            @block.sync
            def _(sp):
                sp.dma_start(t["o_y"].rearrange("(i p) d -> p i d", p=P), x_sb[:, :, :]).then_inc(y_out, 16)
                sp.wait_ge(y_out, 16)


_OUTS = [("o_y", (TOKP, D)), ("o_kp", (DEPTH, SEQ, 512)), ("o_vp", (DEPTH, SEQ, 512)),
         ("o_ks", (DEPTH, SAMP, 512)), ("o_vs", (DEPTH, SAMP, 512)),
         ("o_state_p", (DEPTH, P, 256)), ("o_state_s", (DEPTH, P, 2048)), ("o_tails", (DEPTH, P, 234))]

_SCRATCH = [("rel_scratch", (P, H * (REL + 1))), ("g_scratch", (P, TOK // 32, P, 32))]


def lay_out(i):
    f = lambda n: np.ascontiguousarray(np.asarray(i[n], dtype=None))
    a = {}
    a["x_prompt"] = f("x_prompt").reshape(SEQ, D)
    a["x_sample"] = f("x_sample").reshape(SAMP, D)
    a["cache_k"], a["cache_v"] = f("cache_k"), f("cache_v")
    a["page_table"] = f("page_table")
    a["w_in"], a["w_out"], a["rel_bias"] = f("w_in"), f("w_out"), f("rel_bias")
    per = lambda n: f(n).reshape(DEPTH, -1, P).transpose(0, 2, 1)
    cols = np.zeros((DEPTH, P, NCOL), np.float32)

    def put(name, v):
        o, n = COLS[name]
        cols[:, :, o:o + n] = v
    for name, src in (("mix_g", "rms_mix_g"), ("ffn_g", "rms_ffn_g"), ("mu", "rw_mu"), ("w0", "rw_w0"), ("a0", "rw_a0"),
                      ("kk", "rw_kk"), ("ka", "rw_ka"), ("rk", "rw_rk"), ("ln_g", "rw_ln_g"), ("ln_b", "rw_ln_b"),
                      ("conv", "dn_conv_w"), ("subln", "df_subln_g")):
        put(name, per(src))
    put("dn_g", np.tile(f("dn_norm_g"), (1, 2))[:, :, None])
    halves = lambda n: np.repeat(f(n).reshape(DEPTH, 2, 2).transpose(0, 2, 1), 64, axis=1)
    put("a_log", halves("dn_a_log"))
    put("dt", halves("dn_dt_bias"))
    init = np.array([0.8 - 0.6 * math.exp(-0.3 * l) for l in range(DEPTH)], np.float32)
    put("lam_init", init[:, None, None])
    put("lam_rest", np.array([1.0 - (0.8 - 0.6 * math.exp(-0.3 * l)) for l in range(DEPTH)], np.float32)[:, None, None])
    a["cols"] = cols
    a["rows"] = np.concatenate([f("df_qn_g").reshape(DEPTH, P), f("df_kn_g").reshape(DEPTH, P)]
                               + [f(n) for n in ("df_lq1", "df_lk1", "df_lq2", "df_lk2")], axis=1)
    a["lora"] = np.concatenate([np.concatenate([f("rw_w2"), f("rw_a2")], axis=1), f("rw_g2")], axis=2)
    shift = f("state_rwkv_shift").reshape(DEPTH, NSEQ, 8, P).transpose(0, 3, 2, 1).reshape(DEPTH, P, 64)
    conv = f("state_dn_conv").reshape(DEPTH, NSEQ, 3, 6, P).transpose(0, 4, 3, 1, 2).reshape(DEPTH, P, 144)
    a["tails"] = np.concatenate([shift, conv], axis=2)
    sr = f("state_rwkv").reshape(DEPTH, NSEQ, 2, 2, HD, HD).transpose(0, 3, 5, 2, 1, 4).reshape(DEPTH, P, 1024)
    sd = f("state_dn").reshape(DEPTH, NSEQ, 2, 2, HD, HD).transpose(0, 3, 4, 2, 1, 5).reshape(DEPTH, P, 1024)
    a["states"] = np.concatenate([sr, sd], axis=2)
    a["pk_wq"] = f("pk_wq")
    a["pk_keys"] = f("pk_keys").transpose(0, 4, 1, 2, 3).reshape(DEPTH, P, 16 * P)
    a["pk_u"] = f("pk_u").reshape(DEPTH, P, P, KC, P).transpose(0, 2, 4, 3, 1).reshape(DEPTH, P, P, D)
    a["pk_v"] = f("pk_v")
    a["consts"], a["buckets"], a["future"] = constants()
    return {k: np.ascontiguousarray(v) for k, v in a.items()}


def results_of(r):
    y = r["o_y"]
    kp, vp = (r[n].reshape(1, DEPTH, SEQ, H, 2 * HD) for n in ("o_kp", "o_vp"))
    ks, vs = (r[n].reshape(DEPTH, NSEQ, NEW, H, 2 * HD).transpose(1, 0, 2, 3, 4) for n in ("o_ks", "o_vs"))
    sp = r["o_state_p"].reshape(DEPTH, 2, HD, 2, 2, HD)
    ap = sp[:, :, :, 0].transpose(0, 3, 1, 4, 2).reshape(DEPTH, 1, H, HD, HD)
    bp = sp[:, :, :, 1].transpose(0, 3, 1, 2, 4).reshape(DEPTH, 1, H, HD, HD)
    ss = r["o_state_s"].reshape(DEPTH, 2, HD, 2, 2, NSEQ, HD)
    as_ = ss[:, :, :, 0].transpose(0, 4, 3, 1, 5, 2).reshape(DEPTH, NSEQ, H, HD, HD)
    bs = ss[:, :, :, 1].transpose(0, 4, 3, 1, 2, 5).reshape(DEPTH, NSEQ, H, HD, HD)
    tl = r["o_tails"]
    shp = tl[:, :, 0:8].transpose(0, 2, 1).reshape(DEPTH, 1, A_COLS)
    shs = tl[:, :, 8:72].reshape(DEPTH, P, 8, NSEQ).transpose(0, 3, 2, 1).reshape(DEPTH, NSEQ, A_COLS)
    cvp = tl[:, :, 72:90].reshape(DEPTH, P, 6, 3).transpose(0, 3, 2, 1).reshape(DEPTH, 1, 3, 768)
    cvs = tl[:, :, 90:234].reshape(DEPTH, P, 6, NSEQ, 3).transpose(0, 3, 4, 2, 1).reshape(DEPTH, NSEQ, 3, 768)
    out = (y[:SEQ].reshape(1, SEQ, D), y[SEQ:TOK].reshape(NSEQ, NEW, D), kp, vp, ks, vs, ap, as_, shp, shs, bp, bs, cvp, cvs)
    return tuple(np.ascontiguousarray(o) for o in out)


def kernel(**inputs):
    import concourse.bacc as bacc
    from concourse.bass_utils import run_bass_kernel_spmd

    nc = bacc.Bacc("TRN2", target_bir_lowering=False, num_devices=1)
    arrays = lay_out(inputs)
    t = {n: nc.dram_tensor(n, a.shape, mybir.dt.from_np(a.dtype), kind="ExternalInput").ap() for n, a in arrays.items()}
    for n, shape in _OUTS:
        t[n] = nc.dram_tensor(n, shape, F32, kind="ExternalOutput").ap()
    for n, shape in _SCRATCH:
        t[n] = nc.dram_tensor(n, shape, F32, kind="Internal").ap()
    trunk(nc, t)
    r = run_bass_kernel_spmd(nc, [arrays], core_ids=[0])
    return results_of(r.results[0])
```

```python
import math
from contextlib import ExitStack, contextmanager

import numpy as np

import concourse.bass as bass
from concourse import mybir

F32 = mybir.dt.float32
F32R = mybir.dt.float32r
U32 = mybir.dt.uint32
ALU = mybir.AluOpType
ACT = mybir.ActivationFunctionType
AX = mybir.AxisListType

P = 128
D = 1024
KC = D // P
SEQ = 512
DEPTH = 2
NSEQ = 8
NEW = 8
SAMP = NSEQ * NEW
TOK = SEQ + SAMP
TILES = 5
TOKP = TILES * P
HN = TOK // 2
PAST = 256
PAGE = 128
PAGES = PAST // PAGE
H = 4
HD = 64
CH = 64
NCH = TOK // CH
A_COLS, B_COLS, C_W = 1024, 1032, 512
COL_B, COL_AB, COL_Z, COL_C = 1024, 1792, 1800, 2056
EPS = 1e-6
KAPPA = math.exp(-0.5)
NEG = -1e30
BUCKETS = 32
REL = 639
PK_HEADS, PK_KEYS, TOPK = 8, 128, 16
SLOT = 2 * TOK
XW = KC * TOK + CH
WCH = 2 * P
X_AT = 14 * SLOT + TILES * 3 * C_W
W_AT = X_AT + 2 * XW
ARENA = W_AT + 4 * KC * WCH

COLS = {}
for _name, _n in (("mix_g", 8), ("ffn_g", 8), ("mu", 8), ("w0", 2), ("a0", 2), ("kk", 2), ("ka", 2),
                  ("rk", 2), ("ln_g", 2), ("ln_b", 2), ("conv", 24), ("subln", 1), ("dn_g", 1),
                  ("a_log", 2), ("dt", 2), ("lam_init", 1), ("lam_rest", 1)):
    COLS[_name] = (sum(n for _, n in COLS.values()), _n)
NCOL = sum(n for _, n in COLS.values())

CONST = {}
for _name, _n in (("ident", 128), ("head_mean", 128), ("all_mean", 128), ("iota", 128), ("id64", 64),
                  ("U_p", 64), ("SU_p", 64), ("SUt_p", 64), ("U_s", 64), ("SU_s", 64), ("SUt_s", 64),
                  ("lev", 6 * 64), ("seq_of", 8), ("ones", 64), ("is_c0", 1), ("is_c1", 1), ("last", 8)):
    CONST[_name] = (sum(n for _, n in CONST.values()), _n)
NCONST = sum(n for _, n in CONST.values())


def constants():
    c = np.zeros((P, NCONST), np.float32)

    def put(name, a):
        o, n = CONST[name]
        c[:, o:o + n] = a
    i = np.arange(64)
    s, t = i[:, None], i[None, :]
    same = (s // NEW) == (t // NEW)
    dup = lambda m: np.concatenate([m, m], 0).astype(np.float32)
    put("ident", np.eye(P))
    put("head_mean", np.kron(np.eye(2), np.full((64, 64), 1 / 64)))
    put("all_mean", np.full((P, P), 1 / P))
    put("iota", np.tile(np.arange(P), (P, 1)))
    put("id64", dup(np.eye(64)))
    put("U_p", dup(s <= t)); put("SU_p", dup(s > t)); put("SUt_p", dup(s < t))
    put("U_s", dup((s <= t) & same)); put("SU_s", dup((s > t) & same)); put("SUt_s", dup((s < t) & same))
    lev = [((s // (2 * b)) == (t // (2 * b))) & (s % (2 * b) >= b) & (t % (2 * b) < b) for b in (1, 2, 4, 8, 16, 32)]
    put("lev", np.concatenate([dup(m) for m in lev], 1))
    put("seq_of", dup((i[:, None] // NEW) == np.arange(8)[None, :]))
    put("ones", 1.0)
    row = np.arange(P)
    put("is_c0", ((row // 8) % 2 == 0)[:, None]); put("is_c1", ((row // 8) % 2 == 1)[:, None])
    dist = 511 - np.arange(REL)
    n = np.maximum(dist, 0)
    nf = np.maximum(n, 1).astype(np.float32)
    big = 16 + (np.log(nf / np.float32(16)) / np.float32(math.log(8)) * np.float32(16)).astype(np.int32)
    bucket = np.where(n < 16, n, np.minimum(big, 31))
    buckets = ((np.arange(BUCKETS)[:, None] == bucket[None]) & (dist >= 0)[None]).astype(np.float32)
    future = np.where(dist < 0, NEG, 0.0).astype(np.float32)[None].repeat(P, 0)
    return c, buckets, future


@contextmanager
def stage(nc, *names):
    with ExitStack() as ctx:
        sems = [ctx.enter_context(nc.semaphore(n)) for n in names]
        with nc.Block() as block:
            yield (block, *sems)
        for s in sems:
            nc.gpsimd.sem_clear(s)
        nc.all_engine_barrier()


class Steps:

    def __init__(self, eng, sem):
        self.eng, self.sem, self.n = eng, sem, 0

    def did(self, ins):
        self.n += 1
        ins.then_inc(self.sem, 1)

    def settle(self):
        self.eng.wait_ge(self.sem, self.n)

    def link(self, ins):
        self.did(ins)
        self.settle()


def split_products(pe, out, terms):
    for n, ((lhi, llo), (rhi, rlo)) in enumerate(terms):
        pe.matmul(out, lhi, rhi, start=(n == 0), stop=False)
        pe.matmul(out, lhi, rlo, start=False, stop=False)
        last = pe.matmul(out, llo, rhi, start=False, stop=(n == len(terms) - 1))
    return last


def bc(ap, axis, n):
    shape = list(ap.shape)
    shape.insert(axis, n)
    return ap.unsqueeze(axis).broadcast_to(shape)


def trunk(nc, t):
    ctx = ExitStack()
    with ctx:
        def sb(name, shape, dt=F32):
            return ctx.enter_context(nc.sbuf_tensor(name, shape, dt))

        arena_at = nc.sbuf_base + (-nc.sbuf_base) % 32
        arena = sb("arena", [P, ARENA])
        x_sb = sb("x_sb", [P, TILES, D])
        cst = sb("cst", [P, NCONST])
        cols = sb("cols_sb", [P, NCOL])
        rows = sb("rows_sb", [P, 512])
        bias_p = sb("bias_p", [P, H, 512])
        bias_s = sb("bias_s", [64, PAST + NEW])
        bias_own = sb("bias_own", [64, NSEQ, SAMP])
        work_s = sb("work_s", [64, 2 * (PAST + SAMP)])
        S_sb = sb("S_sb", [P, 256])
        small = sb("small", [P, 736])

        def split_at(name, at, size):
            return nc.alloc_sbuf_tensor_at(name, [P, size], F32R, offset=arena_at + 4 * at)

        x_split = split_at("x_split", X_AT, 2 * XW)
        w_split = split_at("w_split", W_AT, 4 * KC * WCH)
        u_split = split_at("u_split", 4 * SLOT, 4 * D)
        c_split = split_at("c_split", 8 * SLOT, 4 * SLOT)
        ps = ctx.enter_context(nc.psum_tensor("ps", [P, 8, 512], F32))

        def C(name, i=None):
            o, n = CONST[name]
            return cst[:, o:o + n] if i is None else cst[:, o + i * 64:o + (i + 1) * 64]

        def col(name, i=0, p=slice(0, P)):
            o, _ = COLS[name]
            return cols[p, o + i:o + i + 1]

        def slot(i, n=1):
            return arena[:, i * SLOT:(i + n) * SLOT]

        def ch(i):
            return slot(i).rearrange("p (j t) -> p j t", j=2)

        def tm(i):
            return slot(i).rearrange("p (c j t) -> p c j t", c=NCH, j=2)

        small_at = [0]

        def sm(n):
            small_at[0] += n
            assert small_at[0] <= 736
            return small[:, small_at[0] - n:small_at[0]]

        cat = slot(0, 4).rearrange("p (c t) -> p c t", c=KC)
        z_ch = ch(4)
        hA = slot(5, 5)
        hAp = hA[:, 0:8 * 513].rearrange("p (c t) -> p c t", c=8)
        hAs = hA[:, 8 * 513:8 * 513 + 576].rearrange("p (c b t) -> p c b t", c=8, b=8)
        hB = slot(10, 4)
        hBp = hB[:, 0:6 * 515].rearrange("p (c t) -> p c t", c=6)
        hBs = hB[:, 6 * 515:6 * 515 + 528].rearrange("p (c b t) -> p c b t", c=6, b=8)
        hC = slot(14, 7)[:, 0:TILES * 1536].rearrange("p (i n) -> p i n", i=TILES)
        def x_part(h):
            return x_split[:, h * XW:h * XW + KC * TOK].rearrange("p (k t) -> p k t", k=KC)

        def x_tile(k, i):
            return tuple(x_split[:, h * XW + k * TOK + i * P:h * XW + k * TOK + (i + 1) * P] for h in range(2))

        def w_part(s, h):
            return w_split[:, (2 * s + h) * KC * WCH:(2 * s + h + 1) * KC * WCH].rearrange("p (k n) -> p k n", k=KC)

        def w_raw(i):
            return slot(i, 4)[:, 0:2 * KC * WCH].rearrange("p (s k n) -> p s k n", s=2, k=KC)

        beta_g = sm(36).rearrange("p (k c j) -> p k c j", k=2, c=NCH)
        lam = sm(8)
        stat = sm(64)
        GL = sm(36).rearrange("p (m c j) -> p m c j", m=2, c=NCH)
        GLs = sm(32).rearrange("p (m j b) -> p m j b", m=2, j=2)
        gcol = sm(108).rearrange("p (k c j) -> p k c j", k=6, c=NCH)
        tails_o = sm(234)
        tails_i = sm(208)

        RP = REL + 1
        relb = slot(0)[0:32, 0:4]
        relb_bc = slot(0)[0:32, 128:128 + H * P].rearrange("b (h p) -> b h p", h=H)
        onehot = slot(1)[0:32, 0:REL]
        fut = slot(2)[:, 0:REL]
        r4 = slot(3, 3)[:, 0:H * RP].rearrange("p (h n) -> p h n", h=H)
        with stage(nc, "consts_in", "x_in", "steps", "rel_copied", "rel_mm", "rel_row", "rel_out", "rel_in", "own_ready") as (
                block, consts_in, x_in, steps_, rel_copied, rel_mm, rel_row, rel_out, rel_in, own_ready):
            rd = t["rel_scratch"]

            @block.sync
            def _(sp):
                sp.dma_start(relb, t["rel_bias"]).then_inc(consts_in, 16)
                sp.dma_start(onehot, t["buckets"]).then_inc(consts_in, 16)
                sp.dma_start(fut, t["future"]).then_inc(consts_in, 16)
                sp.dma_start(cst[:, :], t["consts"]).then_inc(consts_in, 16)
                sp.dma_start(x_sb[:, 0:4, :], t["x_prompt"].rearrange("(i p) d -> p i d", p=P)).then_inc(x_in, 16)
                sp.dma_start(x_sb[0:64, 4, :], t["x_sample"]).then_inc(x_in, 16)
                sp.wait_ge(rel_row, 2 * H)
                sp.dma_start(rd, r4.rearrange("p h n -> p (h n)")).then_inc(rel_out, 16)
                sp.wait_ge(rel_out, 16)
                for h in range(H):
                    sp.dma_start(bias_p[:, h, :], bass.AP(rd.tensor, h * RP + 127, [[H * RP - 1, P], [1, 512]])).then_inc(rel_in, 16)
                    for c in range(2):
                        r = h * 16 + c * 8
                        sp.dma_start(bias_s[r:r + 8, :], bass.AP(rd.tensor, h * RP + 255, [[H * RP - 1, 8], [1, PAST + NEW]])).then_inc(rel_in, 16)
                sp.wait_ge(rel_in, 12 * 16)
                sp.wait_ge(x_in, 32)

            @block.vector
            def _(dve):
                st = Steps(dve, steps_)
                st.did(dve.memset(x_sb[64:P, 4, :], 0.0))
                st.did(dve.memset(r4[:, :, REL:RP], 0.0))
                st.did(dve.memset(bias_own[:, :, :], NEG))
                st.settle()
                dve.wait_ge(consts_in, 64)
                dve.tensor_copy(relb_bc, bc(relb, 2, P)).then_inc(rel_copied, 1)
                for h in range(H):
                    dve.wait_ge(rel_mm, h + 1)
                    dve.tensor_tensor(r4[:, h, 0:512], ps[:, 2 * h, :], fut[:, 0:512], ALU.add).then_inc(rel_row, 1)
                    dve.tensor_tensor(r4[:, h, 512:REL], ps[:, 2 * h + 1, 0:REL - 512], fut[:, 512:REL], ALU.add).then_inc(rel_row, 1)
                dve.wait_ge(rel_in, 12 * 16)
                for b in range(NSEQ):
                    last = dve.tensor_copy(bias_own[:, b, b * NEW:(b + 1) * NEW], bias_s[:, PAST:PAST + NEW])
                last.then_inc(own_ready, 1)

            @block.tensor
            def _(pe):
                pe.wait_ge(consts_in, 64)
                pe.wait_ge(rel_copied, 1)
                for h in range(H):
                    pe.matmul(ps[:, 2 * h, :], relb_bc[:, h], onehot[:, 0:512], start=True, stop=True)
                    pe.matmul(ps[:, 2 * h + 1, 0:REL - 512], relb_bc[:, h], onehot[:, 512:REL], start=True, stop=True).then_inc(rel_mm, 1)

        with nc.Fori(0, DEPTH) as layer:
            L = bass.ds(layer, 1)

            def at(name):
                a = t[name][L]
                n = len(a.shape)
                names = " ".join("abcdefg"[:n - 1])
                return a.rearrange(f"o {names} -> (o a) {names[2:]}" if n > 2 else f"o {names} -> o {names}")

            def hi_of(act, g, raw, w_in, hi_ready, width=WCH):
                s = g % 2
                act.wait_ge(w_in[s], 16 * (g // 2 + 1))
                act.copy(w_part(s, 0)[:, :, 0:width], raw[:, s, :, 0:width]).then_inc(hi_ready, 1)

            def lo_of(pool, g, raw, hi_ready, lo_ready, width=WCH):
                s = g % 2
                pool.wait_ge(hi_ready, g + 1)
                pool.tensor_tensor(w_part(s, 1)[:, :, 0:width], raw[:, s, :, 0:width], w_part(s, 0)[:, :, 0:width].bitcast(F32),
                                   ALU.subtract).then_inc(lo_ready, 1)

            def norm_transposed(gain, weights):
                raw = w_raw(0)
                junk = slot(9)[:, 0:D]
                xn = slot(4, 5).rearrange("p (i n) -> p i n", n=SLOT)[:, :, 0:D]
                xg = slot(10, 5)[:, 0:10 * 512].rearrange("p (u k t) -> p u k t", u=10, k=4)
                with stage(nc, "par_in", "ssq_ready", "root_ready", "inv_steps", "xn_ready", "tr_done", "xg_ready", "hi_ready", "lo_ready",
                           "w_in0", "w_in1", "w_hi", "w_lo") as (
                        block, par_in, ssq_ready, root_ready, inv_steps, xn_ready, tr_done, xg_ready, hi_ready, lo_ready,
                        w_in0, w_in1, w_hi, w_lo):
                    w_in = (w_in0, w_in1)

                    def part(h, u):
                        i, hf = u // 2, u % 2
                        return x_part(h)[:, 4 * hf:4 * hf + 4, i * P:min(TOK, (i + 1) * P)]

                    def gained(u):
                        return xg[:, u, :, 0:min(P, TOK - (u // 2) * P)]

                    @block.sync
                    def _(sp):
                        sp.dma_start(cols[:, :], at("cols")).then_inc(par_in, 16)
                        sp.dma_start(rows[:, :], t["rows"][L].broadcast_to([P, 512])).then_inc(par_in, 16)
                        for g in range(2):
                            sp.dma_start(raw[:, g], weights[:, :, g * WCH:(g + 1) * WCH]).then_inc(w_in[g], 16)

                    @block.scalar
                    def _(act):
                        sq = Steps(act, ssq_ready)
                        for i in range(TILES):
                            sq.link(act.activation(junk, x_sb[:, i, :], ACT.Square, accum_out=stat[:, i:i + 1]))
                        act.wait_ge(inv_steps, 1)
                        act.activation(stat[:, 16:21], stat[:, 8:13], ACT.Sqrt).then_inc(root_ready, 1)
                        for g in range(2):
                            hi_of(act, g, raw, w_in, w_hi)
                        for u in range(TILES * 2):
                            act.wait_ge(xg_ready, u + 1)
                            act.copy(part(0, u), gained(u)).then_inc(hi_ready, 1)

                    @block.gpsimd
                    def _(pool):
                        for h in range(2):
                            pool.tensor_copy(x_split[:, h * XW + KC * TOK:(h + 1) * XW], C("ones")).then_inc(lo_ready, 1)
                        for g in range(2):
                            lo_of(pool, g, raw, w_hi, w_lo)

                    @block.vector
                    def _(dve):
                        st = Steps(dve, inv_steps)
                        dve.wait_ge(ssq_ready, TILES)
                        st.link(dve.tensor_scalar(stat[:, 8:13], stat[:, 0:5], 1.0 / D, EPS, ALU.mult, ALU.add))
                        dve.wait_ge(root_ready, 1)
                        st.link(dve.reciprocal(stat[:, 24:29], stat[:, 16:21]))
                        for i in range(TILES):
                            dve.tensor_scalar(xn[:, i, :], x_sb[:, i, :], stat[:, 24 + i:25 + i], None, ALU.mult).then_inc(xn_ready, 1)
                        dve.wait_ge(par_in, 32)
                        o, _ = COLS[gain]
                        for u in range(TILES * 2 + 2):
                            if u < TILES * 2:
                                w, hf = min(P, TOK - (u // 2) * P), u % 2
                                dve.wait_ge(tr_done, u + 1)
                                dve.tensor_tensor(gained(u), ps[:, u % 8, :].rearrange("p (k t) -> p k t", k=4)[:, :, 0:w],
                                                  bc(cols[:, o + 4 * hf:o + 4 * hf + 4], 2, w), ALU.mult).then_inc(xg_ready, 1)
                            if u >= 2:
                                v = u - 2
                                dve.wait_ge(hi_ready, v + 1)
                                dve.tensor_tensor(part(1, v), gained(v), part(0, v).bitcast(F32), ALU.subtract).then_inc(lo_ready, 1)

                    @block.tensor
                    def _(pe):
                        for u in range(TILES * 2):
                            i, hf = u // 2, u % 2
                            pe.wait_ge(xn_ready, i + 1)
                            if u >= 8:
                                pe.wait_ge(xg_ready, u - 7)
                            for k in range(4):
                                kc = hf * 4 + k
                                last = pe.transpose(ps[:, u % 8, k * P:(k + 1) * P], xn[:, i, kc * P:(kc + 1) * P], C("ident"))
                            last.then_inc(tr_done, 1)

            w_in_view = at("w_in").rearrange("(k p) n -> p k n", p=P)
            norm_transposed("mix_g", w_in_view)

            groups = ([("A", c, WCH) for c in range(0, A_COLS, WCH)] + [("ab", COL_AB, P)]
                      + [("B", c, WCH) for c in range(COL_B, COL_AB, WCH)] + [("z", COL_Z, WCH)]
                      + [("C", c, WCH) for c in range(COL_C, COL_C + 3 * C_W, WCH)])
            units = []
            for g, (kind, c0, w) in enumerate(groups):
                if kind == "C":
                    units += [(g, kind, c0, i) for i in range(TILES)]
                else:
                    units += [(g, kind, c0 + m * P, part) for m in range(w // P) for part in (0, 1)]
            rows_u = len(units)
            units += [(len(groups) - 1, "ab_rows", COL_AB, 0)]
            abT = work_s[0:8, 0:TOK]
            raw = w_raw(0)
            group_last = [max(u for u, un in enumerate(units) if un[0] == g) for g in range(len(groups))]
            with stage(nc, "w_in0", "w_in1", "hi_ready", "lo_ready", "tails_in", "proj_done", "out_act", "out_dve", "tails_steps",
                       "tail_ready", "tail_out") as (block, w_s0, w_s1, hi_ready, lo_ready, tails_in, proj_done, out_act, out_dve,
                                                     tails_steps, tail_ready, tail_out):
                w_sem = [w_s0, w_s1]
                @block.sync
                def _(sp):
                    sp.dma_start(tails_i, at("tails")).then_inc(tails_in, 16)
                    for g, (kind, c0, w) in enumerate(groups):
                        if g < 2:
                            sp.sem_inc(w_sem[g], 16)
                        else:
                            sp.wait_ge(lo_ready, g - 1)
                            sp.dma_start(raw[:, g % 2, :, 0:w], w_in_view[:, :, c0:c0 + w]).then_inc(w_sem[g % 2], 16)
                    sp.wait_ge(tail_ready, 1)
                    sp.dma_start(at("o_tails"), tails_o).then_inc(tail_out, 16)
                    sp.wait_ge(tail_out, 16)

                def copies(u):
                    g, kind, c0, part = units[u]
                    b = ps[:, u % 8, :]
                    if kind == "C":
                        return [(hC[:, part, c0 - COL_C:c0 - COL_C + WCH], b[:, 0:WCH])]
                    if kind == "ab":
                        return [(abT[:, part * HN:(part + 1) * HN], b[0:8, 0:HN])]
                    if kind == "ab_rows":
                        v = b[:, 0:NCH * 8].rearrange("p (c k j h) -> p h k c j", c=NCH, k=2, j=2)
                        return [(beta_g[64 * hf:64 * hf + 64, k], v[64 * hf:64 * hf + 64, hf, k]) for hf in range(2) for k in range(2)]
                    if kind == "z":
                        j = (c0 - COL_Z) // P
                        return [(z_ch[:, j, part * HN:(part + 1) * HN], b[:, 0:HN])]
                    base, dp, ds_, lead = (0, hAp, hAs, 1) if kind == "A" else (COL_B, hBp, hBs, 3)
                    c = (c0 - base) // P
                    if part == 0:
                        return [(dp[:, c, lead:lead + HN], b[:, 0:HN])]
                    return [(dp[:, c, lead + HN:lead + SEQ], b[:, 0:SEQ - HN]),
                            (ds_[:, c, :, lead:lead + NEW], b[:, SEQ - HN:HN].rearrange("p (b t) -> p b t", b=NSEQ))]

                @block.scalar
                def _(act):
                    act.sem_inc(hi_ready, 2)
                    for u in range(len(units)):
                        g = units[u][0]
                        if u and units[u - 1][0] < g < len(groups) - 1:
                            act.wait_ge(proj_done, group_last[g - 1] + 1)
                            hi_of(act, g + 1, raw, w_sem, hi_ready, groups[g + 1][2])
                        if u % 2 == 0:
                            act.wait_ge(proj_done, u + 1)
                            for d, s in copies(u):
                                last = act.copy(d, s)
                            last.then_inc(out_act, 1)

                @block.gpsimd
                def _(pool):
                    pool.sem_inc(lo_ready, 2)
                    for g in range(2, len(groups)):
                        lo_of(pool, g, raw, hi_ready, lo_ready, groups[g][2])

                @block.vector
                def _(dve):
                    st = Steps(dve, tails_steps)
                    st.did(dve.memset(hAp[:, :, 0:1], 0.0))
                    st.did(dve.memset(hBp[:, :, 0:3], 0.0))
                    dve.wait_ge(tails_in, 16)
                    st.did(dve.tensor_copy(hAs[:, :, :, 0:1], tails_i[:, 0:64].rearrange("p (c b o) -> p c b o", c=8, b=8)))
                    st.did(dve.tensor_copy(hBs[:, :, :, 0:3], tails_i[:, 64:208].rearrange("p (c b k) -> p c b k", c=6, b=8)))
                    for u in range(1, len(units), 2):
                        dve.wait_ge(proj_done, u + 1)
                        for d, s in copies(u):
                            last = dve.tensor_copy(d, s)
                        last.then_inc(out_dve, 1)
                    dve.wait_ge(out_act, (len(units) + 1) // 2)
                    dve.wait_ge(out_dve, len(units) // 2)
                    st.did(dve.tensor_copy(tails_o[:, 0:8].unsqueeze(2), hAp[:, :, SEQ:SEQ + 1]))
                    st.did(dve.tensor_copy(tails_o[:, 8:72].rearrange("p (c b o) -> p c b o", c=8, b=8), hAs[:, :, :, NEW:NEW + 1]))
                    st.did(dve.tensor_copy(tails_o[:, 72:90].rearrange("p (c k) -> p c k", c=6), hBp[:, :, SEQ:SEQ + 3]))
                    st.link(dve.tensor_copy(tails_o[:, 90:234].rearrange("p (c b k) -> p c b k", c=6, b=8), hBs[:, :, :, NEW:NEW + 3]))
                    dve.sem_inc(tail_ready, 1)

                @block.tensor
                def _(pe):
                    for u, (g, kind, c0, part) in enumerate(units):
                        wh, wl = w_part(g % 2, 0), w_part(g % 2, 1)
                        if u == 0 or units[u - 1][0] != g:
                            pe.wait_ge(lo_ready, g + 1)
                        if u >= 8:
                            pe.wait_ge(out_dve if u % 2 else out_act, (u - 8) // 2 + 1)
                        m = c0 - groups[g][1]
                        if kind == "ab_rows":
                            for c in range(NCH):
                                for hf in range(2):
                                    last = pe.matmul(ps[64 * hf:64 * hf + 64, u % 8, c * 8:c * 8 + 8], abT[:, c * CH:(c + 1) * CH],
                                                     C("ident")[0:8, 0:8], start=True, stop=True)
                        elif kind == "C":
                            last = split_products(pe, ps[:, u % 8, 0:WCH], [(x_tile(k, part), (wh[:, k, :], wl[:, k, :])) for k in range(KC)])
                        else:
                            tq = slice(part * HN, (part + 1) * HN)
                            last = split_products(pe, ps[:, u % 8, 0:HN], [((wh[:, k, m:m + P], wl[:, k, m:m + P]),
                                                                           (x_part(0)[:, k, tq], x_part(1)[:, k, tq]))
                                                                          for k in range(KC)])
                        last.then_inc(proj_done, 1)

            QT = slot(21, 5)[:, 0:2560].rearrange("p (h t) -> p h t", h=H)
            KT = slot(21, 5)[:, 2560:5120].rearrange("p (h t) -> p h t", h=H)
            room = slot(26, 8)
            sq2 = room[:, 0:2048].rearrange("p (s n) -> p s n", s=2)
            ssq = room[:, 2048:2128].rearrange("p (i n) -> p i n", i=TILES)
            root = room[:, 2128:2208]
            rinv = room[:, 2208:2288].rearrange("p (i n) -> p i n", i=TILES)
            lprod = room[:, 2304:2432].rearrange("p (a n) -> p a n", a=2)
            coef = lam[0:64, 4:5]
            with stage(nc, "sq_ready", "ssq_steps", "mean_ready", "root_ready", "lam_sum", "lam_exp", "qk_ready", "t_done", "q_out",
                       "k_out", "rows_out") as (block, sq_ready, ssq_steps, mean_ready, root_ready, lam_sum, lam_exp, qk_ready,
                                                t_done, q_out, k_out, rows_out):
                @block.scalar
                def _(act):
                    for i in range(TILES):
                        if i >= 2:
                            act.wait_ge(ssq_steps, i - 1)
                        act.activation(sq2[:, i % 2, :], hC[:, i, 0:1024], ACT.Square).then_inc(sq_ready, 1)
                    act.wait_ge(mean_ready, 1)
                    act.activation(root, root, ACT.Sqrt).then_inc(root_ready, 1)
                    act.wait_ge(lam_sum, 1)
                    act.activation(lam[:, 0:2], lam[:, 0:2], ACT.Exp).then_inc(lam_exp, 1)
                    for i in range(TILES):
                        act.wait_ge(t_done, 2 * i + 1)
                        act.copy(QT[:, :, i * P:(i + 1) * P], ps[:, (2 * i) % 8, :].rearrange("p (h t) -> p h t", h=H)).then_inc(q_out, 1)

                @block.vector
                def _(dve):
                    st = Steps(dve, ssq_steps)
                    for i in range(TILES):
                        dve.wait_ge(sq_ready, i + 1)
                        st.did(dve.tensor_reduce(ssq[:, i, :], sq2[:, i % 2, :].rearrange("p (g n) -> p g n", n=HD), AX.X, ALU.add))
                    st.settle()
                    st.did(dve.tensor_tensor(lprod, rows[:, 256:512].rearrange("p (a b n) -> p b a n", a=2, b=2)[:, 0],
                                             rows[:, 256:512].rearrange("p (a b n) -> p b a n", a=2, b=2)[:, 1], ALU.mult))
                    dve.tensor_scalar(root.rearrange("p (i n) -> p i n", i=TILES), ssq, 1.0 / HD, EPS, ALU.mult, ALU.add).then_inc(mean_ready, 1)
                    st.settle()
                    dve.tensor_reduce(lam[:, 0:2], lprod, AX.X, ALU.add).then_inc(lam_sum, 1)
                    dve.wait_ge(root_ready, 1)
                    st.link(dve.reciprocal(rinv.rearrange("p i n -> p (i n)"), root))
                    for i in range(TILES):
                        v = hC[:, i, 0:1024].rearrange("p (g n) -> p g n", n=HD)
                        st.link(dve.tensor_tensor(v, v, bc(rinv[:, i, :], 2, HD), ALU.mult))
                        v = hC[:, i, 0:1024].rearrange("p (a h n) -> p a h n", a=2, h=H)
                        g = bc(rows[:, 0:256].rearrange("p (a n) -> p a n", a=2), 2, H)
                        dve.tensor_tensor(v, v, g, ALU.mult).then_inc(qk_ready, 1)
                    dve.wait_ge(lam_exp, 1)
                    st.link(dve.tensor_tensor(lam[:, 2:3], lam[:, 0:1], lam[:, 1:2], ALU.subtract))
                    st.link(dve.tensor_tensor(lam[:, 2:3], lam[:, 2:3], col("lam_init"), ALU.add))
                    st.link(dve.tensor_scalar(lam[:, 3:4], lam[:, 2:3], -1.0, None, ALU.mult))
                    st.link(dve.scalar_tensor_tensor(coef, C("is_c1")[0:64], lam[0:64, 3:4], C("is_c0")[0:64], ALU.mult, ALU.add))
                    for i in range(TILES):
                        dve.wait_ge(t_done, 2 * i + 2)
                        dve.tensor_copy(KT[:, :, i * P:(i + 1) * P], ps[:, (2 * i + 1) % 8, :].rearrange("p (h t) -> p h t", h=H)).then_inc(k_out, 1)

                @block.tensor
                def _(pe):
                    for i in range(TILES):
                        pe.wait_ge(qk_ready, i + 1)
                        if i == 4:
                            pe.wait_ge(q_out, 1)
                            pe.wait_ge(k_out, 1)
                        for a in range(2):
                            for h in range(H):
                                last = pe.transpose(ps[:, (2 * i + a) % 8, h * P:(h + 1) * P], hC[:, i, a * C_W + h * P:a * C_W + (h + 1) * P], C("ident"))
                            last.then_inc(t_done, 1)

                @block.sync
                def _(sp):
                    sp.dma_start(at("o_vp").rearrange("(i p) n -> p i n", p=P), hC[:, 0:4, 1024:1536]).then_inc(rows_out, 16)
                    sp.dma_start(at("o_vs"), hC[0:SAMP, 4, 1024:1536]).then_inc(rows_out, 16)
                    sp.wait_ge(qk_ready, TILES)
                    sp.dma_start(at("o_kp").rearrange("(i p) n -> p i n", p=P), hC[:, 0:4, 512:1024]).then_inc(rows_out, 16)
                    sp.dma_start(at("o_ks"), hC[0:SAMP, 4, 512:1024]).then_inc(rows_out, 16)
                    sp.wait_ge(rows_out, 64)

            Sb = room[:, 0:2048].rearrange("p (s c k) -> p s c k", s=2, c=2)
            pd = room[:, 2048:3072].rearrange("p (s k) -> p s k", s=2)
            PT = room[:, 3072:4096].rearrange("p (s k) -> p s k", s=2)
            st4 = room[:, 4096:4096 + 16].rearrange("p (s n) -> p s n", s=2)
            au = [(i, h) for i in range(4) for h in range(H)]
            OC = cat[:, 4:8, :]
            with stage(nc, "s_done", "biased", "max_ready", "exp_done", "fin_steps", "pd_ready", "pt_done", "pt_ready", "pv_done", "oc_ready") as (
                    block, s_done, biased, max_ready, exp_done, fin_steps, pd_ready, pt_done, pt_ready, pv_done, oc_ready):
                @block.tensor
                def _(pe):
                    def scores(u):
                        i, h = au[u]
                        if u >= 2:
                            pe.wait_ge(biased, u - 1)
                        for c in range(2):
                            last = pe.matmul(ps[:, 2 * (u % 2) + c, 0:(i + 1) * P], QT[64 * c:64 * c + 64, h, i * P:(i + 1) * P],
                                             KT[64 * c:64 * c + 64, h, 0:(i + 1) * P], start=True, stop=True)
                        last.then_inc(s_done, 1)

                    def turn(u):
                        i, h = au[u]
                        pe.wait_ge(pd_ready, u + 1)
                        if u >= 2:
                            pe.wait_ge(pt_ready, u - 1)
                        for j in range(i + 1):
                            last = pe.transpose(ps[:, 4 + u % 2, j * P:(j + 1) * P], pd[:, u % 2, j * P:(j + 1) * P], C("ident"))
                        last.then_inc(pt_done, 1)

                    def values(u):
                        i, h = au[u]
                        pe.wait_ge(pt_ready, u + 1)
                        if u >= 2:
                            pe.wait_ge(oc_ready, u - 1)
                        for j in range(i + 1):
                            last = pe.matmul(ps[:, 6 + u % 2, 0:P], hC[:, j, 1024 + h * P:1024 + (h + 1) * P], PT[:, u % 2, j * P:(j + 1) * P],
                                             start=(j == 0), stop=(j == i))
                        last.then_inc(pv_done, 1)
                    n = len(au)
                    scores(0)
                    for u in range(n + 2):
                        if u + 1 < n:
                            scores(u + 1)
                        if u >= 2:
                            values(u - 2)
                        if 1 <= u <= n:
                            turn(u - 1)

                @block.scalar
                def _(act):
                    n = len(au)
                    for u in range(n + 2):
                        if u < n:
                            k, s, m = (au[u][0] + 1) * P, Sb[:, u % 2], st4[:, u % 2]
                            act.wait_ge(max_ready, u + 1)
                            for c in range(2):
                                last = act.activation(s[:, c, 0:k], s[:, c, 0:k], ACT.Exp, bias=m[:, c:c + 1], accum_out=m[:, 2 + c:3 + c])
                            last.then_inc(exp_done, 1)
                        if 1 <= u <= n:
                            v = u - 1
                            k = (au[v][0] + 1) * P
                            act.wait_ge(pt_done, v + 1)
                            if v >= 2:
                                act.wait_ge(pv_done, v - 1)
                            act.copy(PT[:, v % 2, 0:k], ps[:, 4 + v % 2, 0:k]).then_inc(pt_ready, 1)
                        if u >= 2:
                            v = u - 2
                            i, h = au[v]
                            act.wait_ge(pv_done, v + 1)
                            act.copy(OC[:, h, i * P:(i + 1) * P], ps[:, 6 + v % 2, 0:P]).then_inc(oc_ready, 1)

                @block.vector
                def _(dve):
                    st = Steps(dve, fin_steps)

                    def finish(u):
                        i, h = au[u]
                        k, s, m = (i + 1) * P, Sb[:, u % 2], st4[:, u % 2]
                        dve.wait_ge(exp_done, u + 1)
                        st.link(dve.reciprocal(m[:, 4:6], m[:, 2:4]))
                        st.link(dve.tensor_tensor(m[:, 5:6], m[:, 5:6], lam[:, 3:4], ALU.mult))
                        if u >= 2:
                            dve.wait_ge(pt_done, u - 1)
                        st.link(dve.tensor_scalar(pd[:, u % 2, 0:k], s[:, 0, 0:k], m[:, 4:5], None, ALU.mult))
                        dve.scalar_tensor_tensor(pd[:, u % 2, 0:k], s[:, 1, 0:k], m[:, 5:6], pd[:, u % 2, 0:k],
                                                 ALU.mult, ALU.add).then_inc(pd_ready, 1)

                    for u, (i, h) in enumerate(au):
                        k, s, m = (i + 1) * P, Sb[:, u % 2], st4[:, u % 2]
                        dve.wait_ge(s_done, u + 1)
                        if u >= 2:
                            dve.wait_ge(pd_ready, u - 1)
                        dve.scalar_tensor_tensor(s[:, :, 0:k], ps[:, 2 * (u % 2):2 * (u % 2) + 2, 0:k], HD ** -0.5,
                                                 bc(bias_p[:, h, 512 - k:512], 1, 2), ALU.mult, ALU.add).then_inc(biased, 1)
                        dve.wait_ge(biased, u + 1)
                        dve.tensor_reduce(m[:, 0:2], s[:, :, 0:k], AX.X, ALU.max, negate=True).then_inc(max_ready, 1)
                        if u >= 1:
                            finish(u - 1)
                    finish(len(au) - 1)

            QX = room[:, 0:2048].rearrange("p (b h r) -> p b h r", b=NSEQ, h=H)
            NPG = 4
            pages = [a[:, 0:2048].rearrange("p (m j n) -> p m j n", m=2, j=PAGES)
                     for a in (room[:, 2048:4096], room[:, 4096:6144], slot(0, 2), arena[:, 34 * SLOT:ARENA])]
            KTb = room[:, 6144:8192].rearrange("p (s h t) -> p s h t", s=2, h=H)
            W_ = PAST + SAMP
            Ss = work_s[:, 0:2 * W_].rearrange("p (s k) -> p s k", s=2)
            PTa = room[:, 8192:8384].rearrange("p (j r) -> p j r", j=3)
            PTs = room[:, 8384:8384 + 192].rearrange("p (s j h q) -> p s j h q", s=2, j=3, h=H)
            ms = stat[0:64, 32:48].rearrange("p (s n) -> p s n", s=2)
            with stage(nc, *(f"{m}_in{n}" for m in "kv" for n in range(NPG)), "qx_steps", "kt_done", "kt_a", "kt_v", "s_done", "biased", "max_ready", "exp_done",
                       "p_steps", "p_ready", "pt_done", "pta_steps", "pt_ready", "pv_done", "oc_ready", "pid_in") as (
                    block, k_in0, k_in1, k_in2, k_in3, v_in0, v_in1, v_in2, v_in3, qx_steps, kt_done, kt_a, kt_v, s_done, biased, max_ready, exp_done,
                    p_steps, p_ready, pt_done, pta_steps, pt_ready, pv_done, oc_ready, pid_in):
                k_in, v_in = (k_in0, k_in1, k_in2, k_in3), (v_in0, v_in1, v_in2, v_in3)

                @block.sync
                def _(sp):
                    def load(b, m, page_ids, arrived):
                        for j, pid in enumerate(page_ids):
                            src = t[("cache_k", "cache_v")[m]][bass.ds(pid, 1), L].rearrange("o a t h n -> (o a t) (h n)")
                            sp.dma_start(pages[b % NPG][:, m, j, :], src).then_inc(arrived[b % NPG], 16)
                    for b in range(NSEQ + 1):
                        if b < NSEQ:
                            page_ids = [sp.value_load(t["page_table"][b:b + 1, j:j + 1], min_val=0, max_val=t["cache_k"].shape[0] - 1)
                                        for j in range(PAGES)]
                            if b >= NPG:
                                sp.wait_ge(kt_done, 2 * (b - NPG + 1))
                            load(b, 0, page_ids, k_in)
                        if b >= 1:
                            if b - 1 >= NPG:
                                sp.wait_ge(pv_done, b - NPG)
                            load(b - 1, 1, last_ids, v_in)
                        last_ids = page_ids

                @block.tensor
                def _(pe):
                    def keys(b):
                        pe.wait_ge(k_in[b % NPG], 32 * (b // NPG + 1))
                        for j in range(PAGES):
                            if b >= 1:
                                pe.wait_ge(kt_v if j else kt_a, b)
                            for h in range(H):
                                last = pe.transpose(ps[:, j, h * P:(h + 1) * P], pages[b % NPG][:, 0, j, h * P:(h + 1) * P], C("ident"))
                            last.then_inc(kt_done, 1)

                    def scores(b):
                        pe.wait_ge(kt_a, b + 1)
                        pe.wait_ge(kt_v, b + 1)
                        if b == 0:
                            pe.wait_ge(qx_steps, 9)
                        if b >= 2:
                            pe.wait_ge(biased, 2 * (b - 1))
                        for h in range(H):
                            pe.matmul(ps[0:64, 2 + b % 2, 0:PAST], QX[:, b, h, :], KTb[:, b % 2, h, :], start=(h == 0), stop=(h == 3))
                        for h in range(H):
                            last = pe.matmul(ps[0:64, 2 + b % 2, PAST:W_], QX[:, b, h, :], KT[:, h, SEQ:TOK], start=(h == 0), stop=(h == 3))
                        last.then_inc(s_done, 1)

                    def turn(b):
                        pe.wait_ge(p_ready, b + 1)
                        if b >= 2:
                            pe.wait_ge(pt_ready, b - 1)
                        for j in range(3):
                            k = min(P, W_ - j * P)
                            last = pe.transpose(ps[0:k, 4 + b % 2, j * 64:j * 64 + 64], Ss[:, b % 2, j * P:j * P + k], C("ident")[0:64, 0:64])
                        last.then_inc(pt_done, 1)

                    def values(b):
                        pe.wait_ge(v_in[b % NPG], 32 * (b // NPG + 1))
                        pe.wait_ge(pt_ready, b + 1)
                        for h in range(H):
                            o = ps[:, 6, h * 64 + b * NEW:h * 64 + (b + 1) * NEW]
                            for j in range(PAGES):
                                pe.matmul(o, pages[b % NPG][:, 1, j, h * P:(h + 1) * P], PTs[:, b % 2, j, h, :], start=(j == 0), stop=False)
                            last = pe.matmul(o, hC[0:64, 4, 1024 + h * P:1024 + (h + 1) * P], PTs[0:64, b % 2, 2, h, :], start=False, stop=True)
                        last.then_inc(pv_done, 1)
                    for b in range(NSEQ + 3):
                        if b < NSEQ:
                            keys(b)
                        if 1 <= b <= NSEQ:
                            scores(b - 1)
                        if 2 <= b <= NSEQ + 1:
                            turn(b - 2)
                        if b >= 3:
                            values(b - 3)

                @block.scalar
                def _(act):
                    for b in range(NSEQ + 1):
                        if b < NSEQ:
                            act.wait_ge(kt_done, 2 * b + 1)
                            if b >= 2:
                                act.wait_ge(s_done, b - 1)
                            act.copy(KTb[:, b % 2, :, 0:P], ps[:, 0, :].rearrange("p (h t) -> p h t", h=H)).then_inc(kt_a, 1)
                        if b >= 1:
                            u = b - 1
                            act.wait_ge(max_ready, u + 1)
                            act.activation(Ss[:, u % 2, :], Ss[:, u % 2, :], ACT.Exp, bias=ms[:, u % 2, 0:1], accum_out=ms[:, u % 2, 1:2]).then_inc(exp_done, 1)
                    act.wait_ge(pv_done, NSEQ)
                    act.copy(OC[:, :, SEQ:TOK], ps[:, 6, 0:256].rearrange("p (h t) -> p h t", h=H)).then_inc(oc_ready, 1)

                @block.vector
                def _(dve):
                    q = Steps(dve, qx_steps)
                    q.link(dve.memset(QX, 0.0))
                    for h in range(H):
                        for c in range(2):
                            p = slice(64 * c, 64 * c + 64)
                            q.did(dve.tensor_copy(QX[p, :, h, h * 16 + c * 8:h * 16 + c * 8 + 8],
                                                  QT[p, h, SEQ:TOK].rearrange("p (b t) -> p b t", b=NSEQ)))
                    st = Steps(dve, p_steps)
                    pt = Steps(dve, pta_steps)

                    def scaled(b):
                        s, m = Ss[:, b % 2], ms[:, b % 2]
                        dve.wait_ge(s_done, b + 1)
                        if b >= 2:
                            dve.wait_ge(pt_done, b - 1)
                        dve.scalar_tensor_tensor(s[:, 0:PAST], ps[0:64, 2 + b % 2, 0:PAST], HD ** -0.5, bias_s[:, 0:PAST],
                                                 ALU.mult, ALU.add).then_inc(biased, 1)
                        dve.scalar_tensor_tensor(s[:, PAST:W_], ps[0:64, 2 + b % 2, PAST:W_], HD ** -0.5, bias_own[:, b, :],
                                                 ALU.mult, ALU.add).then_inc(biased, 1)
                        dve.wait_ge(biased, 2 * b + 2)
                        dve.tensor_reduce(m[:, 0:1], s, AX.X, ALU.max, negate=True).then_inc(max_ready, 1)

                    def weights(b):
                        s, m = Ss[:, b % 2], ms[:, b % 2]
                        dve.wait_ge(exp_done, b + 1)
                        st.link(dve.reciprocal(m[:, 2:3], m[:, 1:2]))
                        st.link(dve.tensor_tensor(m[:, 2:3], m[:, 2:3], coef, ALU.mult))
                        dve.tensor_scalar(s, s, m[:, 2:3], None, ALU.mult).then_inc(p_ready, 1)

                    def differences(b):
                        dve.wait_ge(pt_done, b + 1)
                        if b >= 2:
                            dve.wait_ge(pv_done, b - 1)
                        for p, js in ((slice(0, P), slice(0, 2)), (slice(0, 64), slice(2, 3))):
                            n = js.stop - js.start
                            raw = ps[p, 4 + b % 2, js.start * 64:js.stop * 64]
                            pt.link(dve.tensor_copy(PTa[p, js, :], raw.rearrange("p (j r) -> p j r", j=n)))
                            v = PTa[p, js, :].rearrange("p j (h c q) -> p c j h q", h=H, c=2)
                            for j in range(n):
                                last = dve.tensor_tensor(PTs[p, b % 2, js.start + j], v[:, 0, j], v[:, 1, j], ALU.add)
                                pt.did(last)
                        pt.settle()
                        dve.sem_inc(pt_ready, 1)
                    for b in range(NSEQ + 2):
                        if b < NSEQ:
                            dve.wait_ge(kt_done, 2 * b + 2)
                            if b >= 2:
                                dve.wait_ge(s_done, b - 1)
                            dve.tensor_copy(KTb[:, b % 2, :, P:PAST], ps[:, 1, :].rearrange("p (h t) -> p h t", h=H)).then_inc(kt_v, 1)
                        if b >= 2:
                            weights(b - 2)
                        if 1 <= b <= NSEQ:
                            scaled(b - 1)
                        if b >= 2:
                            differences(b - 2)

            hs = slot(14, 4).rearrange("p (c t) -> p c t", c=8)
            r_, k_, v_, lora = ch(14), ch(15), ch(16), ch(17)
            sig, a_, gate, kkn = ch(18), ch(19), ch(20), ch(21)
            t1, t2, cumA, cumB = ch(22), ch(23), ch(24), ch(25)
            Gd, Gi = ch(26), ch(27)
            Qr, Ar, Kr, Br, yadd = ch(28), ch(29), ch(30), ch(31), ch(32)
            lw = slot(33)[:, 0:512]
            halves = [(j, q) for j in range(2) for q in range(2)]

            def chunked(a):
                return (a[:, :, 0:SEQ].rearrange("p j (c t) -> p j c t", t=CH), a[:, :, SEQ:TOK].rearrange("p j (b t) -> p j b t", t=NEW))

            def flat(a):
                return a.rearrange("p j t -> p (j t)")

            with stage(nc, "lora_in", "v_steps", "lora_ready", "lora_act", "mm_done", "act_out", "sq_ready", "kk_mm", "root_ready",
                       "rk_ready", "rk_mm", "rk_out", "cum_ready", "exp_ready") as (
                    block, lora_in, v_steps, lora_ready, lora_act, mm_done, act_out, sq_ready, kk_mm, root_ready,
                    rk_ready, rk_mm, rk_out, cum_ready, exp_ready):
                @block.sync
                def _(sp):
                    sp.dma_start(lw, at("lora")).then_inc(lora_in, 16)

                @block.tensor
                def _(pe):
                    pe.wait_ge(lora_in, 16)
                    pe.wait_ge(lora_act, 2)
                    for u in range(12):
                        kind, (j, q) = u // 4, halves[u % 4]
                        if u >= 8:
                            pe.wait_ge(act_out, u - 7)
                        w, x = [(lw[0:64, j * P:(j + 1) * P], lora[0:64, 0]), (lw[64:P, j * P:(j + 1) * P], lora[64:P, 0]),
                                (lw[:, 256 + j * P:256 + (j + 1) * P], lora[:, 1])][kind]
                        pe.matmul(ps[:, u % 8, 0:HN], w, x[:, q * HN:(q + 1) * HN], start=True, stop=True).then_inc(mm_done, 1)
                    pe.wait_ge(sq_ready, 1)
                    pe.wait_ge(act_out, 12)
                    for u, (j, q) in enumerate(halves):
                        pe.matmul(ps[:, u, 0:HN], C("head_mean"), t1[:, j, q * HN:(q + 1) * HN], start=True, stop=True).then_inc(kk_mm, 1)
                    pe.wait_ge(rk_ready, 2)
                    for u, (j, q) in enumerate(halves):
                        pe.matmul(ps[:, 4 + u, 0:HN], C("head_mean"), t1[:, j, q * HN:(q + 1) * HN], start=True, stop=True).then_inc(rk_mm, 1)

                @block.scalar
                def _(act):
                    act.wait_ge(lora_ready, 4)
                    act.activation(lora[0:64, 0], lora[0:64, 0], ACT.Tanh).then_inc(lora_act, 1)
                    act.activation(lora[:, 1], lora[:, 1], ACT.Sigmoid).then_inc(lora_act, 1)
                    for u in range(12):
                        kind, (j, q) = u // 4, halves[u % 4]
                        act.wait_ge(mm_done, u + 1)
                        src = ps[:, u % 8, 0:HN]
                        d = (sig, a_, gate)[kind][:, j, q * HN:(q + 1) * HN]
                        if kind == 2:
                            act.copy(d, src).then_inc(act_out, 1)
                        else:
                            act.activation(d, src, ACT.Sigmoid, bias=col("w0" if kind == 0 else "a0", j)).then_inc(act_out, 1)
                    for u, (j, q) in enumerate(halves):
                        act.wait_ge(kk_mm, u + 1)
                        act.activation(t2[:, j, q * HN:(q + 1) * HN], ps[:, u, 0:HN], ACT.Copy, scale=float(HD), bias=EPS).then_inc(root_ready, 1)
                    act.wait_ge(root_ready, 4)
                    act.activation(flat(t2), flat(t2), ACT.Sqrt).then_inc(root_ready, 1)
                    act.wait_ge(cum_ready, 1)
                    act.activation(flat(Gd), flat(cumB), ACT.Exp, scale=-KAPPA).then_inc(exp_ready, 1)
                    act.activation(flat(Gi), flat(cumB), ACT.Exp, scale=KAPPA).then_inc(exp_ready, 1)
                    act.wait_ge(cum_ready, 2)
                    act.activation(flat(cumA), flat(sig), ACT.Exp, scale=-KAPPA).then_inc(exp_ready, 1)

                @block.vector
                def _(dve):
                    st = Steps(dve, v_steps)
                    hsp, hss = hs[:, :, 0:SEQ], hs[:, :, SEQ:TOK].rearrange("p c (b t) -> p c b t", b=NSEQ)
                    for c in range(8):
                        st.did(dve.tensor_tensor(hsp[:, c], hAp[:, c, 0:SEQ], hAp[:, c, 1:SEQ + 1], ALU.subtract))
                    st.did(dve.tensor_tensor(hss, hAs[:, :, :, 0:NEW], hAs[:, :, :, 1:NEW + 1], ALU.subtract))
                    st.settle()
                    for n, c in enumerate((6, 7, 2, 3, 0, 1, 4, 5)):
                        sem = lora_ready if n < 2 else v_steps
                        dve.scalar_tensor_tensor(hsp[:, c], hsp[:, c], col("mu", c), hAp[:, c, 1:SEQ + 1], ALU.mult, ALU.add).then_inc(sem, 1)
                        dve.scalar_tensor_tensor(hss[:, c], hss[:, c], col("mu", c), hAs[:, c, :, 1:NEW + 1], ALU.mult, ALU.add).then_inc(sem, 1)
                    st.n += 12
                    st.settle()
                    for j in range(2):
                        st.did(dve.tensor_scalar(kkn[:, j], k_[:, j], col("kk", j), None, ALU.mult))
                    st.settle()
                    dve.tensor_tensor(flat(t1), flat(kkn), flat(kkn), ALU.mult).then_inc(sq_ready, 1)
                    dve.wait_ge(root_ready, 5)
                    st.link(dve.reciprocal(flat(t2), flat(t2)))
                    st.did(dve.tensor_tensor(flat(kkn), flat(kkn), flat(t2), ALU.mult))
                    for j in range(2):
                        st.did(dve.tensor_scalar(t1[:, j], a_[:, j], -1.0, col("ka", j), ALU.add, ALU.mult))
                    st.settle()
                    st.link(dve.scalar_tensor_tensor(flat(k_), flat(t1), 1.0, flat(k_), ALU.add, ALU.mult))
                    st.link(dve.tensor_tensor(flat(t1), flat(r_), flat(k_), ALU.mult))
                    for j in range(2):
                        dve.tensor_scalar(t1[:, j], t1[:, j], col("rk", j), None, ALU.mult).then_inc(rk_ready, 1)
                    for u, (j, q) in enumerate(halves):
                        dve.wait_ge(rk_mm, u + 1)
                        dve.scalar_tensor_tensor(yadd[:, j, q * HN:(q + 1) * HN], ps[:, 4 + u, 0:HN], float(HD), v_[:, j, q * HN:(q + 1) * HN],
                                                 ALU.mult, ALU.mult).then_inc(rk_out, 1)
                    src, dst = sig, cumA
                    for n in range(6):
                        w = 1 << n
                        (sp_, ss_), (dp_, ds_) = chunked(src), chunked(dst)
                        st.did(dve.tensor_tensor(dp_[:, :, :, w:], sp_[:, :, :, w:], sp_[:, :, :, :-w], ALU.add))
                        st.did(dve.tensor_copy(dp_[:, :, :, 0:w], sp_[:, :, :, 0:w]))
                        if n < 3:
                            st.did(dve.tensor_tensor(ds_[:, :, :, w:], ss_[:, :, :, w:], ss_[:, :, :, :-w], ALU.add))
                            st.did(dve.tensor_copy(ds_[:, :, :, 0:w], ss_[:, :, :, 0:w]))
                        elif n == 3:
                            st.did(dve.tensor_copy(ds_, ss_))
                        st.settle()
                        src, dst = dst, (cumB if dst is cumA else cumA)
                    assert src is cumB
                    dve.sem_inc(cum_ready, 1)
                    dve.tensor_tensor(flat(sig), flat(cumB), flat(sig), ALU.subtract).then_inc(cum_ready, 1)
                    dve.wait_ge(exp_ready, 2)
                    st.did(dve.tensor_tensor(flat(Qr), flat(r_), flat(Gd), ALU.mult))
                    st.did(dve.tensor_tensor(flat(Kr), flat(k_), flat(Gi), ALU.mult))
                    dve.wait_ge(rk_out, 4)
                    st.link(dve.tensor_tensor(flat(t1), flat(kkn), flat(a_), ALU.mult))
                    st.did(dve.tensor_tensor(flat(Br), flat(t1), flat(Gi), ALU.mult))
                    dve.wait_ge(exp_ready, 3)
                    st.did(dve.scalar_tensor_tensor(flat(Ar), flat(kkn), -1.0, flat(cumA), ALU.mult, ALU.mult))
                    (gp, gs) = chunked(Gd)
                    st.did(dve.tensor_copy(GL[:, 0, 0:8, :].rearrange("p c j -> p j c").unsqueeze(3), gp[:, :, :, CH - 1:CH]))
                    st.did(dve.tensor_copy(GLs[:, 0].unsqueeze(3), gs[:, :, :, NEW - 1:NEW]))
                    st.settle()
                    for d, s in ((t1, Kr), (t2, Br)):
                        (dp_, ds_), (sp_, ss_) = chunked(d), chunked(s)
                        for j in range(2):
                            st.did(dve.tensor_tensor(dp_[:, j], sp_[:, j], gp[:, j, :, CH - 1:CH].broadcast_to([P, 8, CH]), ALU.mult))
                            st.did(dve.tensor_tensor(ds_[:, j], ss_[:, j], gs[:, j, :, NEW - 1:NEW].broadcast_to([P, NSEQ, NEW]), ALU.mult))
                    st.settle()

            cg = [range(0, 4), range(4, 8), range(8, 9)]
            heads4 = [(j, hf, slice(64 * hf, 64 * hf + 64)) for j in range(2) for hf in range(2)]

            def per_head(g):
                return [((n * 2 + j) * CH, c, j, p) for n, c in enumerate(cg[g]) for j, hf, p in heads4]

            def bank3(b, g, n=CH):
                w = len(cg[g]) * 2
                return ps[:, b, 0:w * n].rearrange("p (x t) -> p x t", t=n)

            def part3(i, g):
                return tm(i)[:, cg[g].start:cg[g].stop].rearrange("p c j t -> p (c j) t")

            def mask3(m, g):
                return bc(C(m + ("_s" if g == 2 else "_p")), 1, len(cg[g]) * 2)

            En_r, MT, PB, PK, V_t, A_t, K_t, B_t, MV = 5, 6, 7, 8, 9, 14, 15, 17, 18
            rkinds = [("turn", v_, V_t), ("turn", Ar, A_t), ("turn", t1, K_t), ("turn", t2, B_t),
                      ("En", Ar, Br, En_r), ("MT", Kr, Ar, MT), ("PB", Br, Qr, PB), ("PK", Kr, Qr, PK), ("MV", MT, V_t, MV)]
            runits = [(k, g) for k in rkinds for g in range(3)]
            on_act = lambda kind: kind in ("turn", "En", "MV", "KK")
            with stage(nc, "mm_done", "act_out", "dve_out") as (block, mm_done, act_out, dve_out):
                def counts(units):
                    n, out = {True: 0, False: 0}, []
                    for k, g in units:
                        n[on_act(k[0])] += 1
                        out.append((on_act(k[0]), n[on_act(k[0])]))
                    return out
                cnt = counts(runits)

                @block.tensor
                def _(pe):
                    for u, (k, g) in enumerate(runits):
                        if u >= 8:
                            a, n = cnt[u - 8]
                            pe.wait_ge(act_out if a else dve_out, n)
                        if k[0] == "MV" and g == 0:
                            pe.wait_ge(dve_out, cnt[u - 1][1])
                            pe.wait_ge(act_out, 3)
                        for x, c, j, p in per_head(g):
                            tk = slice(c * CH, (c + 1) * CH)
                            if k[0] == "turn":
                                lhsT, rhs = k[1][p, j, tk], C("id64")[p]
                            elif k[0] == "MV":
                                lhsT, rhs = tm(MT)[p, c, j], tm(V_t)[p, c, j]
                            else:
                                lhsT, rhs = k[1][p, j, tk], k[2][p, j, tk]
                            last = pe.matmul(ps[p, u % 8, x:x + CH], lhsT, rhs, start=True, stop=True)
                        last.then_inc(mm_done, 1)

                @block.scalar
                def _(act):
                    for u, (k, g) in enumerate(runits):
                        if on_act(k[0]):
                            act.wait_ge(mm_done, u + 1)
                            act.activation(part3(k[-1], g), bank3(u % 8, g), ACT.Copy, scale=-1.0 if k[0] == "En" else 1.0).then_inc(act_out, 1)

                @block.vector
                def _(dve):
                    for u, (k, g) in enumerate(runits):
                        if not on_act(k[0]):
                            dve.wait_ge(mm_done, u + 1)
                            dve.tensor_tensor(part3(k[-1], g), bank3(u % 8, g), mask3("SUt" if k[0] == "MT" else "U", g), ALU.mult).then_inc(dve_out, 1)

            cv = slot(21, 3).rearrange("p (c t) -> p c t", c=6)
            sg3 = slot(24, 3).rearrange("p (c t) -> p c t", c=6)
            qd_, kd_, vd_ = ch(21), ch(22), ch(23)
            nq, nk = ch(24), ch(25)
            nrm2 = slot(24, 2)
            rt2 = slot(29, 2)
            g_, beta = beta_g[:, 0], beta_g[:, 1]
            sp_m, sp_a, sp_e = gcol[:, 3], gcol[:, 4], gcol[:, 5]
            eg, et, beg = gcol[:, 0], gcol[:, 1], gcol[:, 2]
            alog = stat[:, 48:50]
            g8 = stat[:, 0:16].rearrange("p (j b) -> p j b", j=2)
            with stage(nc, "v_steps", "conv_ready", "sig_ready", "sqn_ready", "mm_done", "root_ready", "ab_ready", "sp_exp", "g_ready",
                       "gsum_done", "gexp_ready") as (block, v_steps, conv_ready, sig_ready, sqn_ready, mm_done, root_ready, ab_ready,
                                                      sp_exp, g_ready, gsum_done, gexp_ready):
                @block.vector
                def _(dve):
                    st = Steps(dve, v_steps)
                    st.link(dve.tensor_tensor(g_, g_, bc(cols[:, COLS["dt"][0]:COLS["dt"][0] + 2], 1, NCH), ALU.add))
                    st.link(dve.tensor_scalar(sp_m, g_, 0.0, None, ALU.max))
                    dve.scalar_tensor_tensor(sp_a, sp_m, 2.0, g_, ALU.mult, ALU.subtract).then_inc(ab_ready, 1)
                    for n in range(4):
                        for c in range(6):
                            xp, xs = hBp[:, c, n:n + SEQ], hBs[:, c, :, n:n + NEW]
                            dp_, ds_ = cv[:, c, 0:SEQ], cv[:, c, SEQ:TOK].rearrange("p (b t) -> p b t", b=NSEQ)
                            w = col("conv", n * 6 + c)
                            for d, x in ((dp_, xp), (ds_, xs)):
                                if n == 0:
                                    i = dve.tensor_scalar(d, x, w, None, ALU.mult)
                                else:
                                    i = dve.scalar_tensor_tensor(d, x, w, d, ALU.mult, ALU.add)
                                if n == 3:
                                    i.then_inc(conv_ready, 1)
                                else:
                                    st.did(i)
                        if n < 3:
                            st.settle()
                    dve.wait_ge(conv_ready, 12)
                    dve.wait_ge(sig_ready, 3)
                    st.link(dve.tensor_tensor(slot(21, 3), slot(21, 3), slot(24, 3), ALU.mult))
                    dve.tensor_tensor(nrm2, slot(21, 2), slot(21, 2), ALU.mult).then_inc(sqn_ready, 1)
                    dve.wait_ge(sig_ready, 4)
                    st.did(dve.tensor_tensor(flat(z_ch), flat(z_ch), slot(27), ALU.mult))
                    dve.wait_ge(sp_exp, 3)
                    st.link(dve.tensor_tensor(sp_m, sp_m, sp_e, ALU.add))
                    st.link(dve.scalar_tensor_tensor(g_, sp_m, -1.0, bc(alog, 1, NCH), ALU.mult, ALU.mult))
                    st.did(dve.tensor_tensor(g8, bc(g_[:, 8], 2, NSEQ), bc(C("seq_of"), 1, 2), ALU.mult))
                    su, gb = tm(26), tm(31)
                    for m, a, b in (("_p", 0, 8), ("_s", 8, 9)):
                        for j in range(2):
                            st.did(dve.tensor_tensor(su[:, a:b, j], bc(C("SU" + m), 1, b - a), bc(g_[:, a:b, j], 2, CH), ALU.mult))
                    st.did(dve.tensor_copy(gb.rearrange("p c j t -> p (c j) t"), bc(g_.rearrange("p c j -> p (c j)"), 2, CH)))
                    st.settle()
                    dve.sem_inc(g_ready, 1)
                    dve.wait_ge(root_ready, 10)
                    st.link(dve.reciprocal(rt2, rt2))
                    st.did(dve.scalar_tensor_tensor(flat(qd_), flat(qd_), HD ** -0.5, slot(29), ALU.mult, ALU.mult))
                    st.did(dve.tensor_tensor(flat(kd_), flat(kd_), slot(30), ALU.mult))
                    dve.wait_ge(gexp_ready, 4)
                    st.did(dve.scalar_tensor_tensor(beg, eg, -1.0, beta, ALU.mult, ALU.mult))
                    st.settle()

                @block.scalar
                def _(act):
                    act.wait_ge(conv_ready, 12)
                    for n in range(3):
                        act.activation(slot(24 + n), slot(21 + n), ACT.Sigmoid).then_inc(sig_ready, 1)
                    act.activation(slot(27), flat(z_ch), ACT.Sigmoid).then_inc(sig_ready, 1)
                    act.activation(beta, beta, ACT.Sigmoid).then_inc(sp_exp, 1)
                    act.wait_ge(ab_ready, 1)
                    act.activation(sp_e, sp_a, ACT.Exp, scale=-1.0).then_inc(root_ready, 1)
                    act.activation(alog, cols[:, COLS["a_log"][0]:COLS["a_log"][0] + 2], ACT.Exp).then_inc(sp_exp, 1)
                    act.wait_ge(root_ready, 1)
                    act.activation(sp_e, sp_e, ACT.Ln, bias=1.0).then_inc(sp_exp, 1)
                    for u in range(8):
                        act.wait_ge(mm_done, u + 1)
                        i, (j, q) = u // 4, halves[u % 4]
                        act.activation(ch(29 + i)[:, j, q * HN:(q + 1) * HN], ps[:, u, 0:HN], ACT.Copy, scale=float(HD), bias=EPS).then_inc(root_ready, 1)
                    act.wait_ge(root_ready, 9)
                    act.activation(rt2, rt2, ACT.Sqrt).then_inc(root_ready, 1)
                    act.wait_ge(gsum_done, 1)
                    act.activation(eg.rearrange("p c j -> p (c j)"), ps[:, 0, 0:18], ACT.Exp).then_inc(gexp_ready, 1)
                    act.activation(et.rearrange("p c j -> p (c j)"), ps[:, 0, 18:36], ACT.Exp).then_inc(gexp_ready, 1)
                    act.activation(GL[:, 1, 0:8, :].rearrange("p c j -> p (c j)"), ps[:, 0, 36:52], ACT.Exp).then_inc(gexp_ready, 1)
                    act.activation(GLs[:, 1].rearrange("p j b -> p (j b)"), ps[:, 0, 54:70], ACT.Exp).then_inc(gexp_ready, 1)

                @block.tensor
                def _(pe):
                    pe.wait_ge(sqn_ready, 1)
                    for u in range(8):
                        i, (j, q) = u // 4, halves[u % 4]
                        pe.matmul(ps[:, u, 0:HN], C("head_mean"), ch(24 + i)[:, j, q * HN:(q + 1) * HN], start=True, stop=True).then_inc(mm_done, 1)
                    pe.wait_ge(g_ready, 1)
                    pe.wait_ge(root_ready, 9)
                    for hf in range(2):
                        p = slice(64 * hf, 64 * hf + 64)
                        gp, gs = g_[p, 0:8].rearrange("p c j -> p (c j)"), g_[p, 8]
                        for at_, mat, rhs in ((0, "U_p", gp), (16, "U_s", gs), (18, "SU_p", gp), (34, "SU_s", gs),
                                              (36, "ones", gp), (54, "ones", g8[p].rearrange("p j b -> p (j b)"))):
                            n = rhs.shape[1]
                            last = pe.matmul(ps[p, 0, at_:at_ + n], C(mat)[p], rhs, start=True, stop=True)
                    last.then_inc(gsum_done, 1)

            En_g, ATT, Kd_t, Vd_t, KB_t, Qg = 6, 16, 25, 24, 27, 19
            dkinds = [("turn", kd_, Kd_t), ("turn", vd_, Vd_t), ("Dts", None, 29), ("Dst", None, 30), ("row", None, 33),
                      ("KKn", kd_, kd_, En_g), ("KQ", kd_, qd_, ATT)]
            dunits = [(k, g) for k in dkinds for g in range(3)]
            on_act2 = lambda kind: kind in ("turn", "Dts", "Dst", "row")
            with stage(nc, "mm_done", "act_out", "dve_out", "v_steps") as (block, mm_done, act_out, dve_out, v_steps):
                su, gb = tm(26), tm(31)
                na = sum(on_act2(k[0]) for k, g in dunits)

                @block.tensor
                def _(pe):
                    for u, (k, g) in enumerate(dunits):
                        if u >= 8:
                            v = u - 8
                            if v < na:
                                pe.wait_ge(act_out, v + 1)
                            else:
                                pe.wait_ge(dve_out, v - na + 1)
                        Um = C("U_s" if g == 2 else "U_p")
                        for x, c, j, p in per_head(g):
                            tk = slice(c * CH, (c + 1) * CH)
                            lhsT, rhs = {"turn": lambda: (k[1][p, j, tk], C("id64")[p]), "Dts": lambda: (Um[p], su[p, c, j]),
                                         "Dst": lambda: (su[p, c, j], Um[p]), "row": lambda: (gb[p, c, j], Um[p]),
                                         "KKn": lambda: (k[1][p, j, tk], k[2][p, j, tk]), "KQ": lambda: (k[1][p, j, tk], k[2][p, j, tk])}[k[0]]()
                            last = pe.matmul(ps[p, u % 8, x:x + CH], lhsT, rhs, start=True, stop=True)
                        last.then_inc(mm_done, 1)

                @block.scalar
                def _(act):
                    for u, (k, g) in enumerate(dunits[:na]):
                        act.wait_ge(mm_done, u + 1)
                        act.activation(part3(k[-1], g), bank3(u % 8, g), ACT.Copy if k[0] == "turn" else ACT.Exp).then_inc(act_out, 1)

                @block.vector
                def _(dve):
                    st = Steps(dve, v_steps)
                    dve.wait_ge(act_out, 6)
                    whole = lambda i: tm(i).rearrange("p c j t -> p (c j) t")
                    per_row = lambda a: bc(a.rearrange("p c j -> p (c j)"), 2, CH)
                    st.did(dve.tensor_tensor(whole(KB_t), whole(Kd_t), per_row(beg), ALU.mult))
                    st.did(dve.tensor_tensor(whole(Vd_t), whole(Vd_t), per_row(beta), ALU.mult))
                    st.settle()
                    st.did(dve.tensor_tensor(whole(Kd_t), whole(Kd_t), per_row(et), ALU.mult))
                    dve.wait_ge(act_out, na)
                    for u, (k, g) in enumerate(dunits[na:]):
                        dve.wait_ge(mm_done, na + u + 1)
                        dve.tensor_tensor(part3(k[-1], g), bank3((na + u) % 8, g), part3(29 if k[0] == "KKn" else 30, g), ALU.mult).then_inc(dve_out, 1)
                    for j in range(2):
                        st.did(dve.tensor_tensor(ch(Qg)[:, j].rearrange("p (c t) -> p c t", t=CH), qd_[:, j].rearrange("p (c t) -> p c t", t=CH),
                                                 tm(33)[:, :, j], ALU.mult))
                    dve.wait_ge(dve_out, 6)
                    st.did(dve.tensor_tensor(whole(En_g), whole(En_g), per_row(beta), ALU.mult))
                    for g in range(3):
                        st.did(dve.tensor_tensor(part3(ATT, g), part3(ATT, g), mask3("U", g), ALU.mult))
                    st.settle()

            TM, TTm, P1, Em = (10, 11), (12, 13), (21, 22), (23, 26)
            En = (En_r, En_g)
            steps = [(lv, m, g) for lv in range(6) for m in range(2) for g in range(3 if lv < 3 else 2)]
            with stage(nc, "em_ready", "p1_done", "p1_out", "tt_done", "t_ready") as (
                    block, em_ready, p1_done, p1_out, tt_done, t_ready):
                place = {s: n for n, s in enumerate(steps)}
                FIRST = 6

                @block.gpsimd
                def _(pool):
                    for lv in range(6):
                        for m in range(2):
                            if lv:
                                pool.wait_ge(p1_done, place[(lv - 1, m, 1 if lv > 3 else 2)] + 1)
                            if lv == 1:
                                pool.wait_ge(t_ready, 6 * (m + 1))
                            pool.tensor_tensor(tm(Em[m]).rearrange("p c j t -> p (c j) t"), tm(En[m]).rearrange("p c j t -> p (c j) t"),
                                               bc(C("lev", lv), 1, 2 * NCH), ALU.mult).then_inc(em_ready, 1)

                @block.tensor
                def _(pe):
                    for n in range(FIRST):
                        _, m, g = steps[n]
                        pe.wait_ge(em_ready, m + 1)
                        if n >= 2:
                            pe.wait_ge(t_ready, 2 * (n - 1))
                        for x, c, j, p in per_head(g):
                            last = pe.matmul(ps[p, n % 2, x:x + CH], tm(Em[m])[p, c, j], C("id64")[p], start=True, stop=True)
                        last.then_inc(p1_done, 1)
                    for lv in range(1, 6):
                        ns = [n for n, s in enumerate(steps) if s[0] == lv]
                        for n in ns:
                            _, m, g = steps[n]
                            pe.wait_ge(em_ready, 2 * lv + m + 1)
                            pe.wait_ge(t_ready, 2 * place[(lv - 1, m, g)] + 2)
                            if n >= FIRST + 2:
                                pe.wait_ge(p1_out, n - FIRST - 1)
                            elif n >= FIRST:
                                pe.wait_ge(t_ready, 2 * (n - 1))
                            for x, c, j, p in per_head(g):
                                last = pe.matmul(ps[p, n % 2, x:x + CH], tm(Em[m])[p, c, j], tm(TTm[m])[p, c, j], start=True, stop=True)
                            last.then_inc(p1_done, 1)
                        for n in ns:
                            _, m, g = steps[n]
                            pe.wait_ge(p1_out, n - FIRST + 1)
                            pe.wait_ge(t_ready, 2 * (n - 2))
                            b = 2 + 2 * (n % 3)
                            for x, c, j, p in per_head(g):
                                pe.matmul(ps[p, b, x:x + CH], tm(P1[m])[p, c, j], tm(TM[m])[p, c, j], start=True, stop=True)
                            for x, c, j, p in per_head(g):
                                last = pe.matmul(ps[p, b + 1, x:x + CH], tm(TM[m])[p, c, j], tm(P1[m])[p, c, j], start=True, stop=True)
                            last.then_inc(tt_done, 1)

                @block.scalar
                def _(act):
                    for n, (lv, m, g) in enumerate(steps[FIRST:], FIRST):
                        act.wait_ge(p1_done, n + 1)
                        if lv > 1:
                            act.wait_ge(tt_done, place[(lv - 1, m, g)] - FIRST + 1)
                        act.copy(part3(P1[m], g), bank3(n % 2, g)).then_inc(p1_out, 1)

                @block.vector
                def _(dve):
                    for n, (_, m, g) in enumerate(steps[:FIRST]):
                        eye = bc(C("id64"), 1, 2 * len(cg[g]))
                        dve.wait_ge(em_ready, m + 1)
                        dve.tensor_tensor(part3(TM[m], g), eye, part3(Em[m], g), ALU.subtract).then_inc(t_ready, 1)
                        dve.wait_ge(p1_done, n + 1)
                        dve.tensor_tensor(part3(TTm[m], g), eye, bank3(n % 2, g), ALU.subtract).then_inc(t_ready, 1)
                    for n, (lv, m, g) in enumerate(steps[FIRST:], FIRST):
                        dve.wait_ge(tt_done, n - FIRST + 1)
                        b = 2 + 2 * (n % 3)
                        dve.wait_ge(t_ready, 2 * place[(lv - 1, m, g)] + 2)
                        dve.tensor_tensor(part3(TM[m], g), part3(TM[m], g), bank3(b, g), ALU.subtract).then_inc(t_ready, 1)
                        dve.tensor_tensor(part3(TTm[m], g), part3(TTm[m], g), bank3(b + 1, g), ALU.subtract).then_inc(t_ready, 1)

            WT, UU = (29, 30), (31, 33)
            wu = [(k, m, g) for m in range(2) for k in range(2) for g in range(3)]
            with stage(nc, "mm_done", "act_out", "dve_out") as (block, mm_done, act_out, dve_out):
                @block.tensor
                def _(pe):
                    for u, (k, m, g) in enumerate(wu):
                        if u >= 8:
                            pe.wait_ge(dve_out if u % 2 else act_out, (u - 8) // 2 + 1)
                        for x, c, j, p in per_head(g):
                            tt = tm(TTm[m])[p, c, j]
                            lhsT, rhs = (tm((A_t, KB_t)[m])[p, c, j], tt) if k == 0 else (tt, tm((MV, Vd_t)[m])[p, c, j])
                            last = pe.matmul(ps[p, u % 8, x:x + CH], lhsT, rhs, start=True, stop=True)
                        last.then_inc(mm_done, 1)

                def target(u):
                    k, m, g = wu[u]
                    return part3((WT, UU)[k][m], g), bank3(u % 8, g)

                @block.scalar
                def _(act):
                    for u in range(0, len(wu), 2):
                        act.wait_ge(mm_done, u + 1)
                        act.copy(*target(u)).then_inc(act_out, 1)

                @block.vector
                def _(dve):
                    for u in range(1, len(wu), 2):
                        dve.wait_ge(mm_done, u + 1)
                        dve.tensor_copy(*target(u)).then_inc(dve_out, 1)

            S = S_sb[:, :].rearrange("p (m j n) -> p m j n", m=2, j=2)
            SA = slot(21)[:, 0:512].rearrange("p (s m j n) -> p s m j n", s=2, m=2, j=2)
            Y = (14, 27)
            Qx = (Qr, ch(Qg))
            Px = (PB, ATT)
            Kx = (B_t, Kd_t)
            mh = [(m, j, p) for m in range(2) for j, hf, p in heads4]
            S0 = slot(10, 2)[:, 0:2048].rearrange("p (m j b n) -> p m j b n", m=2, j=2, b=NSEQ)
            with stage(nc, "s_ready", "ws_done", "sa_ready", "out_done", "ds_done", "y_out", "scaled", "state_out", "s0_in") as (
                    block, s_ready, ws_done, sa_ready, out_done, ds_done, y_out, scaled, state_out, s0_in):
                @block.tensor
                def _(pe):
                    for c in range(8):
                        tk = slice(c * CH, (c + 1) * CH)
                        bw, bo, bd = c % 2, 2 + c % 2, 4 + c % 2
                        at_ = lambda m, j: slice((m * 2 + j) * CH, (m * 2 + j + 1) * CH)
                        pe.wait_ge(s_ready, c + 1)
                        if c >= 2:
                            pe.wait_ge(sa_ready, 2 * (c - 1))
                            pe.wait_ge(y_out, 2 * (c - 1))
                        for m, j, p in mh:
                            last = pe.matmul(ps[p, bw, at_(m, j)], tm(WT[m])[p, c, j], S[p, m, j], start=True, stop=True)
                        last.then_inc(ws_done, 1)
                        pe.wait_ge(sa_ready, 2 * (c + 1))
                        for m, j, p in mh:
                            pe.matmul(ps[p, bd, at_(m, j)], tm(Kx[m])[p, c, j], SA[p, c % 2, m, j], start=True, stop=(m == 1))
                            if m == 0:
                                pe.matmul(ps[p, bd, at_(m, j)], tm(K_t)[p, c, j], tm(V_t)[p, c, j], start=False, stop=True)
                        for m, j, p in mh:
                            o = ps[p, bo, at_(m, j)]
                            pe.matmul(o, S[p, m, j], Qx[m][p, j, tk], start=True, stop=False)
                            last = pe.matmul(o, SA[p, c % 2, m, j], tm(Px[m])[p, c, j], start=False, stop=(m == 1))
                            if m == 0:
                                last = pe.matmul(o, tm(V_t)[p, c, j], tm(PK)[p, c, j], start=False, stop=True)
                        last.then_inc(out_done, 1)

                @block.vector
                def _(dve):
                    dve.memset(S, 0.0).then_inc(s_ready, 1)
                    dve.wait_ge(s_ready, 1)
                    for c in range(8):
                        dve.wait_ge(ws_done, c + 1)
                        for m in range(2):
                            dve.tensor_tensor(SA[:, c % 2, m], tm(UU[m])[:, c], ps[:, c % 2, m * 128:(m + 1) * 128].rearrange("p (j n) -> p j n", j=2),
                                              ALU.add).then_inc(sa_ready, 1)
                        dve.wait_ge(out_done, c + 1)
                        dve.tensor_tensor(S, S, bc(GL[:, :, c], 3, HD), ALU.mult).then_inc(scaled, 1)
                        dve.wait_ge(scaled, c + 1)
                        dve.tensor_tensor(S, S, ps[:, 4 + c % 2, 0:256].rearrange("p (m j n) -> p m j n", m=2, j=2), ALU.add).then_inc(s_ready, 1)
                        dve.wait_ge(s_ready, c + 2)

                @block.scalar
                def _(act):
                    for c in range(8):
                        act.wait_ge(out_done, c + 1)
                        for m in range(2):
                            act.copy(ch(Y[m])[:, :, c * CH:(c + 1) * CH],
                                     ps[:, 2 + c % 2, m * 128:(m + 1) * 128].rearrange("p (j t) -> p j t", j=2)).then_inc(y_out, 1)

                @block.sync
                def _(sp):
                    sp.dma_start(slot(10, 2)[:, 0:2048], at("states")).then_inc(s0_in, 16)
                    sp.wait_ge(s_ready, 9)
                    sp.dma_start(at("o_state_p"), S_sb[:, :]).then_inc(state_out, 16)
                    sp.wait_ge(state_out, 16)
                    sp.wait_ge(s0_in, 16)

            SAT = slot(21)[:, 512:768].rearrange("p (x t) -> p x t", x=4)
            SA1 = slot(21)[:, 0:256].rearrange("p (m j n) -> p m j n", m=2, j=2)
            SAx = slot(12, 2)[:, 0:2048].rearrange("p (x b n) -> p x b n", x=4, b=NSEQ)
            Vx = slot(22)[:, 0:1024].rearrange("p (j b n) -> p j b n", j=2, b=NSEQ)
            with stage(nc, "sat_done", "sat_out", "sa_done", "sa_ready", "x_ready", "y_done", "y_out", "ds_done", "s_ready", "state_out") as (
                    block, sat_done, sat_out, sa_done, sa_ready, x_ready, y_done, y_out, ds_done, s_ready, state_out):
                tk = lambda b: slice(SEQ + b * NEW, SEQ + (b + 1) * NEW)

                @block.tensor
                def _(pe):
                    for m, j, p in mh:
                        for b in range(NSEQ):
                            last = pe.matmul(ps[p, 0, (m * 2 + j) * CH + b * NEW:(m * 2 + j) * CH + (b + 1) * NEW], S0[p, m, j, b],
                                             tm(WT[m])[p, 8, j, b * NEW:(b + 1) * NEW], start=True, stop=True)
                    last.then_inc(sat_done, 1)
                    pe.wait_ge(sat_out, 1)
                    for m, j, p in mh:
                        x = m * 2 + j
                        last = pe.matmul(ps[p, 1, x * CH:(x + 1) * CH], SAT[p, x], C("id64")[p], start=True, stop=True)
                    last.then_inc(sa_done, 1)
                    pe.wait_ge(sa_ready, 2)
                    for m, j, p in mh:
                        x = m * 2 + j
                        pe.matmul(ps[p, 2, x * CH:(x + 1) * CH], SA1[p, m, j], tm(Px[m])[p, 8, j], start=True, stop=False)
                        if m == 0:
                            pe.matmul(ps[p, 2, x * CH:(x + 1) * CH], tm(V_t)[p, 8, j], tm(PK)[p, 8, j], start=False, stop=False)
                        for b in range(NSEQ):
                            last = pe.matmul(ps[p, 2, x * CH + b * NEW:x * CH + (b + 1) * NEW], S0[p, m, j, b], Qx[m][p, j, tk(b)],
                                             start=False, stop=(b == NSEQ - 1))
                    last.then_inc(y_done, 1)
                    pe.wait_ge(x_ready, 6)
                    for m, j, p in mh:
                        x = m * 2 + j
                        last = pe.matmul(ps[p, 4 + x, :], tm(Kx[m])[p, 8, j], SAx[p, x].rearrange("p b n -> p (b n)"), start=True, stop=(m == 1))
                        if m == 0:
                            last = pe.matmul(ps[p, 4 + x, :], tm(K_t)[p, 8, j], Vx[p, j].rearrange("p b n -> p (b n)"), start=False, stop=True)
                    last.then_inc(ds_done, 1)

                @block.scalar
                def _(act):
                    act.wait_ge(sat_done, 1)
                    act.copy(SAT.rearrange("p x t -> p (x t)"), ps[:, 0, 0:256]).then_inc(sat_out, 1)
                    act.wait_ge(y_done, 1)
                    for m in range(2):
                        act.copy(ch(Y[m])[:, :, SEQ:TOK], ps[:, 2, m * 128:(m + 1) * 128].rearrange("p (j t) -> p j t", j=2)).then_inc(y_out, 1)

                @block.vector
                def _(dve):
                    of = bc(C("seq_of"), 2, HD)
                    for j in range(2):
                        dve.tensor_tensor(Vx[:, j], bc(tm(V_t)[:, 8, j], 1, NSEQ), of, ALU.mult).then_inc(x_ready, 1)
                    dve.wait_ge(sa_done, 1)
                    for m in range(2):
                        dve.tensor_tensor(SA1[:, m], tm(UU[m])[:, 8], ps[:, 1, m * 128:(m + 1) * 128].rearrange("p (j n) -> p j n", j=2),
                                          ALU.add).then_inc(sa_ready, 1)
                    dve.wait_ge(sa_ready, 2)
                    for x in range(4):
                        dve.tensor_tensor(SAx[:, x], bc(SA1[:, x // 2, x % 2], 1, NSEQ), of, ALU.mult).then_inc(x_ready, 1)
                    dve.wait_ge(y_done, 1)
                    for x in range(4):
                        s = S0[:, x // 2, x % 2]
                        dve.tensor_tensor(s, s, bc(GLs[:, x // 2, x % 2], 2, HD), ALU.mult).then_inc(s_ready, 1)
                    dve.wait_ge(ds_done, 1)
                    dve.wait_ge(s_ready, 4)
                    for x in range(4):
                        s = S0[:, x // 2, x % 2]
                        dve.tensor_tensor(s, s, ps[:, 4 + x, :].rearrange("p (b n) -> p b n", b=NSEQ), ALU.add).then_inc(s_ready, 1)

                @block.sync
                def _(sp):
                    sp.wait_ge(s_ready, 8)
                    sp.dma_start(at("o_state_s"), slot(10, 2)[:, 0:2048]).then_inc(state_out, 16)
                    sp.wait_ge(state_out, 16)

            yr, yg = ch(14), ch(27)
            sqr, rtr, sqg, rtg = ch(21), ch(22), ch(23), ch(24)
            sqc, rtc = slot(5, 2), slot(7, 2)
            with stage(nc, "v_steps", "mean_done", "yc_ready", "sq_ready", "mm_done", "root_ready", "cat_ready") as (
                    block, v_steps, mean_done, yc_ready, sq_ready, mm_done, root_ready, cat_ready):
                vu = [("g", u) for u in range(4)] + [("c", u) for u in range(8)] + [("r", u) for u in range(4)]

                @block.tensor
                def _(pe):
                    for u, (j, q) in enumerate(halves):
                        pe.matmul(ps[:, u, 0:HN], C("head_mean"), yr[:, j, q * HN:(q + 1) * HN], start=True, stop=True).then_inc(mean_done, 1)
                    for n, (k, u) in enumerate(vu):
                        pe.wait_ge(sq_ready, {"g": 1, "c": 2, "r": 3}[k])
                        if n >= 4:
                            pe.wait_ge(root_ready, n - 3)
                        src = {"g": slot(23), "c": sqc, "r": slot(21)}[k][:, u * HN:(u + 1) * HN]
                        pe.matmul(ps[:, 4 + n % 4, 0:HN], C("all_mean" if k == "c" else "head_mean"), src, start=True, stop=True).then_inc(mm_done, 1)

                @block.scalar
                def _(act):
                    for n, (k, u) in enumerate(vu):
                        act.wait_ge(mm_done, n + 1)
                        d = {"g": slot(24), "c": rtc, "r": slot(22)}[k][:, u * HN:(u + 1) * HN]
                        act.activation(d, ps[:, 4 + n % 4, 0:HN], ACT.Copy, bias=64e-5 if k == "r" else EPS).then_inc(root_ready, 1)
                    act.wait_ge(root_ready, 16)
                    for n, d in enumerate((slot(24), rtc, slot(22))):
                        act.activation(d, d, ACT.Sqrt).then_inc(root_ready, 1)

                @block.vector
                def _(dve):
                    st = Steps(dve, v_steps)
                    OCf = slot(2, 2)
                    dve.tensor_tensor(flat(sqg), flat(yg), flat(yg), ALU.mult).then_inc(sq_ready, 1)
                    dve.tensor_tensor(sqc, OCf, OCf, ALU.mult).then_inc(sq_ready, 1)
                    for u, (j, q) in enumerate(halves):
                        dve.wait_ge(mean_done, u + 1)
                        v = yr[:, j, q * HN:(q + 1) * HN]
                        st.did(dve.tensor_tensor(v, v, ps[:, u, 0:HN], ALU.subtract))
                    st.settle()
                    dve.tensor_tensor(flat(sqr), flat(yr), flat(yr), ALU.mult).then_inc(sq_ready, 1)
                    st.link(dve.tensor_tensor(stat[:, 50:51], col("subln"), col("lam_rest"), ALU.mult))
                    dve.wait_ge(root_ready, 17)
                    st.link(dve.reciprocal(flat(rtg), flat(rtg)))
                    st.link(dve.tensor_tensor(flat(rtg), flat(rtg), flat(z_ch), ALU.mult))
                    st.link(dve.tensor_tensor(flat(rtg), flat(rtg), flat(yg), ALU.mult))
                    st.did(dve.tensor_scalar(slot(1), flat(rtg), col("dn_g"), None, ALU.mult))
                    dve.wait_ge(root_ready, 18)
                    st.link(dve.reciprocal(rtc, rtc))
                    st.did(dve.scalar_tensor_tensor(OCf, OCf, stat[:, 50:51], rtc, ALU.mult, ALU.mult))
                    dve.wait_ge(root_ready, 19)
                    st.link(dve.reciprocal(flat(rtr), flat(rtr)))
                    st.link(dve.tensor_tensor(flat(yr), flat(yr), flat(rtr), ALU.mult))
                    for j in range(2):
                        st.did(dve.tensor_scalar(yr[:, j], yr[:, j], col("ln_g", j), col("ln_b", j), ALU.mult, ALU.add))
                    st.settle()
                    st.link(dve.tensor_tensor(flat(yr), flat(yr), flat(yadd), ALU.add))
                    st.did(dve.tensor_tensor(slot(0), flat(yr), flat(gate), ALU.mult))
                    st.settle()

            with stage(nc, "wo_in0", "wo_in1", "hi_ready", "lo_ready", "cat_hi", "cat_ready", "mm_done", "x_steps") as (
                    block, wo_in0, wo_in1, hi_ready, lo_ready, cat_hi, cat_ready, mm_done, x_steps):
                ou = [(g, i) for g in range(D // WCH) for i in range(TILES)]
                wo_in = (wo_in0, wo_in1)
                raw = w_raw(4)

                @block.sync
                def _(sp):
                    wv = at("w_out").rearrange("(k p) n -> p k n", p=P)
                    for g in range(D // WCH):
                        if g >= 2:
                            sp.wait_ge(lo_ready, g - 1)
                        sp.dma_start(raw[:, g % 2], wv[:, :, g * WCH:(g + 1) * WCH]).then_inc(wo_in[g % 2], 16)

                @block.tensor
                def _(pe):
                    for u, (g, i) in enumerate(ou):
                        if i == 0:
                            pe.wait_ge(lo_ready, g + 1)
                        if u == 0:
                            pe.wait_ge(cat_ready, KC + 2)
                        if u >= 8:
                            pe.wait_ge(x_steps, u - 7)
                        wh, wl = w_part(g % 2, 0), w_part(g % 2, 1)
                        split_products(pe, ps[:, u % 8, 0:WCH], [(x_tile(k, i), (wh[:, k, :], wl[:, k, :])) for k in range(KC)]).then_inc(mm_done, 1)

                @block.scalar
                def _(act):
                    for k in range(KC):
                        act.copy(x_part(0)[:, k], cat[:, k]).then_inc(cat_hi, 1)
                    for g in range(D // WCH):
                        if g >= 2:
                            act.wait_ge(mm_done, TILES * (g - 1))
                        hi_of(act, g, raw, wo_in, hi_ready)

                @block.gpsimd
                def _(pool):
                    for h in range(2):
                        pool.tensor_copy(x_split[:, h * XW + KC * TOK:(h + 1) * XW], C("ones")).then_inc(cat_ready, 1)
                    for g in range(D // WCH):
                        lo_of(pool, g, raw, hi_ready, lo_ready)

                @block.vector
                def _(dve):
                    for k in range(KC):
                        dve.wait_ge(cat_hi, k + 1)
                        dve.tensor_tensor(x_part(1)[:, k], cat[:, k], x_part(0)[:, k].bitcast(F32), ALU.subtract).then_inc(cat_ready, 1)
                    for u, (g, i) in enumerate(ou):
                        w = min(P, TOK - i * P)
                        dve.wait_ge(mm_done, u + 1)
                        d = x_sb[0:w, i, g * WCH:(g + 1) * WCH]
                        dve.tensor_tensor(d, d, ps[0:w, u % 8, 0:WCH], ALU.add).then_inc(x_steps, 1)

            wq_view = at("pk_wq").rearrange("(k p) n -> p k n", p=P)
            norm_transposed("ffn_g", wq_view)
            qT = slot(4).rearrange("p (s t) -> p s t", s=2)
            SC = slot(5, 2)[:, 0:2 * TILES * P].rearrange("p (s i n) -> p s i n", s=2, i=TILES)
            keys = slot(14, 2)[:, 0:2048].rearrange("p (c n) -> p c n", c=16)
            best = arena[:, 8192:8192 + 2 * TILES * 256]
            SV = best[:, 0:TILES * 256].rearrange("p (i c n) -> p i c n", i=TILES, c=16)
            SI = best[:, TILES * 256:2 * TILES * 256].bitcast(U32).rearrange("p (i c n) -> p i c n", i=TILES, c=16)
            with stage(nc, "keys_in", "wq_in0", "wq_in1", "hi_ready", "lo_ready", "q_done", "q_out", "s_done", "s_out", "v_steps", "ranked") as (
                    block, keys_in, wq_in0, wq_in1, hi_ready, lo_ready, q_done, q_out, s_done, s_out, v_steps, ranked):
                wq_in = (wq_in0, wq_in1)
                raw = w_raw(0)

                @block.sync
                def _(sp):
                    sp.dma_start(keys, at("pk_keys")).then_inc(keys_in, 16)
                    for g in range(8):
                        if g < 2:
                            sp.sem_inc(wq_in[g], 16)
                        else:
                            sp.wait_ge(lo_ready, g - 1)
                            sp.dma_start(raw[:, g % 2], wq_view[:, :, g * WCH:(g + 1) * WCH]).then_inc(wq_in[g % 2], 16)

                @block.tensor
                def _(pe):
                    def queries(c):
                        g, m = c // 2, (c % 2) * P
                        pe.wait_ge(lo_ready, g + 1)
                        wh, wl = w_part(g % 2, 0), w_part(g % 2, 1)
                        for q in range(2):
                            u = 2 * c + q
                            if u >= 4:
                                pe.wait_ge(q_out, u - 3)
                            tq = slice(q * HN, (q + 1) * HN)
                            split_products(pe, ps[:, u % 4, 0:HN], [((wh[:, k, m:m + P], wl[:, k, m:m + P]), (x_part(0)[:, k, tq], x_part(1)[:, k, tq]))
                                                                    for k in range(KC)]).then_inc(q_done, 1)

                    def scores(c):
                        pe.wait_ge(q_out, 2 * c + 2)
                        if c == 0:
                            pe.wait_ge(keys_in, 16)
                        if c >= 2:
                            pe.wait_ge(s_out, 2 * (c - 1))
                        for i in range(TILES):
                            w = min(P, TOK - i * P)
                            last = pe.matmul(ps[0:w, 4 + 2 * (c % 2) + i // 4, (i % 4) * P:(i % 4 + 1) * P], qT[:, c % 2, i * P:i * P + w],
                                             keys[:, c, :], start=True, stop=True)
                        last.then_inc(s_done, 1)
                    for c in range(17):
                        if c < 16:
                            queries(c)
                        if c >= 1:
                            scores(c - 1)

                @block.scalar
                def _(act):
                    act.sem_inc(hi_ready, 2)
                    for c in range(17):
                        if c < 16:
                            if c % 2 == 0 and 2 <= c < 14:
                                act.wait_ge(q_done, 2 * c)
                                hi_of(act, c // 2 + 1, raw, wq_in, hi_ready)
                            if c >= 2:
                                act.wait_ge(s_done, c - 1)
                            for q in range(2):
                                act.wait_ge(q_done, 2 * c + q + 1)
                                act.copy(qT[:, c % 2, q * HN:(q + 1) * HN], ps[:, (2 * c + q) % 4, 0:HN]).then_inc(q_out, 1)
                        if c >= 1:
                            d = c - 1
                            act.wait_ge(s_done, d + 1)
                            if d >= 2:
                                act.wait_ge(ranked, d - 1)
                            act.copy(SC[:, d % 2, 0:4], ps[:, 4 + 2 * (d % 2), :].rearrange("p (i n) -> p i n", i=4)).then_inc(s_out, 1)
                            act.copy(SC[0:SAMP, d % 2, 4], ps[0:SAMP, 5 + 2 * (d % 2), 0:P]).then_inc(s_out, 1)

                @block.gpsimd
                def _(pool):
                    pool.sem_inc(lo_ready, 2)
                    for g in range(2, 8):
                        lo_of(pool, g, raw, hi_ready, lo_ready)

                @block.vector
                def _(dve):
                    st = Steps(dve, v_steps)
                    for c in range(16):
                        dve.wait_ge(s_out, 2 * (c + 1))

                        def each(step):
                            for i in range(TILES):
                                r = slice(0, min(P, TOK - i * P))
                                st.did(step(SV[r, i, c], SI[r, i, c], SC[r, c % 2, i]))
                            st.settle()
                        each(lambda v, n, sc: dve.max(v[:, 0:8], sc))
                        each(lambda v, n, sc: dve.max_index(n[:, 0:8], v[:, 0:8], sc))
                        each(lambda v, n, sc: dve.match_replace(sc, v[:, 0:8], sc, -3.0e38))
                        each(lambda v, n, sc: dve.max(v[:, 8:16], sc))
                        each(lambda v, n, sc: dve.max_index(n[:, 8:16], v[:, 8:16], sc))
                        dve.sem_inc(ranked, 1)

            TG = 32
            NTG = TOK // TG
            OCT = 8
            stg = arena[:, 0:2 * P * TG].rearrange("p (s e t) -> p s e t", s=2, e=P)
            cands = [arena[:, a:a + 2048].rearrange("p (h n) -> p h n", h=PK_HEADS) for a in (10752, 12800, 14848)]
            rest = arena[:, W_AT:ARENA]
            SIf = rest[:, 0:256].rearrange("p (h c n) -> p h c n", h=PK_HEADS, c=2)
            TV = rest[:, 256:384].rearrange("p (h n) -> p h n", h=PK_HEADS)
            TI = rest[:, 384:512].bitcast(U32).rearrange("p (h n) -> p h n", h=PK_HEADS)
            TA = rest[:, 512:768].bitcast(U32).rearrange("p (c n) -> p c n", c=2)
            TAf = rest[:, 768:1024].rearrange("p (c n) -> p c n", c=2)
            route = rest[:, 1024:1408].rearrange("p (k n) -> p k n", k=3)
            ex = rest[:, 1408:1536].rearrange("p (h n) -> p h n", h=PK_HEADS)
            sums = rest[:, 1536:1552]
            routeT = rest[:, 1552:1552 + 3 * TOKP].rearrange("p (k t) -> p k t", k=3)
            NAB = 4
            ABs = [a.rearrange("p (m t n) -> p m t n", m=2, t=OCT)
                   for a in (arena[:, 16896:18944], arena[:, 18944:20992], rest[:, 4096:6144], rest[:, 6144:8192])]
            gd = t["g_scratch"]
            octets = lambda i: (min(P, TOK - i * P)) // OCT
            with stage(nc, "v_steps", "cand_ready", "shifted", "exp_done", "eq_ready", "looked_up", "route_ready", "t_done", "t_out",
                       "onehots_ready", "b_ready", "g_done", "g_out", "g_saved0", "g_saved1") as (
                    block, v_steps, cand_ready, shifted, exp_done, eq_ready, looked_up, route_ready, t_done, t_out,
                    onehots_ready, b_ready, g_done, g_out, g_saved0, g_saved1):
                g_saved = (g_saved0, g_saved1)

                def of_octets(i, first, n):
                    return range(i * P // OCT + first, i * P // OCT + min(first + n, octets(i))) if i >= 0 else ()

                def lookup(i, c, r):
                    return cands[i % 2 if c == 0 else 2][r]

                @block.tensor
                def _(pe):
                    def turn(i):
                        w = min(P, TOK - i * P)
                        pe.wait_ge(route_ready, i + 1)
                        if i >= 1:
                            pe.wait_ge(t_out, i)
                        for k in range(3):
                            last = pe.transpose(ps[:, 0, k * P:k * P + w], route[0:w, k, :], C("ident")[0:w, 0:w])
                        last.then_inc(t_done, 1)

                    pe.sem_inc(g_out, 4)
                    turn(0)
                    for i in range(TILES):
                        with pe.Fori(0, octets(i) // NAB) as o4:
                            for s in range(NAB):
                                o = o4 * NAB + (i * P // OCT + s)
                                pe.wait_ge(g_out, o * 2 + 2)
                                pe.wait_ge(b_ready, o + 1)
                                for k in range(OCT):
                                    last = pe.matmul(ps[:, 4 + 2 * (s % 2) + k // 4, (k % 4) * P:(k % 4 + 1) * P], ABs[s][:, 0, k], ABs[s][:, 1, k],
                                                     start=True, stop=True)
                                    if k % 4 == 3:
                                        last.then_inc(g_done, 1)
                        if i + 1 < TILES:
                            turn(i + 1)

                @block.scalar
                def _(act):
                    def exponentials(i):
                        w = min(P, TOK - i * P)
                        act.wait_ge(shifted, i + 1)
                        act.activation(ex[0:w], ex[0:w], ACT.Exp).then_inc(exp_done, 1)

                    def routes_out(i):
                        w = min(P, TOK - i * P)
                        act.wait_ge(t_done, i + 1)
                        act.copy(routeT[:, :, i * P:i * P + w], ps[:, 0, 0:3 * P].rearrange("p (k t) -> p k t", k=3)[:, :, 0:w]).then_inc(t_out, 1)

                    for sg in range(2):
                        act.sem_inc(g_saved[sg], 16)
                    exponentials(0)
                    routes_out(0)
                    for i in range(TILES):
                        for g in range(i * P // TG, (i * P + octets(i) * OCT) // TG):
                            act.wait_ge(g_saved[g % 2], g // 2 * 16 + 16)
                            for q in range(TG // 4):
                                act.wait_ge(g_done, g * (TG // 4) + (q + 1))
                                act.copy(stg[:, g % 2, :, q * 4:q * 4 + 4], ps[:, 4 + q % 4, :].rearrange("p (t e) -> p e t", t=4)).then_inc(g_out, 1)
                            if g == i * P // TG + 1 and i + 1 < TILES:
                                exponentials(i + 1)
                        if i + 1 < TILES:
                            routes_out(i + 1)

                @block.gpsimd
                def _(pool):
                    def gated(i, first, n):
                        for o in of_octets(i, first, n):
                            ab = ABs[o % NAB][:, 1]
                            pool.wait_ge(onehots_ready, o + 1)
                            pool.tensor_tensor(ab, ab, bc(routeT[:, 2, o * OCT:(o + 1) * OCT], 2, P), ALU.mult).then_inc(b_ready, 1)

                    def candidates(i):
                        r = slice(0, min(P, TOK - i * P))
                        if i >= 2:
                            pool.wait_ge(route_ready, i - 1)
                        v = SV[:, i].rearrange("p (h c) n -> p h c n", c=2)[r]
                        pool.tensor_tensor(cands[i % 2][r].rearrange("p h (a b) -> p h a b", a=TOPK), bc(v[:, :, 0], 3, TOPK), bc(v[:, :, 1], 2, TOPK),
                                           ALU.add).then_inc(cand_ready, 1)
                    candidates(0)
                    for i in range(TILES):
                        r = slice(0, min(P, TOK - i * P))
                        gated(i - 1, 0, 4)
                        if i + 1 < TILES:
                            candidates(i + 1)
                        gated(i - 1, 4, 8)
                        for c in range(2):
                            e = lookup(i, c, r).rearrange("p h (j a) -> p h j a", a=TOPK)
                            pool.wait_ge(eq_ready, 2 * i + c + 1)
                            pool.tensor_tensor(e, e, bc(SIf[r, :, c], 2, TOPK), ALU.mult).then_inc(looked_up, 1)
                        gated(i - 1, 12, 4)
                    gated(TILES - 1, 0, 16)

                @block.vector
                def _(dve):
                    st = Steps(dve, v_steps)

                    def onehots(i, first, n):
                        for o in of_octets(i, first, n):
                            if o >= NAB:
                                dve.wait_ge(g_done, 2 * (o - NAB + 1))
                            dve.tensor_tensor(ABs[o % NAB], bc(bc(C("iota"), 1, OCT), 1, 2), bc(routeT[:, 0:2, o * OCT:(o + 1) * OCT], 3, P),
                                              ALU.is_equal).then_inc(onehots_ready, 1)
                    for i in range(TILES):
                        w = min(P, TOK - i * P)
                        r = slice(0, w)
                        src = cands[i % 2][r]
                        st.did(dve.tensor_copy(SIf[r].rearrange("p h c n -> p (h c n)"), SI[r, i].rearrange("p c n -> p (c n)")))
                        dve.wait_ge(cand_ready, i + 1)
                        for n, step in enumerate((lambda h: dve.max(TV[r, h, 0:8], src[:, h]),
                                                  lambda h: dve.max_index(TI[r, h, 0:8], TV[r, h, 0:8], src[:, h]),
                                                  lambda h: dve.match_replace(src[:, h], TV[r, h, 0:8], src[:, h], -3.0e38),
                                                  lambda h: dve.max(TV[r, h, 8:16], src[:, h]),
                                                  lambda h: dve.max_index(TI[r, h, 8:16], TV[r, h, 8:16], src[:, h]))):
                            if i and n == 1:
                                dve.wait_ge(t_out, i)
                            for h in range(PK_HEADS):
                                st.did(step(h))
                                if n and h % 4 == 3:
                                    onehots(i - 1, 2 * n - 2 + h // 4, 1)
                            st.settle()
                        dve.tensor_tensor(ex[r], TV[r], TV[r, :, 0:1].broadcast_to([w, PK_HEADS, TOPK]), ALU.subtract).then_inc(shifted, 1)
                        onehots(i - 1, 8, 2)
                        ti = TI[r].rearrange("p h n -> p (h n)")
                        st.did(dve.tensor_scalar(TA[r, 0], ti, 4, None, ALU.logical_shift_right))
                        st.did(dve.tensor_scalar(TA[r, 1], ti, 15, None, ALU.bitwise_and))
                        st.settle()
                        st.link(dve.tensor_copy(TAf[r], TA[r]))
                        for c in range(2):
                            onehots(i - 1, 10 + c, 1)
                            dve.tensor_tensor(lookup(i, c, r).rearrange("p h (j a) -> p (h j) a", a=TOPK), bc(C("iota")[r, 0:TOPK], 1, P),
                                              bc(TAf[r, c], 2, TOPK), ALU.is_equal).then_inc(eq_ready, 1)
                        onehots(i - 1, 12, 4)
                        for c in range(2):
                            dve.wait_ge(looked_up, 2 * i + c + 1)
                            st.did(dve.tensor_reduce(route[r, c], lookup(i, c, r).rearrange("p h (j a) -> p (h j) a", a=TOPK), AX.X, ALU.add))
                        dve.wait_ge(exp_done, i + 1)
                        st.link(dve.tensor_reduce(sums[r, 0:8], ex[r], AX.X, ALU.add))
                        st.link(dve.reciprocal(sums[r, 8:16], sums[r, 0:8]))
                        dve.tensor_tensor(route[r, 2].rearrange("p (h n) -> p h n", h=PK_HEADS), ex[r], bc(sums[r, 8:16], 2, TOPK), ALU.mult).then_inc(route_ready, 1)
                    dve.wait_ge(t_out, TILES)
                    onehots(TILES - 1, 0, 16)

                @block.sync
                def _(sp):
                    with sp.Fori(0, NTG // 2) as it:
                        for sg in range(2):
                            sp.wait_ge(g_out, it * (TG // 2) + (sg + 1) * (TG // 4) + 4)
                            sp.dma_start(gd[:, bass.ds(it * 2 + sg, 1)].rearrange("p g e t -> p (g e t)"),
                                         stg[:, sg].rearrange("p e t -> p (e t)")).then_inc(g_saved[sg], 16)
                    for sg in range(2):
                        sp.wait_ge(g_saved[sg], NTG // 2 * 16 + 16)

            PAIRS = PK_KEYS // 2
            acc = slot(0, 4).rearrange("p (d q t) -> p d q t", d=KC, q=2)
            u_raw = slot(12, 2)[:, 0:2 * D].rearrange("p (e n) -> p e n", e=2)
            v_raw = slot(14, 2)[:, 0:2 * D].rearrange("p (e n) -> p e n", e=2)
            Gt = slot(16, 2).rearrange("p (s g e t) -> p s g e t", s=2, g=NTG, e=2)
            gh = slot(18).rearrange("p (e t) -> p e t", e=2)
            us = u_split[:, :].rearrange("p (e h n) -> p e h n", e=2, h=2)
            vs = w_split[:, :].rearrange("p (s e h n) -> p s e h n", s=2, e=2, h=2)
            cs = c_split[:, :].rearrange("p (s e h t) -> p s e h t", s=2, e=2, h=2)
            uv = at("pk_u")
            vv = at("pk_v").rearrange("(p n e) d -> n e p d", p=P, e=2)
            with stage(nc, "u_in0", "u_in1", "v_in0", "v_in1", "g_in0", "g_in1", "u_hi", "u_ready", "v_hi", "v_ready", "h_done", "gelu_done",
                       "c_steps", "o_done", "o_free", "zeroed") as (
                    block, u_in0, u_in1, v_in0, v_in1, g_in0, g_in1, u_hi, u_ready, v_hi, v_ready, h_done, gelu_done, c_steps, o_done,
                    o_free, zeroed):
                u_in, v_in, g_in = (u_in0, u_in1), (v_in0, v_in1), (g_in0, g_in1)

                @block.sync
                def _(sp):
                    def load_u(k, e):
                        sp.dma_start(u_raw[:, e], uv[bass.ds(k * 2 + e, 1)].rearrange("o p x -> (o p) x")).then_inc(u_in[e], 16)

                    def load_v(k, e):
                        sp.dma_start(v_raw[:, e], vv[bass.ds(k, 1), e].rearrange("o p d -> (o p) d")).then_inc(v_in[e], 16)

                    def load_g(k, s):
                        sp.dma_start(Gt[:, s].rearrange("p g e t -> p g (e t)"),
                                     gd[:, :, bass.ds(k * 2, 2)].rearrange("p g e t -> p g (e t)")).then_inc(g_in[s], 16)

                    def loads(k, s):
                        for e in range(2):
                            sp.wait_ge(u_ready, k * 2 + (e - 1))
                            load_u(k, e)
                        for e in range(2):
                            sp.wait_ge(v_ready, k * 2 + (e - 1))
                            load_v(k, e)
                        sp.wait_ge(c_steps, k * 6)
                        load_g(k, s)
                    for e in range(2):
                        load_u(0, e)
                        load_v(0, e)
                    load_g(0, 0)
                    sp.sem_inc(c_steps, 6)
                    loads(1, 1)
                    with sp.Fori(0, PAIRS // 2 - 1) as i:
                        for s in range(2):
                            loads(i * 2 + (2 + s), s)

                @block.scalar
                def _(act):
                    def u_hi_of(k, e):
                        act.wait_ge(u_in[e], k * 16 + 16)
                        act.copy(us[:, e, 0], u_raw[:, e]).then_inc(u_hi, 1)

                    def v_hi_of(k, s, e):
                        act.wait_ge(v_in[e], k * 16 + 16)
                        act.copy(vs[:, s, e, 0], v_raw[:, e]).then_inc(v_hi, 1)

                    def steps(k, s, more):
                        for e in range(2):
                            act.wait_ge(c_steps, k * 6 + (3 * e + 3))
                            for q in range(2):
                                act.wait_ge(h_done, k * 4 + (2 * e + q + 1))
                                act.activation(gh[:, e, q * HN:(q + 1) * HN], ps[:, 2 * e + q, 0:HN], ACT.Gelu).then_inc(gelu_done, 1)
                            if more:
                                u_hi_of(k + 1, e)
                        if more:
                            act.wait_ge(o_done, k * 16 + 32)
                            for e in range(2):
                                v_hi_of(k + 1, 1 - s, e)
                    act.sem_inc(gelu_done, 4)
                    for e in range(2):
                        u_hi_of(0, e)
                        v_hi_of(0, 0, e)
                    with act.Fori(0, PAIRS // 2 - 1) as i:
                        for s in range(2):
                            steps(i * 2 + s, s, True)
                    steps(PAIRS - 2, 0, True)
                    steps(PAIRS - 1, 1, False)

                @block.gpsimd
                def _(pool):
                    def lo_parts(k, s):
                        for e in range(2):
                            pool.wait_ge(u_hi, k * 2 + (e + 1))
                            pool.tensor_tensor(us[:, e, 1], u_raw[:, e], us[:, e, 0].bitcast(F32), ALU.subtract).then_inc(u_ready, 1)
                        for e in range(2):
                            pool.wait_ge(v_hi, k * 2 + (e + 1))
                            pool.tensor_tensor(vs[:, s, e, 1], v_raw[:, e], vs[:, s, e, 0].bitcast(F32), ALU.subtract).then_inc(v_ready, 1)
                    with pool.Fori(0, PAIRS // 2) as i:
                        for s in range(2):
                            lo_parts(i * 2 + s, s)

                @block.tensor
                def _(pe):
                    def hidden(k):
                        for e in range(2):
                            pe.wait_ge(u_ready, k * 2 + (e + 1))
                            pe.wait_ge(gelu_done, k * 4 + (2 * e + 2))
                            for q in range(2):
                                tq = slice(q * HN, (q + 1) * HN)
                                split_products(pe, ps[:, 2 * e + q, 0:HN],
                                               [((us[:, e, 0, c * P:(c + 1) * P], us[:, e, 1, c * P:(c + 1) * P]),
                                                 (x_part(0)[:, c, tq], x_part(1)[:, c, tq])) for c in range(KC)]).then_inc(h_done, 1)

                    def output(k, s):
                        pe.wait_ge(v_ready, k * 2 + 2)
                        pe.wait_ge(c_steps, k * 6 + 12)
                        for u in range(16):
                            d, q = u // 2, u % 2
                            tq = slice(q * HN, (q + 1) * HN)
                            if q == 0:
                                pe.wait_ge(o_free, k * 16 + (u + 2))
                            split_products(pe, ps[:, 4 + u % 4, 0:HN],
                                           [((vs[:, s, e, 0, d * P:(d + 1) * P], vs[:, s, e, 1, d * P:(d + 1) * P]),
                                             (cs[:, s, e, 0, tq], cs[:, s, e, 1, tq])) for e in range(2)]).then_inc(o_done, 1)
                    pe.sem_inc(o_done, 32)
                    hidden(0)
                    with pe.Fori(0, PAIRS // 2 - 1) as i:
                        for s in range(2):
                            hidden(i * 2 + (s + 1))
                            output(i * 2 + s, s)
                    hidden(PAIRS - 1)
                    output(PAIRS - 2, 0)
                    output(PAIRS - 1, 1)

                @block.vector
                def _(dve):
                    def product(k, s, e, n):
                        dve.wait_ge(g_in[s], n)
                        dve.wait_ge(gelu_done, k * 4 + (2 * e + 6))
                        h = gh[:, e].rearrange("p (g t) -> p g t", t=TG)
                        dve.tensor_tensor(h, h, Gt[:, s, :, e], ALU.mult).then_inc(c_steps, 1)

                    def hi(k, s, e):
                        dve.wait_ge(c_steps, k * 6 + (3 * e + 7))
                        dve.wait_ge(o_done, k * 16 + 16)
                        dve.tensor_copy(cs[:, s, e, 0], gh[:, e]).then_inc(c_steps, 1)

                    def lo(k, s, e):
                        dve.wait_ge(c_steps, k * 6 + (3 * e + 8))
                        dve.tensor_tensor(cs[:, s, e, 1], gh[:, e], cs[:, s, e, 0].bitcast(F32), ALU.subtract).then_inc(c_steps, 1)

                    def add(k, units):
                        for u in units:
                            d, q = u // 2, u % 2
                            dve.wait_ge(o_done, k * 16 + (u + 33))
                            dve.tensor_tensor(acc[:, d, q], acc[:, d, q], ps[:, 4 + u % 4, 0:HN], ALU.add).then_inc(o_free, 1)

                    def steps(k, s, n):
                        product(k, s, 0, n)
                        hi(k, s, 0)
                        lo(k, s, 0)
                        dve.wait_ge(o_free, k * 16 - 12)
                        add(k - 1, range(0, 3))
                        product(k, s, 1, n)
                        add(k - 1, range(3, 6))
                        hi(k, s, 1)
                        add(k - 1, range(6, 9))
                        lo(k, s, 1)
                        add(k - 1, range(9, 16))
                    dve.sem_inc(o_free, 4)
                    dve.memset(slot(0, 4), 0.0).then_inc(zeroed, 1)
                    dve.wait_ge(zeroed, 1)
                    for e in range(2):
                        product(0, 0, e, 16)
                        hi(0, 0, e)
                        lo(0, 0, e)
                    with dve.Fori(0, PAIRS // 2 - 1) as i:
                        steps(i * 2 + 1, 1, i * 16 + 16)
                        steps(i * 2 + 2, 0, i * 16 + 32)
                    steps(PAIRS - 1, 1, PAIRS // 2 * 16)
                    dve.wait_ge(o_free, (PAIRS - 1) * 16 + 4)
                    add(PAIRS - 1, range(16))

            with stage(nc, "t_done", "x_ready") as (block, t_done, x_ready):
                accT = slot(0, 4).rearrange("p (d t) -> p d t", d=KC)

                @block.tensor
                def _(pe):
                    for u in range(2 * TILES):
                        i, n = u // 2, u % 2
                        w = min(P, TOK - i * P)
                        if u >= 8:
                            pe.wait_ge(x_ready, u - 7)
                        for d in range(4):
                            last = pe.transpose(ps[0:w, u % 8, d * P:(d + 1) * P], accT[:, n * 4 + d, i * P:i * P + w], C("ident"))
                        last.then_inc(t_done, 1)

                @block.vector
                def _(dve):
                    for u in range(2 * TILES):
                        i, n = u // 2, u % 2
                        w = min(P, TOK - i * P)
                        dve.wait_ge(t_done, u + 1)
                        d = x_sb[0:w, i, n * 512:(n + 1) * 512]
                        dve.tensor_tensor(d, d, ps[0:w, u % 8, :], ALU.add).then_inc(x_ready, 1)


        with stage(nc, "y_out") as (block, y_out):
            @block.sync
            def _(sp):
                sp.dma_start(t["o_y"].rearrange("(i p) d -> p i d", p=P), x_sb[:, :, :]).then_inc(y_out, 16)
                sp.wait_ge(y_out, 16)


_OUTS = [("o_y", (TOKP, D)), ("o_kp", (DEPTH, SEQ, 512)), ("o_vp", (DEPTH, SEQ, 512)),
         ("o_ks", (DEPTH, SAMP, 512)), ("o_vs", (DEPTH, SAMP, 512)),
         ("o_state_p", (DEPTH, P, 256)), ("o_state_s", (DEPTH, P, 2048)), ("o_tails", (DEPTH, P, 234))]

_SCRATCH = [("rel_scratch", (P, H * (REL + 1))), ("g_scratch", (P, TOK // 32, P, 32))]


def lay_out(i):
    f = lambda n: np.ascontiguousarray(np.asarray(i[n], dtype=None))
    a = {}
    a["x_prompt"] = f("x_prompt").reshape(SEQ, D)
    a["x_sample"] = f("x_sample").reshape(SAMP, D)
    a["cache_k"], a["cache_v"] = f("cache_k"), f("cache_v")
    a["page_table"] = f("page_table")
    a["w_in"], a["w_out"], a["rel_bias"] = f("w_in"), f("w_out"), f("rel_bias")
    per = lambda n: f(n).reshape(DEPTH, -1, P).transpose(0, 2, 1)
    cols = np.zeros((DEPTH, P, NCOL), np.float32)

    def put(name, v):
        o, n = COLS[name]
        cols[:, :, o:o + n] = v
    for name, src in (("mix_g", "rms_mix_g"), ("ffn_g", "rms_ffn_g"), ("mu", "rw_mu"), ("w0", "rw_w0"), ("a0", "rw_a0"),
                      ("kk", "rw_kk"), ("ka", "rw_ka"), ("rk", "rw_rk"), ("ln_g", "rw_ln_g"), ("ln_b", "rw_ln_b"),
                      ("conv", "dn_conv_w"), ("subln", "df_subln_g")):
        put(name, per(src))
    put("dn_g", np.tile(f("dn_norm_g"), (1, 2))[:, :, None])
    halves = lambda n: np.repeat(f(n).reshape(DEPTH, 2, 2).transpose(0, 2, 1), 64, axis=1)
    put("a_log", halves("dn_a_log"))
    put("dt", halves("dn_dt_bias"))
    init = np.array([0.8 - 0.6 * math.exp(-0.3 * l) for l in range(DEPTH)], np.float32)
    put("lam_init", init[:, None, None])
    put("lam_rest", np.array([1.0 - (0.8 - 0.6 * math.exp(-0.3 * l)) for l in range(DEPTH)], np.float32)[:, None, None])
    a["cols"] = cols
    a["rows"] = np.concatenate([f("df_qn_g").reshape(DEPTH, P), f("df_kn_g").reshape(DEPTH, P)]
                               + [f(n) for n in ("df_lq1", "df_lk1", "df_lq2", "df_lk2")], axis=1)
    a["lora"] = np.concatenate([np.concatenate([f("rw_w2"), f("rw_a2")], axis=1), f("rw_g2")], axis=2)
    shift = f("state_rwkv_shift").reshape(DEPTH, NSEQ, 8, P).transpose(0, 3, 2, 1).reshape(DEPTH, P, 64)
    conv = f("state_dn_conv").reshape(DEPTH, NSEQ, 3, 6, P).transpose(0, 4, 3, 1, 2).reshape(DEPTH, P, 144)
    a["tails"] = np.concatenate([shift, conv], axis=2)
    sr = f("state_rwkv").reshape(DEPTH, NSEQ, 2, 2, HD, HD).transpose(0, 3, 5, 2, 1, 4).reshape(DEPTH, P, 1024)
    sd = f("state_dn").reshape(DEPTH, NSEQ, 2, 2, HD, HD).transpose(0, 3, 4, 2, 1, 5).reshape(DEPTH, P, 1024)
    a["states"] = np.concatenate([sr, sd], axis=2)
    a["pk_wq"] = f("pk_wq")
    a["pk_keys"] = f("pk_keys").transpose(0, 4, 1, 2, 3).reshape(DEPTH, P, 16 * P)
    a["pk_u"] = f("pk_u").reshape(DEPTH, P, P, KC, P).transpose(0, 2, 4, 3, 1).reshape(DEPTH, P, P, D)
    a["pk_v"] = f("pk_v")
    a["consts"], a["buckets"], a["future"] = constants()
    return {k: np.ascontiguousarray(v) for k, v in a.items()}


def results_of(r):
    y = r["o_y"]
    kp, vp = (r[n].reshape(1, DEPTH, SEQ, H, 2 * HD) for n in ("o_kp", "o_vp"))
    ks, vs = (r[n].reshape(DEPTH, NSEQ, NEW, H, 2 * HD).transpose(1, 0, 2, 3, 4) for n in ("o_ks", "o_vs"))
    sp = r["o_state_p"].reshape(DEPTH, 2, HD, 2, 2, HD)
    ap = sp[:, :, :, 0].transpose(0, 3, 1, 4, 2).reshape(DEPTH, 1, H, HD, HD)
    bp = sp[:, :, :, 1].transpose(0, 3, 1, 2, 4).reshape(DEPTH, 1, H, HD, HD)
    ss = r["o_state_s"].reshape(DEPTH, 2, HD, 2, 2, NSEQ, HD)
    as_ = ss[:, :, :, 0].transpose(0, 4, 3, 1, 5, 2).reshape(DEPTH, NSEQ, H, HD, HD)
    bs = ss[:, :, :, 1].transpose(0, 4, 3, 1, 2, 5).reshape(DEPTH, NSEQ, H, HD, HD)
    tl = r["o_tails"]
    shp = tl[:, :, 0:8].transpose(0, 2, 1).reshape(DEPTH, 1, A_COLS)
    shs = tl[:, :, 8:72].reshape(DEPTH, P, 8, NSEQ).transpose(0, 3, 2, 1).reshape(DEPTH, NSEQ, A_COLS)
    cvp = tl[:, :, 72:90].reshape(DEPTH, P, 6, 3).transpose(0, 3, 2, 1).reshape(DEPTH, 1, 3, 768)
    cvs = tl[:, :, 90:234].reshape(DEPTH, P, 6, NSEQ, 3).transpose(0, 3, 4, 2, 1).reshape(DEPTH, NSEQ, 3, 768)
    out = (y[:SEQ].reshape(1, SEQ, D), y[SEQ:TOK].reshape(NSEQ, NEW, D), kp, vp, ks, vs, ap, as_, shp, shs, bp, bs, cvp, cvs)
    return tuple(np.ascontiguousarray(o) for o in out)


def kernel(**inputs):
    import concourse.bacc as bacc
    from concourse.bass_utils import run_bass_kernel_spmd

    nc = bacc.Bacc("TRN2", target_bir_lowering=False, num_devices=1)
    arrays = lay_out(inputs)
    t = {n: nc.dram_tensor(n, a.shape, mybir.dt.from_np(a.dtype), kind="ExternalInput").ap() for n, a in arrays.items()}
    for n, shape in _OUTS:
        t[n] = nc.dram_tensor(n, shape, F32, kind="ExternalOutput").ap()
    for n, shape in _SCRATCH:
        t[n] = nc.dram_tensor(n, shape, F32, kind="Internal").ap()
    trunk(nc, t)
    r = run_bass_kernel_spmd(nc, [arrays], core_ids=[0])
    return results_of(r.results[0])
```
